# Optimizing a Trainium2 kernel written in Bass

```python
import jax, jax.numpy as jnp
from jax import lax
import numpy as np

D_MODEL = 1024
BATCH = 1
SEQ = 1024
DEPTH = 1
DEC_BATCH = 8
DEC_SEQ = 16
PAST_LEN = 256

CHUNK = 64
EPS = 1e-6
SSM_HEADS = 32
SSM_HEADDIM = 64
D_INNER = SSM_HEADS * SSM_HEADDIM
D_STATE = 128
SSM_GROUPS = 8
HEADS_PER_GROUP = SSM_HEADS // SSM_GROUPS
CONV_W = 4
CONV_DIM = D_INNER + 2 * SSM_GROUPS * D_STATE
GROUP_NORM_DIM = D_INNER // SSM_GROUPS
N_HEADS = 16
N_KV = 4
HEAD_DIM = 64
Q_PER_KV = N_HEADS // N_KV
WINDOW = 128
WIN_CHUNKS = WINDOW // CHUNK
ATTN_DIM = N_HEADS * HEAD_DIM
KV_DIM = N_KV * HEAD_DIM
ATTN_SCALE = HEAD_DIM ** -0.5
PEER_HEADS = 8
N_KEYS = 128
N_EXPERTS = N_KEYS * N_KEYS
PEER_TOPK = 16
D_KEY = 256
D_HALF = D_KEY // 2
PEER_BLOCK = 256
OFF_XBC = D_INNER
OFF_DT = OFF_XBC + CONV_DIM
OFF_Q = OFF_DT + SSM_HEADS
OFF_K = OFF_Q + ATTN_DIM
OFF_V = OFF_K + KV_DIM
OFF_GATE = OFF_V + KV_DIM
IN_DIM = OFF_GATE + 2 * D_MODEL

kernel_name = "hybrid_ssd_swa_peer_stream_step"

def rmsnorm(x, g):
    xf = x.astype(jnp.float32)
    xf = xf * lax.rsqrt(jnp.mean(xf * xf, axis=-1, keepdims=True) + EPS)
    return (xf * g.astype(jnp.float32)).astype(x.dtype)

def sink_softmax(s, sink):
    m = jnp.maximum(jnp.max(s, axis=-1, keepdims=True), sink)
    e = jnp.exp(s - m)
    return e / (jnp.sum(e, axis=-1, keepdims=True) + jnp.exp(sink - m))

def ssd_scan(xh, a, bm, cm, h0):
    b, T = xh.shape[:2]
    L = min(T, CHUNK)
    nc = T // L

    def chunks(t):
        return jnp.moveaxis(t.reshape((b, nc, L) + t.shape[2:]), 1, 0)

    causal = jnp.tril(jnp.ones((L, L), bool))[None, :, :, None, None]

    def step(h, inp):
        xc, ac, bc, cc = inp
        xc = xc.astype(jnp.float32)
        bc = bc.astype(jnp.float32)
        cc = cc.astype(jnp.float32)
        acum = jnp.cumsum(ac.astype(jnp.float32), axis=1)
        seg = acum[:, :, None] - acum[:, None, :]
        decay = jnp.exp(jnp.where(causal, seg, -jnp.inf))
        cb = jnp.einsum("blgn,bsgn->blsg", cc, bc)
        y = jnp.einsum("blsgr,bsgrp->blgrp", cb[..., None] * decay, xc)
        y = y + jnp.einsum("blgn,bgrpn->blgrp", cc, h) * jnp.exp(acum)[..., None]
        to_end = jnp.exp(acum[:, -1:] - acum)
        h = (jnp.exp(acum[:, -1])[..., None, None] * h
             + jnp.einsum("blgn,blgrp->bgrpn", bc, to_end[..., None] * xc))
        return h, y

    h, ys = lax.scan(step, h0, (chunks(xh), chunks(a), chunks(bm), chunks(cm)))
    y = jnp.moveaxis(ys, 0, 1).reshape(xh.shape)
    return y, h

def ssd_branch(z, xbc, dt_raw, conv_hist, h0, conv_w, conv_b, dt_bias, a_log, d_skip, norm_g):
    b, T = z.shape[:2]
    xpad = jnp.concatenate([conv_hist.astype(xbc.dtype), xbc], axis=1)
    conv = conv_b
    for j in range(CONV_W):
        conv = conv + xpad[:, j:j + T] * conv_w[j]
    xbc = jax.nn.silu(conv)
    xs, bm, cm = jnp.split(xbc, [D_INNER, D_INNER + SSM_GROUPS * D_STATE], axis=-1)
    xs = xs.reshape(b, T, SSM_GROUPS, HEADS_PER_GROUP, SSM_HEADDIM)
    bm = bm.reshape(b, T, SSM_GROUPS, D_STATE)
    cm = cm.reshape(b, T, SSM_GROUPS, D_STATE)
    dt = jax.nn.softplus(dt_raw.astype(jnp.float32) + dt_bias.astype(jnp.float32))
    dt = dt.reshape(b, T, SSM_GROUPS, HEADS_PER_GROUP)
    A = -jnp.exp(a_log.astype(jnp.float32)).reshape(SSM_GROUPS, HEADS_PER_GROUP)
    h0 = h0.astype(jnp.float32).reshape(b, SSM_GROUPS, HEADS_PER_GROUP, SSM_HEADDIM, D_STATE)
    y, h = ssd_scan(xs * dt[..., None], dt * A, bm, cm, h0)
    y = y + d_skip.astype(jnp.float32).reshape(SSM_GROUPS, HEADS_PER_GROUP)[..., None] * xs
    y = y * jax.nn.silu(z.astype(jnp.float32)).reshape(y.shape)
    y = y.reshape(b, T, SSM_GROUPS, GROUP_NORM_DIM)
    y = y * lax.rsqrt(jnp.mean(y * y, axis=-1, keepdims=True) + EPS)
    y = (y.reshape(b, T, D_INNER) * norm_g.astype(jnp.float32)).astype(z.dtype)
    return y, xpad[:, T:], h.reshape(b, SSM_HEADS, SSM_HEADDIM, D_STATE)

def banded_attention(q, k, v, sinks):
    b, T = q.shape[:2]
    nc = T // CHUNK
    qc = q.reshape(b, nc, CHUNK, N_KV, Q_PER_KV, HEAD_DIM)

    def band(t):
        tc = t.reshape(b, nc, CHUNK, N_KV, HEAD_DIM)
        tp = jnp.pad(tc, ((0, 0), (WIN_CHUNKS, 0), (0, 0), (0, 0), (0, 0)))
        return jnp.concatenate([tp[:, j:j + nc] for j in range(WIN_CHUNKS + 1)], axis=2)

    kb, vb = band(k), band(v)
    s = jnp.einsum("bcqgrd,bckgd->bcgrqk", qc, kb).astype(jnp.float32) * ATTN_SCALE
    n_band = (WIN_CHUNKS + 1) * CHUNK
    key_chunk = jnp.arange(nc)[:, None] + (jnp.arange(n_band) // CHUNK)[None, :] - WIN_CHUNKS
    valid = (key_chunk >= 0)[None, :, None, None, None, :]
    s = jnp.where(valid, s, -jnp.inf)
    sink = sinks.astype(jnp.float32).reshape(N_KV, Q_PER_KV)[None, None, :, :, None, None]
    p = sink_softmax(s, sink)
    o = jnp.einsum("bcgrqk,bckgd->bcqgrd", p.astype(vb.dtype), vb)
    return o.reshape(b, T, ATTN_DIM)

def cached_attention(q, k, v, k_hist, v_hist, sinks):
    b, T = q.shape[:2]
    kk = jnp.concatenate([k_hist.astype(k.dtype), k], axis=1)
    vv = jnp.concatenate([v_hist.astype(v.dtype), v], axis=1)
    s = jnp.einsum("bqgrd,bkgd->bgrqk", q, kk).astype(jnp.float32) * ATTN_SCALE
    sink = sinks.astype(jnp.float32).reshape(N_KV, Q_PER_KV)[None, :, :, None, None]
    p = sink_softmax(s, sink)
    o = jnp.einsum("bgrqk,bkgd->bqgrd", p.astype(vv.dtype), vv)
    return o.reshape(b, T, ATTN_DIM)

def peer_ffn(h, wq, sub_keys, u, v):
    b, T, D = h.shape
    n = b * T
    nb = -(-n // PEER_BLOCK)
    t = jnp.pad(h.reshape(n, D), ((0, nb * PEER_BLOCK - n), (0, 0))).reshape(nb, PEER_BLOCK, D)
    keys = sub_keys.astype(jnp.float32)

    def one(tb):
        q = (tb @ wq).astype(jnp.float32).reshape(PEER_BLOCK, PEER_HEADS, 2, D_HALF)
        s = jnp.einsum("thid,hikd->thik", q, keys)
        sv, si = lax.top_k(s, PEER_TOPK)
        comb = sv[:, :, 0, :, None] + sv[:, :, 1, None, :]
        comb_idx = si[:, :, 0, :, None] * N_KEYS + si[:, :, 1, None, :]
        comb = comb.reshape(PEER_BLOCK, PEER_HEADS, PEER_TOPK * PEER_TOPK)
        comb_idx = comb_idx.reshape(PEER_BLOCK, PEER_HEADS, PEER_TOPK * PEER_TOPK)
        fv, fi = lax.top_k(comb, PEER_TOPK)
        eidx = jnp.take_along_axis(comb_idx, fi, axis=-1)
        w = jax.nn.softmax(fv, axis=-1)
        act = jax.nn.gelu(jnp.einsum("thkd,td->thk", u[eidx], tb).astype(jnp.float32))
        return jnp.einsum("thk,thkd->td", (w * act).astype(tb.dtype), v[eidx])

    out = lax.map(one, t).reshape(nb * PEER_BLOCK, D)[:n]
    return out.reshape(b, T, D).astype(h.dtype)

def layer(x, c, conv_hist, ssm0, k_hist, v_hist, ada_w, ada_b, norm1_g, w_in, conv_w, conv_b,
          dt_bias, a_log, d_skip, ssm_norm_g, attn_sinks, w_branch_ssm, w_branch_attn, w_out,
          norm2_g, peer_wq, peer_keys, peer_u, peer_v):
    b, T, _ = x.shape
    mod = jax.nn.silu(c) @ ada_w + ada_b
    shift1, scale1, gate1, shift2, scale2, gate2 = [m[:, None] for m in jnp.split(mod, 6, axis=-1)]
    h = rmsnorm(x, norm1_g) * (1 + scale1) + shift1
    proj = h @ w_in
    z, xbc, dt_raw, q, k, v, gates = jnp.split(
        proj, [OFF_XBC, OFF_DT, OFF_Q, OFF_K, OFF_V, OFF_GATE], axis=-1)
    y_ssm, conv_new, ssm_new = ssd_branch(z, xbc, dt_raw, conv_hist, ssm0, conv_w, conv_b,
                                          dt_bias, a_log, d_skip, ssm_norm_g)
    q = q.reshape(b, T, N_KV, Q_PER_KV, HEAD_DIM)
    k = k.reshape(b, T, N_KV, HEAD_DIM)
    v = v.reshape(b, T, N_KV, HEAD_DIM)
    if k_hist is None:
        o = banded_attention(q, k, v, attn_sinks)
        k_new, v_new = k[:, T - WINDOW:], v[:, T - WINDOW:]
    else:
        o = cached_attention(q, k, v, k_hist, v_hist, attn_sinks)
        k_new, v_new = k, v
    g_ssm, g_attn = jnp.split(jax.nn.sigmoid(gates), 2, axis=-1)
    merged = g_ssm * (y_ssm @ w_branch_ssm) + g_attn * (o @ w_branch_attn)
    x = x + gate1 * (merged @ w_out)
    h2 = rmsnorm(x, norm2_g) * (1 + scale2) + shift2
    x = x + gate2 * peer_ffn(h2, peer_wq, peer_keys, peer_u, peer_v)
    return x, k_new, v_new, conv_new, ssm_new

def setup_inputs(seed: int = 0) -> dict:
    key = jax.random.key(seed)
    ks = jax.random.split(key, 32)
    f32 = jnp.float32

    def nrm(k, shape, scale):
        return jax.random.normal(k, shape, f32) * scale

    win_cache = min(WINDOW, PAST_LEN)
    dt0 = jnp.exp(jax.random.uniform(ks[12], (DEPTH, SSM_HEADS), f32, np.log(1e-3), np.log(1e-1)))
    return {
        "x_prompt": nrm(ks[0], (BATCH, SEQ, D_MODEL), 1.0),
        "x_sample": nrm(ks[1], (DEC_BATCH, DEC_SEQ, D_MODEL), 1.0),
        "cache_attn_k": nrm(ks[2], (DEPTH, DEC_BATCH, win_cache, N_KV, HEAD_DIM), 1.0),
        "cache_attn_v": nrm(ks[3], (DEPTH, DEC_BATCH, win_cache, N_KV, HEAD_DIM), 1.0),
        "state_conv": nrm(ks[4], (DEPTH, DEC_BATCH, CONV_W - 1, CONV_DIM), 1.0),
        "state_ssm": nrm(ks[5], (DEPTH, DEC_BATCH, SSM_HEADS, SSM_HEADDIM, D_STATE), 0.1),
        "c_prompt": nrm(ks[6], (BATCH, D_MODEL), 1.0),
        "c_sample": nrm(ks[7], (DEC_BATCH, D_MODEL), 1.0),
        "ada_w": nrm(ks[8], (DEPTH, D_MODEL, 6 * D_MODEL), 0.5 * D_MODEL ** -0.5),
        "ada_b": nrm(ks[9], (DEPTH, 6 * D_MODEL), 0.01),
        "norm1_g": 1.0 + nrm(ks[10], (DEPTH, D_MODEL), 0.05),
        "w_in": nrm(ks[11], (DEPTH, D_MODEL, IN_DIM), D_MODEL ** -0.5),
        "conv_w": nrm(ks[13], (DEPTH, CONV_W, CONV_DIM), CONV_W ** -0.5),
        "conv_b": nrm(ks[14], (DEPTH, CONV_DIM), 0.01),
        "dt_bias": dt0 + jnp.log(-jnp.expm1(-dt0)),
        "a_log": jnp.log(jax.random.uniform(ks[15], (DEPTH, SSM_HEADS), f32, 1.0, 16.0)),
        "d_skip": 1.0 + nrm(ks[16], (DEPTH, SSM_HEADS), 0.1),
        "ssm_norm_g": 1.0 + nrm(ks[17], (DEPTH, D_INNER), 0.05),
        "attn_sinks": nrm(ks[18], (DEPTH, N_HEADS), 1.0),
        "w_branch_ssm": nrm(ks[19], (DEPTH, D_INNER, D_MODEL), D_INNER ** -0.5),
        "w_branch_attn": nrm(ks[20], (DEPTH, ATTN_DIM, D_MODEL), ATTN_DIM ** -0.5),
        "w_out": nrm(ks[21], (DEPTH, D_MODEL, D_MODEL), D_MODEL ** -0.5),
        "norm2_g": 1.0 + nrm(ks[22], (DEPTH, D_MODEL), 0.05),
        "peer_wq": nrm(ks[23], (DEPTH, D_MODEL, PEER_HEADS * D_KEY), D_MODEL ** -0.5),
        "peer_keys": nrm(ks[24], (DEPTH, PEER_HEADS, 2, N_KEYS, D_HALF), D_HALF ** -0.5),
        "peer_u": nrm(ks[25], (DEPTH, N_EXPERTS, D_MODEL), D_MODEL ** -0.5),
        "peer_v": nrm(ks[26], (DEPTH, N_EXPERTS, D_MODEL), PEER_HEADS ** -0.5),
        "final_g": 1.0 + nrm(ks[27], (D_MODEL,), 0.05),
    }

def reference(x_prompt, x_sample, cache_attn_k, cache_attn_v, state_conv, state_ssm, c_prompt, c_sample,
              ada_w, ada_b, norm1_g, w_in, conv_w, conv_b, dt_bias, a_log, d_skip, ssm_norm_g,
              attn_sinks, w_branch_ssm, w_branch_attn, w_out, norm2_g, peer_wq, peer_keys,
              peer_u, peer_v, final_g):
    xp, xs = x_prompt, x_sample
    bp = xp.shape[0]
    kp_l, vp_l, cp_l, sp_l = [], [], [], []
    ks_l, vs_l, cs_l, ss_l = [], [], [], []
    for l in range(DEPTH):
        lw = (ada_w[l], ada_b[l], norm1_g[l], w_in[l], conv_w[l], conv_b[l], dt_bias[l], a_log[l],
              d_skip[l], ssm_norm_g[l], attn_sinks[l], w_branch_ssm[l], w_branch_attn[l], w_out[l],
              norm2_g[l], peer_wq[l], peer_keys[l], peer_u[l], peer_v[l])
        conv0 = jnp.zeros((bp, CONV_W - 1, CONV_DIM), xp.dtype)
        ssm0 = jnp.zeros((bp, SSM_HEADS, SSM_HEADDIM, D_STATE), jnp.float32)
        xp, kp, vp, cp, sp = layer(xp, c_prompt, conv0, ssm0, None, None, *lw)
        xs, kn, vn, cn, sn = layer(xs, c_sample, state_conv[l], state_ssm[l],
                                   cache_attn_k[l], cache_attn_v[l], *lw)
        kp_l.append(kp); vp_l.append(vp); cp_l.append(cp); sp_l.append(sp)
        ks_l.append(kn); vs_l.append(vn); cs_l.append(cn); ss_l.append(sn)
    y_prompt = rmsnorm(xp, final_g)
    y_sample = rmsnorm(xs, final_g)
    return (y_prompt, y_sample,
            jnp.stack(kp_l), jnp.stack(vp_l), jnp.stack(cp_l), jnp.stack(sp_l),
            jnp.stack(ks_l), jnp.stack(vs_l), jnp.stack(cs_l), jnp.stack(ss_l))


_drawn_inputs = setup_inputs


def setup_inputs(seed=0):
    import zlib

    import numpy as np

    out = dict(_drawn_inputs(seed))
    spreads = {}
    factors = {'cache_attn_k': 2.869,
     'conv_b': 3.904,
     'd_skip': 4.764,
     'ssm_norm_g': 5.676,
     'attn_sinks': 8.0,
     'norm2_g': 4.24}
    for name, (base, spread) in spreads.items():
        noise = np.random.default_rng([zlib.crc32(name.encode()), seed]).standard_normal(out[name].shape)
        drawn = base * np.exp(spread * noise) if base else spread * noise
        out[name] = __import__('jax').numpy.asarray(drawn.astype(out[name].dtype))
    for name, factor in factors.items():
        out[name] = (out[name] * factor).astype(out[name].dtype)
    return out
```

```python
import concourse.bass as bass
from concourse import mybir
from contextlib import ExitStack

P = 128
D = 1024
KD = D // P
SEQ = 1024
NB, TS = 8, 16
T = SEQ + NB * TS
NT = T // P
NC_ = 1 + NB
EPS = 1e-6
COLS = ((0, 512), (512, 512), (1024, 128))
TB = 1536

H, HD, N = 32, 64, 128
G, R = 8, 4
INNER, CONV = H * HD, H * HD + 2 * G * N
TAPS = 4
NKV, QH, DH = 4, 4, 64
ATTN, KV = NKV * QH * DH, NKV * DH
PAST, CHUNK, N_KEYS = 128, 64, 128
PH, TOPK = 8, 16
HK = PH * TOPK
MZ, MG, MQ, MK, MX = INNER // P, 2 * D // P, ATTN // P, KV // P, CONV // P
TZ, TG, TQ = 0, MZ, MZ + MG
TK = TQ + MQ
NPLAIN = TK + MK
NEG = -1e30

F32 = mybir.dt.float32
U32 = mybir.dt.uint32
ALU = mybir.AluOpType
ACT = mybir.ActivationFunctionType
AX = mybir.AxisListType
ds = bass.ds
START = 1

C_ID, C_ONE, C_TRI, C_STRI, C_NEG, C_AM, C_IOTA, C_BM = 0, 128, 256, 512, 768, 1024, 1280, 1408
C_N = C_BM + NB


class Steps:

    def __init__(self, eng, sem, per_turn=0, turn=0, before=0):
        self.eng, self.sem, self.per_turn, self.turn = eng, sem, per_turn, turn
        self.before = self.n = before

    def step(self, ins):
        ins.then_inc(self.sem, 1)
        self.n += 1

    def wait(self):
        self.eng.wait_ge(self.sem, self.turn * self.per_turn + self.n + START)

    def link(self, ins):
        self.step(ins)
        self.wait()

    def close(self):
        assert self.n - self.before == self.per_turn, (self.n - self.before, self.per_turn)


def open_(nc, ctx):
    held = []

    def clear():
        if held:
            nc.clear_and_free_semaphores(held)
            nc.all_engine_barrier()
    ctx.callback(clear)

    def sb(name, shape, dt=F32):
        return ctx.enter_context(nc.sbuf_tensor(name, shape, dt))

    def pb(name, shape):
        return ctx.enter_context(nc.psum_tensor(name, shape, F32))

    def sem(name, n=None):
        got = [nc.alloc_semaphore(name if n is None else f"{name}{i}") for i in range(n or 1)]
        held.extend(got)
        for s in got:
            nc.gpsimd.sem_inc(s, START)
        return got[0] if n is None else got
    return sb, pb, sem


def begin(nc, ctx):
    nc.all_engine_barrier()
    return ctx.enter_context(nc.Block())


def phase_modulation(nc, io, per):
    M = 6 * KD
    with ExitStack() as ctx:
        sb, pb, sem = open_(nc, ctx)
        c = sb("cond", [P, KD, NC_])
        cs = sb("cond_silu", [P, KD, NC_])
        bias = sb("ada_bias", [P, M])
        g1 = sb("norm_gains", [P, 2, KD])
        w = sb("ada_ring", [P, 4, KD, P])
        raw = sb("mod_raw", [P, M, NC_])
        ps = pb("mod_psum", [P, 4, 512])
        consts_in, small_in, c_silu = sem("mod_consts_in"), sem("mod_small_in"), sem("mod_c_silu")
        w_in, mm, copied = sem("mod_w_in", 4), sem("mod_mm", 4), sem("mod_copied", 4)
        added = sem("mod_added")
        block = begin(nc, ctx)

        @block.sync
        def _(sp):
            sp.dma_start(c[:], io["c"][:]).then_inc(small_in, 16)
            sp.dma_start(bias[:], io["ada_b"][:]).then_inc(small_in, 16)
            sp.dma_start(g1[:], io["norm_g"][:]).then_inc(small_in, 16)
            sp.dma_start(per["const"][:], io["const"][:]).then_inc(consts_in, 16)
            with sp.Fori(0, M // 4) as i:
                for s in range(4):
                    sp.wait_ge(mm[s], i + START)
                    sp.dma_start(w[:, s], io["ada_w"][ds(i * 4 + s, 1)].rearrange("m p k c -> p (m k) c")).then_inc(w_in[s], 16)
            sp.wait_ge(consts_in, 16 + START)

        @block.scalar
        def _(act):
            act.wait_ge(small_in, 48 + START)
            nc.scalar.activation(cs[:], c[:], ACT.Silu).then_inc(c_silu, 1)

        @block.tensor
        def _(pe):
            pe.wait_ge(c_silu, 1 + START)
            with pe.Fori(0, M // 4) as i:
                for s in range(4):
                    pe.wait_ge(w_in[s], i * 16 + 16 + START)
                    pe.wait_ge(copied[s], i + START)
                    for k in range(KD):
                        last = nc.tensor.matmul(ps[:, s, 0:NC_], w[:, s, k], cs[:, k], start=(k == 0), stop=(k == KD - 1))
                    last.then_inc(mm[s], 1)

        @block.vector
        def _(dve):
            with dve.Fori(0, M // 4) as i:
                for s in range(4):
                    dve.wait_ge(mm[s], i + 1 + START)
                    nc.vector.tensor_copy(raw[:, ds(i * 4 + s, 1)].rearrange("p m c -> p (m c)"), ps[:, s, 0:NC_]).then_inc(copied[s], 1)
            dve.wait_ge(copied[3], M // 4 + START)
            for s in range(3):
                dve.wait_ge(copied[s], M // 4 + START)
            dve.wait_ge(small_in, 48 + START)
            mod = per["mod"]
            nc.vector.tensor_tensor(mod[:], raw[:], bias[:].unsqueeze(2).to_broadcast([P, M, NC_]), ALU.add).then_inc(added, 1)
            dve.wait_ge(added, 1 + START)
            for n, first in ((0, KD), (1, 4 * KD)):
                sc = mod[:, first:first + KD]
                nc.vector.scalar_tensor_tensor(out=per["gain"][:, n], in0=sc, scalar=1.0,
                                               in1=g1[:, n].unsqueeze(2).to_broadcast([P, KD, NC_]), op0=ALU.add, op1=ALU.mult)


def per_token(v, k):
    return v[:, k, 1:NC_].unsqueeze(2).to_broadcast([P, NB, TS])


def samples(x):
    return x[:, SEQ:T].rearrange("p (b t) -> p b t", t=TS)


def norm_engines(nc, block, per, x, xs_ready, xs_value, sq, ps, rstd, sems, finish):
    squared, summed, rooted, chain = sems
    ones = per["const"][:, C_ONE:C_ONE + P]

    @block.scalar
    def _(act):
        act.wait_ge(xs_ready, xs_value + START)
        for k in range(KD):
            if k >= 2:
                act.wait_ge(summed, k - 1 + START)
            nc.scalar.activation(sq[:, k % 2], x[:, k], ACT.Square).then_inc(squared, 1)
        act.wait_ge(summed, KD + START)
        nc.scalar.activation(rstd[:], ps[:, 0:T], ACT.Sqrt, bias=per["eps"][:, 0:1], scale=1.0 / D).then_inc(rooted, 1)

    @block.tensor
    def _(pe):
        for k in range(KD):
            pe.wait_ge(squared, k + 1 + START)
            for a, n in COLS:
                last = nc.tensor.matmul(ps[:, a:a + n], ones, sq[:, k % 2, a:a + n], start=(k == 0), stop=(k == KD - 1))
            last.then_inc(summed, 1)

    @block.vector
    def _(dve):
        ch = Steps(dve, chain)
        dve.wait_ge(rooted, 1 + START)
        ch.link(nc.vector.reciprocal(rstd[:], rstd[:]))
        for k in range(KD):
            finish(dve, k, ch)


def modulated(nc, per, x, rstd, out, which, shift_at, tmp):
    def finish(dve, k, ch):
        gain, mod = per["gain"][:, which], per["mod"]
        b = k % 2
        ch.link(nc.vector.tensor_tensor(tmp[:, b], x[:, k], rstd[:], ALU.mult))
        ch.step(nc.vector.tensor_scalar(out[:, k, 0:SEQ], tmp[:, b, 0:SEQ], gain[:, k, 0:1], mod[:, shift_at + k, 0:1], ALU.mult, ALU.add))
        ch.link(nc.vector.tensor_tensor(samples(out[:, k]), samples(tmp[:, b]), per_token(gain, k), ALU.mult))
        ch.link(nc.vector.tensor_tensor(samples(out[:, k]), samples(out[:, k]), per_token(mod[:, shift_at:shift_at + KD], k), ALU.add))
    return finish


def phase_norm1(nc, io, per, h):
    with ExitStack() as ctx:
        sb, pb, sem = open_(nc, ctx)
        x = sb("n1_x", [P, KD, T])
        sq, tmp, rstd = sb("n1_sq", [P, 2, T]), sb("n1_tmp", [P, 2, T]), sb("n1_rstd", [P, T])
        ps = pb("n1_ps", [P, TB])
        x_in = sem("n1_x_in")
        sems = [sem(f"n1_{n}") for n in ("squared", "summed", "rooted", "chain")]
        block = begin(nc, ctx)

        @block.sync
        def _(sp):
            sp.dma_start(x[:], io["x"][:]).then_inc(x_in, 16)
        norm_engines(nc, block, per, x, x_in, 16, sq, ps, rstd, sems, modulated(nc, per, x, rstd, h, 0, 0, tmp))


def product(nc, ps, w, x, kt):
    for k in range(kt):
        for a, n in COLS:
            last = nc.tensor.matmul(ps[:, a:a + n], w[:, k], x[:, k, a:a + n], start=(k == 0), stop=(k == kt - 1))
    return last


def phase_projection(nc, io, per, h, scr):
    runs = ((TZ, MZ, ACT.Silu), (TG, MG, ACT.Sigmoid), (TQ, MQ + MK, ACT.Copy))
    turns = NPLAIN // 2
    XT = MX // 2
    PADP, PADS = TAPS - 1 + SEQ, TAPS - 1 + TS
    with ExitStack() as ctx:
        sb, pb, sem = open_(nc, ctx)
        w = sb("pr_w", [P, 2, KD, P])
        o = sb("pr_out", [P, 2, T])
        raw = sb("pr_raw", [P, 2, PADP + NB * PADS])
        acc = sb("pr_acc", [P, 2, T])
        acc2 = sb("pr_acc2", [P, 2, T])
        hist = sb("pr_hist", [P, MX, NB * (TAPS - 1)])
        cw = sb("pr_convw", [P, MX, TAPS + 1])
        cwt = sb("pr_convw_tile", [P, 2, TAPS + 1])
        tail_p, tail_s = sb("pr_tail_p", [P, MX, TAPS - 1]), sb("pr_tail_s", [P, MX, NB * (TAPS - 1)])
        wvd = sb("pr_wvd", [P, KD, KV + H])
        vd = sb("pr_vd", [P, NT, KV + H])
        ps = pb("pr_ps", [P, 2, TB])
        pv = pb("pr_pv", [P, 2, 512])
        small_in, wvd_in = sem("pr_small_in"), sem("pr_wvd_in")
        w_in, mm = sem("pr_w_in", 2), sem("pr_mm", 2)
        evac, stored = sem("pr_evac", 2), sem("pr_stored", 2)
        vmm, vcopied, vstored = sem("pr_vmm"), sem("pr_vcopied"), sem("pr_vstored")
        conv_ready, silu_done, tail_done = sem("pr_conv", 2), sem("pr_silu", 2), sem("pr_tails", 2)
        kept = sem("pr_kept")
        chains = sem("pr_chain")
        block = begin(nc, ctx)

        @block.sync
        def _(sp):
            sp.dma_start(wvd[:], io["w_vdt"][:]).then_inc(wvd_in, 16)
            sp.dma_start(hist[:], io["conv_hist"][:]).then_inc(small_in, 16)
            sp.dma_start(cw[:], io["conv_w"][:]).then_inc(small_in, 16)
            with sp.Fori(0, turns + XT) as i:
                for s in range(2):
                    sp.wait_ge(mm[s], i + START)
                    sp.dma_start(w[:, s], io["w_main"][ds(i * 2 + s, 1)].rearrange("m p k c -> p (m k) c")).then_inc(w_in[s], 16)
            sp.wait_ge(vcopied, NT + START)
            sp.dma_start(scr["vd"][:], vd[:]).then_inc(vstored, 16)
            sp.dma_start(io["v_prompt"][:], vd[:, NT - 2, 0:KV]).then_inc(vstored, 16)
            sp.dma_start(io["v_sample"][:], vd[:, NT - 1, 0:KV]).then_inc(vstored, 16)
            for s in range(2):
                sp.wait_ge(tail_done[s], XT + START)
            sp.dma_start(io["conv_prompt"][:], tail_p[:]).then_inc(kept, 16)
            sp.dma_start(io["conv_sample"][:], tail_s[:]).then_inc(kept, 16)
            sp.wait_ge(vstored, 48 + START)
            sp.wait_ge(kept, 32 + START)

        @block.tensor
        def _(pe):
            pe.wait_ge(wvd_in, 16 + START)
            for t in range(NT):
                if t >= 2:
                    pe.wait_ge(vcopied, t - 1 + START)
                for k in range(KD):
                    last = nc.tensor.matmul(pv[:, t % 2, 0:KV + H], h[:, k, t * P:(t + 1) * P], wvd[:, k], start=(k == 0), stop=(k == KD - 1))
                last.then_inc(vmm, 1)
            with pe.Fori(0, turns + XT) as i:
                for s in range(2):
                    pe.wait_ge(w_in[s], i * 16 + 16 + START)
                    pe.wait_ge(evac[s], i + START)
                    product(nc, ps[:, s], w[:, s], h, KD).then_inc(mm[s], 1)

        @block.scalar
        def _(act):
            for first, count, func in runs:
                f = first // 2
                with act.Fori(f, f + count // 2) as i:
                    for s in range(2):
                        act.wait_ge(mm[s], i + 1 + START)
                        act.wait_ge(stored[s], i * 16 + START)
                        nc.scalar.activation(o[:, s], ps[:, s, 0:T], func).then_inc(evac[s], 1)
                        act.wait_ge(evac[s], i + 1 + START)
                        act.dma_start(scr["plain"][ds(i * 2 + s, 1)].rearrange("m p t -> p (m t)"), o[:, s]).then_inc(stored[s], 16)
            with act.Fori(0, XT) as i:
                for s in range(2):
                    act.wait_ge(mm[s], i + turns + 1 + START)
                    act.wait_ge(tail_done[s], i + START)
                    nc.scalar.copy(raw[:, s, TAPS - 1:PADP], ps[:, s, 0:SEQ])
                    nc.scalar.copy(raw[:, s, PADP:].rearrange("p (b t) -> p b t", t=PADS)[:, :, TAPS - 1:], samples(ps[:, s])).then_inc(evac[s], 1)
                    act.wait_ge(conv_ready[s], i + 1 + START)
                    act.wait_ge(stored[s], (i + turns) * 16 + START)
                    nc.scalar.activation(o[:, s], acc2[:, s], ACT.Silu).then_inc(silu_done[s], 1)
                    act.wait_ge(silu_done[s], i + 1 + START)
                    act.dma_start(scr["xbc"][ds(i * 2 + s, 1)].rearrange("m p t -> p (m t)"), o[:, s]).then_inc(stored[s], 16)
            for s in range(2):
                act.wait_ge(stored[s], (turns + XT) * 16 + START)

        @block.vector
        def _(dve):
            for t in range(NT):
                dve.wait_ge(vmm, t + 1 + START)
                nc.vector.tensor_copy(vd[:, t], pv[:, t % 2, 0:KV + H]).then_inc(vcopied, 1)
            Steps(dve, chains).step(nc.vector.memset(raw[:, :, 0:TAPS - 1], 0.0))
            dve.wait_ge(small_in, 32 + START)
            with dve.Fori(0, XT) as i:
                ch = Steps(dve, chains, 12, i, before=1)
                for s in range(2):
                    rp, rs = raw[:, s, 0:PADP], raw[:, s, PADP:].rearrange("p (b t) -> p b t", t=PADS)
                    dve.wait_ge(evac[s], i + turns + 1 + START)
                    m = i * 2 + s
                    ch.step(nc.vector.tensor_copy(rs[:, :, 0:TAPS - 1], hist[:, ds(m, 1)].rearrange("p m (b t) -> p (m b) t", t=TAPS - 1)))
                    ch.link(nc.vector.tensor_copy(cwt[:, s], cw[:, ds(m, 1)].rearrange("p m j -> p (m j)")))
                    dve.wait_ge(silu_done[s], i + START)
                    views = ((rp, lambda j: rp[:, j:j + SEQ], lambda a: a[:, s, 0:SEQ]),
                             (rs, lambda j: rs[:, :, j:j + TS], lambda a: samples(a[:, s])))
                    bufs = (acc, acc2, acc, acc2)
                    for j in range(TAPS):
                        for _, src, dst in views:
                            if j == 0:
                                ins = nc.vector.tensor_scalar(dst(bufs[0]), src(0), cwt[:, s, 0:1], cwt[:, s, TAPS:TAPS + 1], ALU.mult, ALU.add)
                            else:
                                ins = nc.vector.scalar_tensor_tensor(out=dst(bufs[j]), in0=src(j), scalar=cwt[:, s, j:j + 1], in1=dst(bufs[j - 1]), op0=ALU.mult, op1=ALU.add)
                        if j < TAPS - 1:
                            ch.link(ins)
                        else:
                            ins.then_inc(conv_ready[s], 1)
                    ch.step(nc.vector.tensor_copy(tail_p[:, ds(m, 1)].rearrange("p m t -> p (m t)"), rp[:, SEQ:PADP]))
                    nc.vector.tensor_copy(tail_s[:, ds(m, 1)].rearrange("p m (b t) -> p (m b) t", t=TAPS - 1), rs[:, :, TS:PADS]).then_inc(tail_done[s], 1)
                    ch.wait()
                ch.close()


def phase_decay(nc, io, per, scr, vec):
    NP8 = NT - 1
    with ExitStack() as ctx:
        sb, pb, sem = open_(nc, ctx)
        raw, rows = sb("dc_raw", [P, NT, H]), sb("dc_rows", [P, 2, H])
        t1, t2 = sb("dc_t1", [P, NT, H]), sb("dc_t2", [P, NT, H])
        rate = sb("dc_rate", [P, H])
        dt, na, a, toend = (sb("dc_" + n, [P, NT, H]) for n in ("dt", "na", "a", "toend"))
        ps = pb("dc_ps", [P, 2, 512])
        loaded, chain, exped, logged, summed, ended = (sem("dc_" + n) for n in ("in", "chain", "exp", "log", "sum", "end"))
        block = begin(nc, ctx)
        tri = [per["const"][:, C_TRI + n * P:C_TRI + (n + 1) * P] for n in range(2)]
        stri = [per["const"][:, C_STRI + n * P:C_STRI + (n + 1) * P] for n in range(2)]

        @block.sync
        def _(sp):
            sp.dma_start(raw[:], scr["vd"][:, :, KV:KV + H]).then_inc(loaded, 16)
            sp.dma_start(rows[:], io["dt_rows"][:]).then_inc(loaded, 16)

        @block.vector
        def _(dve):
            v, ch = nc.vector, Steps(dve, chain)
            dve.wait_ge(loaded, 32 + START)
            ch.link(v.tensor_tensor(raw[:], raw[:], rows[:, 0].unsqueeze(1).to_broadcast([P, NT, H]), ALU.add))
            ch.link(v.tensor_scalar(t1[:], raw[:], -1.0, None, ALU.mult))
            ch.link(v.tensor_tensor(t1[:], t1[:], raw[:], ALU.min))
            dve.wait_ge(logged, 1 + START)
            ch.link(v.scalar_tensor_tensor(out=dt[:], in0=raw[:], scalar=0.0, in1=t2[:], op0=ALU.max, op1=ALU.add))
            ch.link(v.tensor_tensor(na[:], dt[:], rate[:].unsqueeze(1).to_broadcast([P, NT, H]), ALU.mult))
            ch.link(v.tensor_scalar(a[:], na[:], -1.0, None, ALU.mult))
            dve.wait_ge(ended, 1 + START)
            ch.link(v.tensor_tensor(toend[:], toend[:], dt[:], ALU.mult))
            dve.wait_ge(summed, 1 + START)
            by_group = lambda x: x[:].rearrange("p t (g r) -> p t g r", g=G)
            for n, x in ((0, a), (2, dt), (3, toend)):
                ch.link(v.tensor_copy(vec[:, :, n].rearrange("p g t r -> p t g r"), by_group(x)))
            ch.link(v.tensor_copy(vec[:, :, 1].rearrange("p g t r -> p t g r"), ps[:, 0, 0:NT * H].rearrange("p (t g r) -> p t g r", g=G, t=NT)))

        @block.scalar
        def _(act):
            act.wait_ge(loaded, 32 + START)
            nc.scalar.activation(rate[:], rows[:, 1], ACT.Exp).then_inc(exped, 1)
            act.wait_ge(chain, 3 + START)
            nc.scalar.activation(t2[:], t1[:], ACT.Exp).then_inc(exped, 1)
            act.wait_ge(exped, 2 + START)
            nc.scalar.activation(t2[:], t2[:], ACT.Ln, bias=1.0).then_inc(logged, 1)
            act.wait_ge(summed, 1 + START)
            nc.scalar.activation(toend[:], ps[:, 1, 0:NT * H].rearrange("p (t h) -> p t h", t=NT), ACT.Exp).then_inc(ended, 1)

        @block.tensor
        def _(pe):
            pe.wait_ge(chain, 6 + START)
            for b, (m, x) in enumerate(((tri, na), (stri, a))):
                nc.tensor.matmul(ps[:, b, 0:NP8 * H], m[0], x[:, 0:NP8].rearrange("p t h -> p (t h)"), start=True, stop=True)
                last = nc.tensor.matmul(ps[:, b, NP8 * H:NT * H], m[1], x[:, NP8], start=True, stop=True)
            last.then_inc(summed, 1)


def phase_ssd(nc, io, per, scr):
    with ExitStack() as ctx0:
        vec = ctx0.enter_context(nc.sbuf_tensor("decay_vec", [P, G, 4, NT, R], F32))
        phase_decay(nc, io, per, scr, vec)
        ssd_groups(nc, io, per, scr, vec)


def ssd_groups(nc, io, per, scr, vec):
    LAST = NT - 1
    CH = 18
    W = R * HD
    with ExitStack() as ctx:
        sb, pb, sem = open_(nc, ctx)
        xT, bT, cT, zT = sb("sd_xT", [P, 2, 2, T]), sb("sd_bT", [P, 2, T]), sb("sd_cT", [P, 2, T]), sb("sd_zT", [P, 2, 2, T])
        h0 = sb("sd_h0", [P, NB, W])
        hp = sb("sd_h", [P, W])
        vg = sb("sd_vec", [P, 2, 4, NT, R])
        skip, gain = sb("sd_skip", [P, G, 2]), sb("sd_gain", [P, G, 2])
        sg = sb("sd_skip_gain", [P, 2, 2, 2])
        y, sq, rs = sb("sd_y", [P, 2, 2, T]), sb("sd_sq", [P, 2, T]), sb("sd_rs", [P, T])
        xdt, xe, bk = sb("sd_xdt", [P, 2, W]), sb("sd_xe", [P, 2, W]), sb("sd_bk", [P, 2, N])
        seg, dec, ea, mt, cts = (sb("sd_" + n, [P, 2, R, P]) for n in ("seg", "dec", "ea", "mt", "cts"))
        xeb = sb("sd_xeb", [P, 2, W])
        psT = pb("sd_psT", [P, 2, 512])
        psA = pb("sd_psA", [P, 2, 512])
        psY = pb("sd_psY", [P, 2, 512])
        psR = pb("sd_psR", [P, 2, 512])
        x_in, h_in = sem("sd_in", 2), sem("sd_h_in")
        small = sem("sd_small")
        vg_ready = sem("sd_vg", 2)
        tr, cum = sem("sd_tr", 2), sem("sd_cum", 2)
        xdt_r, bk_r, seg_r, ea_r, dec_r, mt_r, cts_r = (sem("sd_" + n, 2) for n in ("xdtr", "bkr", "segr", "ear", "decr", "mtr", "ctsr"))
        y_r, s_r, y_read, h_done = (sem("sd_" + n, 2) for n in ("yr", "sr", "yread", "hdone"))
        xeb_r, sb_r, sb_done = (sem("sd_" + n, 2) for n in ("xebr", "sbr", "sbdone"))
        sq_r, var_r, root_r = (sem("sd_" + n) for n in ("sqr", "varr", "rootr"))
        y_out, y_st, hs_st, hp_st = sem("sd_yout", 2), sem("sd_yst", 2), sem("sd_hsst"), sem("sd_hpst")
        yg_r = sem("sd_yg")
        chain = sem("sd_chain")
        block = begin(nc, ctx)
        ident, ones = per["const"][:, C_ID:C_ID + P], per["const"][:, C_ONE:C_ONE + P]
        tri = [per["const"][:, C_TRI + n * P:C_TRI + (n + 1) * P] for n in range(2)]
        neg = [per["const"][:, C_NEG + n * P:C_NEG + (n + 1) * P] for n in range(2)]

        def chunk(s, c):
            k = s * NT + c
            return k % 2, k // 2, int(c == LAST), slice(c * P, (c + 1) * P)

        def previous(i, s, c):
            k = s * NT + c - 1
            return k % 2, i * (CH // 2) + k // 2 + 1

        SEMS_OF = (NB // 2, NB // 2 - 1)

        def sample_states_done(eng, i, s):
            q, u, _, _ = chunk(s, LAST)
            for e in range(2):
                eng.wait_ge(sb_done[e], (i * 2 + s + 1) * SEMS_OF[e] + START)
            eng.wait_ge(h_done[q], i * (CH // 2) + u + 1 + START)

        @block.sync
        def _(sp):
            sp.dma_start(skip[:], io["d_skip"][:]).then_inc(small, 16)
            sp.dma_start(gain[:], io["ssm_g"][:]).then_inc(small, 16)
            with sp.Fori(0, G // 2) as i:
                for s in range(2):
                    g = i * 2 + s
                    sp.wait_ge(y_out[s], i + START)
                    tile_of = lambda src, m: src[ds(m, 1)].rearrange("m p t -> p (m t)")
                    for j in range(2):
                        sp.dma_start(xT[:, s, j], tile_of(scr["xbc"], g * 2 + j)).then_inc(x_in[s], 16)
                        sp.dma_start(zT[:, s, j], tile_of(scr["plain"], g * 2 + (TZ + j))).then_inc(x_in[s], 16)
                    sp.dma_start(bT[:, s], tile_of(scr["xbc"], g + INNER // P)).then_inc(x_in[s], 16)
                    sp.dma_start(cT[:, s], tile_of(scr["xbc"], g + (INNER // P + G))).then_inc(x_in[s], 16)
                    sp.wait_ge(hs_st, g * 16 + START)
                    sp.dma_start(h0[:], io["ssm_in"][ds(g, 1)].rearrange("g n b w -> n (g b) w")).then_inc(h_in, 16)

        @block.tensor
        def _(pe):
            mm = nc.tensor.matmul

            def prepare(i, s, c):
                q, u, ms, at = chunk(s, c)
                u = i * (CH // 2) + u
                if c == 0:
                    pe.wait_ge(x_in[s], i * 96 + 96 + START)
                    pe.wait_ge(vg_ready[s], i + 1 + START)
                pe.wait_ge(xdt_r[q], u + START)
                pe.wait_ge(bk_r[q], u + START)
                pe.wait_ge(mt_r[q], u + START)
                for j in range(2):
                    nc.tensor.transpose(psT[:, q, j * P:(j + 1) * P], xT[:, s, j, at], ident)
                nc.tensor.transpose(psT[:, q, 2 * P:3 * P], bT[:, s, at], ident)
                mm(psT[:, q, 3 * P:4 * P], bT[:, s, at], cT[:, s, at], start=True, stop=True).then_inc(tr[q], 1)
                pe.wait_ge(seg_r[q], u + START)
                pe.wait_ge(ea_r[q], u + START)
                for r in range(R):
                    last = mm(psA[:, q, r * P:(r + 1) * P], vg[:, s, 0, c, r:r + 1].to_broadcast([P, P]), tri[ms], start=True, stop=True)
                last.then_inc(cum[q], 1)

            def scan(i, s, c):
                q, u, ms, at = chunk(s, c)
                u = i * (CH // 2) + u
                pe.wait_ge(mt_r[q], u + 1 + START)
                pe.wait_ge(xdt_r[q], u + 1 + START)
                pe.wait_ge(cts_r[q], u + 1 + START)
                pe.wait_ge(y_read[q], u + START)
                pe.wait_ge(h_done[q], u + START)
                if c == LAST:
                    pe.wait_ge(h_in, i * 32 + (s + 1) * 16 + START)
                elif c > 0:
                    pq, n = previous(i, s, c)
                    pe.wait_ge(h_done[pq], n + START)
                for r in range(R):
                    o = psY[HD * (r % 2):HD * (r % 2) + HD, q, (r // 2) * P:(r // 2 + 1) * P]
                    if c == LAST:
                        for b in range(NB):
                            t = slice(b * TS, (b + 1) * TS)
                            mm(o[:, t], h0[:, b, r * HD:(r + 1) * HD], cts[:, q, r, t], start=(b == 0), stop=False, skip_group_check=True)
                    elif c > 0:
                        mm(o, hp[:, r * HD:(r + 1) * HD], cts[:, q, r], start=True, stop=False)
                    last = mm(o, xdt[:, q, r * HD:(r + 1) * HD], mt[:, q, r], start=(c == 0), stop=True, skip_group_check=(c == LAST))
                last.then_inc(y_r[q], 1)
                pe.wait_ge(bk_r[q], u + 1 + START)
                if c < LAST:
                    mm(psY[:, q, 256:512], bk[:, q], xe[:, q], start=True, stop=True).then_inc(s_r[q], 1)
                    return
                for b in range(NB):
                    e, n = b % 2, b // 2
                    pe.wait_ge(xeb_r[e], i * NB + s * (NB // 2) + n + 1 + START)
                    if n == 0:
                        pe.wait_ge(root_r, i * 6 + s * 3 + START)
                    pe.wait_ge(sb_done[e], (i * 2 + s) * SEMS_OF[e] + n + START)
                    last = mm(psR[:, e, 0:W], bk[:, q], xeb[:, e], start=True, stop=True)
                    last.then_inc(s_r[q] if b == NB - 1 else sb_r[e], 1)

            with pe.Fori(0, G // 2) as i:
                for s in range(2):
                    prepare(i, s, 0)
                    for c in range(NT):
                        if c < LAST:
                            prepare(i, s, c + 1)
                        scan(i, s, c)
                    pe.wait_ge(sq_r, i * 2 + s + 1 + START)
                    sample_states_done(pe, i, s)
                    for n, (a, w) in enumerate(COLS):
                        if n == 2:
                            pe.wait_ge(root_r, i * 6 + s * 3 + 1 + START)
                        for j in range(2):
                            last = mm(psR[:, n % 2, 0:w], ones, sq[:, j, a:a + w], start=(j == 0), stop=(j == 1))
                        last.then_inc(var_r, 1)

        @block.scalar
        def _(act):
            with act.Fori(0, G // 2) as i:
                for s in range(2):
                    for c in range(NT):
                        q, u, ms, at = chunk(s, c)
                        u = i * (CH // 2) + u
                        act.wait_ge(tr[q], u + 1 + START)
                        act.wait_ge(s_r[q], u + START)
                        act.wait_ge(xdt_r[q], u + 1 + START)
                        nc.scalar.copy(bk[:, q], psT[:, q, 2 * P:3 * P]).then_inc(bk_r[q], 1)
                        act.wait_ge(cum[q], u + 1 + START)
                        act.wait_ge(cts_r[q], u + START)
                        act.wait_ge(h_done[q], u + START)
                        act.wait_ge(seg_r[q], u + 1 + START)
                        nc.scalar.activation(ea[:, q].rearrange("p r l -> p (r l)"), psA[:, q], ACT.Exp).then_inc(ea_r[q], 1)
                        act.wait_ge(mt_r[q], u + START)
                        for r in range(R):
                            last = nc.scalar.activation(dec[:, q, r], seg[:, q, r], ACT.Exp, bias=vg[:, s, 1, c, r:r + 1])
                        last.then_inc(dec_r[q], 1)
                    act.wait_ge(yg_r, i * 2 + s + 1 + START)
                    act.wait_ge(var_r, i * 6 + s * 3 + START)
                    nc.scalar.activation(sq[:], y[:, s], ACT.Square).then_inc(sq_r, 1)
                    act.wait_ge(y_out[1 - s], i + s + START)
                    for n, (a, w) in enumerate(COLS):
                        act.wait_ge(var_r, i * 6 + s * 3 + n + 1 + START)
                        nc.scalar.activation(rs[:, a:a + w], psR[:, n % 2, 0:w], ACT.Sqrt, bias=per["eps"][:, 0:1], scale=1.0 / W).then_inc(root_r, 1)
                    act.wait_ge(y_out[s], i + 1 + START)
                    act.dma_start(scr["ynorm"][ds((i * 2 + s) * 2, 2)].rearrange("m p t -> p m t"), y[:, s]).then_inc(y_st[s], 16)
                    sample_states_done(act, i, s)
                    act.dma_start(io["ssm_sample"][ds(i * 2 + s, 1)].rearrange("g n b w -> n (g b) w"), h0[:]).then_inc(hs_st, 16)
                    act.dma_start(io["ssm_prompt"][ds(i * 2 + s, 1)].rearrange("g n w -> n (g w)"), hp[:]).then_inc(hp_st, 16)
            for s in range(2):
                act.wait_ge(y_st[s], G // 2 * 16 + START)
            act.wait_ge(hs_st, G * 16 + START)
            act.wait_ge(hp_st, G * 16 + START)

        @block.gpsimd
        def _(pool):
            with pool.Fori(0, G // 2) as i:
                for s in range(2):
                    for c in range(NT):
                        q, u, ms, at = chunk(s, c)
                        u = i * (CH // 2) + u
                        pool.wait_ge(ea_r[q], u + 1 + START)
                        pool.wait_ge(y_r[q], u + START)
                        if c == 0:
                            pool.wait_ge(x_in[s], i * 96 + 96 + START)
                        nc.gpsimd.tensor_tensor(cts[:, q], cT[:, s, at].unsqueeze(1).to_broadcast([P, R, P]), ea[:, q], ALU.mult).then_inc(cts_r[q], 1)

        @block.vector
        def _(dve):
            v = nc.vector
            PER = 2 * (2 + (LAST - 1) + NB + 1)
            dve.wait_ge(small, 32 + START)
            with dve.Fori(0, G // 2) as i:
                ch = Steps(dve, chain, PER, i)
                for s in range(2):
                    g = i * 2 + s
                    v.tensor_copy(vg[:, s].rearrange("p k t r -> p (k t r)"), vec[:, ds(g, 1)].rearrange("p g k t r -> p (g k t r)")).then_inc(vg_ready[s], 1)
                    ch.link(v.tensor_copy(sg[:, s, 0], skip[:, ds(g, 1)].rearrange("p g j -> p (g j)")))
                    ch.link(v.tensor_copy(sg[:, s, 1], gain[:, ds(g, 1)].rearrange("p g j -> p (g j)")))
                    dve.wait_ge(vg_ready[s], i + 1 + START)
                    dve.wait_ge(x_in[s], i * 96 + 96 + START)
                    dve.wait_ge(y_st[s], i * 16 + START)

                    def before(c):
                        q, u, ms, at = chunk(s, c)
                        u = i * (CH // 2) + u
                        scaled = lambda out, kind: v.tensor_tensor(
                            out[:, q].rearrange("p (r d) -> p r d", d=HD), psT[:, q, 0:W].rearrange("p (r d) -> p r d", d=HD),
                            vg[:, s, kind, c].unsqueeze(2).to_broadcast([P, R, HD]), ALU.mult)
                        dve.wait_ge(cum[q], u + 1 + START)
                        v.tensor_tensor(seg[:, q], psA[:, q].rearrange("p (r l) -> p r l", r=R),
                                        neg[ms].unsqueeze(1).to_broadcast([P, R, P]), ALU.add).then_inc(seg_r[q], 1)
                        dve.wait_ge(tr[q], u + 1 + START)
                        dve.wait_ge(s_r[q], u + START)
                        scaled(xdt, 2)
                        scaled(xe, 3).then_inc(xdt_r[q], 1)
                        dve.wait_ge(dec_r[q], u + 1 + START)
                        dve.wait_ge(bk_r[q], u + 1 + START)
                        dve.wait_ge(y_r[q], u + START)
                        v.tensor_tensor(mt[:, q], dec[:, q], psT[:, q, 3 * P:4 * P].unsqueeze(1).to_broadcast([P, R, P]), ALU.mult).then_inc(mt_r[q], 1)

                    def after(c):
                        q, u, ms, at = chunk(s, c)
                        u = i * (CH // 2) + u
                        dve.wait_ge(y_r[q], u + 1 + START)
                        if c < LAST:
                            dve.wait_ge(s_r[q], u + 1 + START)
                        for j in range(2):
                            ins = v.scalar_tensor_tensor(out=y[:, s, j, at], in0=xT[:, s, j, at], scalar=sg[:, s, 0, j:j + 1],
                                                         in1=psY[:, q, j * P:(j + 1) * P], op0=ALU.mult, op1=ALU.add)
                        ins.then_inc(y_read[q], 1)
                        if c == 0:
                            dve.wait_ge(hp_st, g * 16 + START)
                            v.tensor_copy(hp[:], psY[:, q, 256:512]).then_inc(h_done[q], 1)
                        elif c < LAST:
                            hv = hp[:].rearrange("p (r d) -> p r d", d=HD)
                            pq, n = previous(i, s, c)
                            dve.wait_ge(h_done[pq], n + START)
                            ch.link(v.tensor_tensor(hv, hv, ea[:, q, :, P - 1:P].to_broadcast([P, R, HD]), ALU.mult))
                            v.tensor_tensor(hp[:], hp[:], psY[:, q, 256:512], ALU.add).then_inc(h_done[q], 1)
                        else:
                            dve.wait_ge(xdt_r[q], u + 1 + START)
                            dve.wait_ge(h_in, g * 16 + 16 + START)

                            def rows_of(b):
                                e, n = b % 2, b // 2
                                dve.wait_ge(sb_r[e], g * SEMS_OF[e] + n + START)
                                v.tensor_scalar(xeb[:, e], xe[:, q], per["const"][:, C_BM + b:C_BM + b + 1], None, ALU.mult).then_inc(xeb_r[e], 1)

                            def update(b):
                                e, n = b % 2, b // 2
                                hv = h0[:, b].rearrange("p (r d) -> p r d", d=HD)
                                ch.link(v.tensor_tensor(hv, hv, ea[:, q, :, b * TS + TS - 1:(b + 1) * TS].to_broadcast([P, R, HD]), ALU.mult))
                                if b < NB - 1:
                                    dve.wait_ge(sb_r[e], g * SEMS_OF[e] + n + 1 + START)
                                else:
                                    dve.wait_ge(s_r[q], u + 1 + START)
                                v.tensor_tensor(h0[:, b], h0[:, b], psR[:, e, 0:W], ALU.add).then_inc(h_done[q] if b == NB - 1 else sb_done[e], 1)

                            rows_of(0)
                            for b in range(NB):
                                if b < NB - 1:
                                    rows_of(b + 1)
                                update(b)

                    before(0)
                    for c in range(NT):
                        if c < LAST:
                            before(c + 1)
                        after(c)
                    q, u, _, _ = chunk(s, LAST)
                    dve.wait_ge(y_read[q], i * (CH // 2) + u + 1 + START)
                    v.tensor_tensor(y[:, s], y[:, s], zT[:, s], ALU.mult).then_inc(yg_r, 1)
                    dve.wait_ge(root_r, g * 3 + 3 + START)
                    ch.link(v.reciprocal(rs[:], rs[:]))
                    dve.wait_ge(yg_r, g + 1 + START)
                    for j in range(2):
                        ins = v.scalar_tensor_tensor(out=y[:, s, j], in0=y[:, s, j], scalar=sg[:, s, 1, j:j + 1], in1=rs[:], op0=ALU.mult, op1=ALU.mult)
                    ins.then_inc(y_out[s], 1)
                ch.close()


def phase_attention(nc, io, per, scr):
    SCALE = DH ** -0.5
    LAST = NT - 1
    K2 = 2 * P
    with ExitStack() as ctx:
        sb, pb, sem = open_(nc, ctx)
        qT, kT = sb("at_qT", [DH, 2, QH, T]), sb("at_kT", [DH, 2, T])
        v, vn = sb("at_v", [P, 2, NT, DH]), sb("at_vnew", [TS, 2, NB, DH])
        kc, vc = sb("at_kc", [DH, 2, NB, P]), sb("at_vc", [P, 2, NB, DH])
        sink_p, sink_s = sb("at_sink_p", [P, NKV, QH]), sb("at_sink_s", [P, NKV])
        sink = sb("at_sink", [P, 2, 2, QH])
        s_ = sb("at_s", [P, 2, QH, K2])
        pr = sb("at_p", [P, 2, QH, K2])
        pT = sb("at_pT", [P, 2, 2, QH * P])
        qs = sb("at_qs", [DH, 2, NB, QH * TS])
        mx, nm, es, den = (sb("at_" + n, [P, 2, QH]) for n in ("mx", "nm", "es", "den"))
        o = sb("at_o", [DH, 2, QH, T])
        psS = pb("at_psS", [P, 2, QH, K2])
        psT = pb("at_psT", [P, 2, QH * P])
        psO = pb("at_psO", [P, 2, QH * P])
        small, loaded, qs_r = sem("at_small"), sem("at_in", 2), sem("at_qsr", 2)
        s_r, m_r, nm_r, es_r, p_r, pn_r, pt_r, ptc_r, o_r, oc_r = (
            sem("at_" + n, 2) for n in ("sr", "mr", "nmr", "esr", "pr", "pnr", "ptr", "ptcr", "or", "ocr"))
        chain, o_st, copied = sem("at_chain"), sem("at_ost", 2), sem("at_kout")
        block = begin(nc, ctx)
        ident = per["const"][:, C_ID:C_ID + P]
        amask = per["const"][:, C_AM:C_AM + K2]
        heads = lambda x, a, n: x[ds(a, n)].rearrange("m (h d) t -> d (m h) t", d=DH)

        def tile_(s, c):
            k = s * NT + c
            return k % 2, k // 2

        def halves(c):
            return ((1, P),) if c == 0 else ((0, P), (1, P if c < LAST else TS))

        @block.sync
        def _(sp):
            sp.dma_start(sink_p[:], io["sink_prompt"][:]).then_inc(small, 16)
            sp.dma_start(sink_s[:], io["sink_sample"][:]).then_inc(small, 16)
            for n, t in (("k_prompt", NT - 2), ("k_sample", LAST)):
                sp.dma_start(io[n][:], scr["plain"][TK:TK + MK, :, t * P:(t + 1) * P]).then_inc(copied, 16)
            with sp.Fori(0, NKV // 2) as i:
                for s in range(2):
                    g = i * 2 + s
                    sp.wait_ge(o_st[s], i * 16 + START)
                    sp.dma_start(qT[:, s], heads(scr["plain"], TQ + g * 2, 2)).then_inc(loaded[s], 16)
                    sp.dma_start(kT[:, s], scr["plain"][ds(TK + i, 1)][:, s * DH:(s + 1) * DH].rearrange("m d t -> d (m t)")).then_inc(loaded[s], 16)
                    sp.dma_start(v[:, s], scr["vd"][:, :, ds(g * DH, DH)]).then_inc(loaded[s], 16)
                    sp.dma_start(vn[:, s], scr["vd"][:, LAST, ds(g * DH, DH)].rearrange("(b t) d -> t b d", t=TS)).then_inc(loaded[s], 16)
                    sp.dma_start(kc[:, s], io["k_cache"][ds(g, 1)].rearrange("g d b k -> d (g b) k")).then_inc(loaded[s], 16)
                    sp.dma_start(vc[:, s], io["v_cache"][ds(g, 1)].rearrange("g k b d -> k (g b) d")).then_inc(loaded[s], 16)
            sp.wait_ge(copied, 32 + START)

        @block.tensor
        def _(pe):
            mm = nc.tensor.matmul

            def scores(i, s, c):
                q, u = tile_(s, c)
                u = i * NT + u
                if c == 0:
                    pe.wait_ge(loaded[s], i * 96 + 96 + START)
                pe.wait_ge(m_r[q], u + START)
                if c < LAST:
                    lo = P if c == 0 else 0
                    for r in range(QH):
                        last = mm(psS[:, q, r, lo:K2], qT[:, s, r, c * P:(c + 1) * P], kT[:, s, (c - 1) * P + lo:(c + 1) * P], start=True, stop=True)
                else:
                    pe.wait_ge(qs_r[s], i + 1 + START)
                    for b in range(NB):
                        at = slice(SEQ + b * TS, SEQ + (b + 1) * TS)
                        rows, n = (slice(0, P), 2) if b % 2 == 0 else (slice(64, P), 1)
                        own = qs[:, s, b:b + n].rearrange("d b m -> d (b m)")
                        mm(psS[rows, q, b // 2, 0:P], own, kc[:, s, b], start=True, stop=True)
                        last = mm(psS[rows, q, b // 2, P:P + TS], own, kT[:, s, at], start=True, stop=True)
                last.then_inc(s_r[q], 1)

            def values(i, s, c):
                q, u = tile_(s, c)
                u = i * NT + u
                pe.wait_ge(pn_r[q], u + 1 + START)
                k = s * NT + c
                if k > 0:
                    pe.wait_ge(ptc_r[(k - 1) % 2], i * NT + (k - 1) // 2 + 1 + START)
                else:
                    pe.wait_ge(ptc_r[1], i * NT + START)
                for h, n in halves(c):
                    for r in range(QH):
                        last = nc.tensor.transpose(psT[0:n, h, r * P:(r + 1) * P], pr[:, q, r, h * P:h * P + n], ident)
                last.then_inc(pt_r[q], 1)
                pe.wait_ge(ptc_r[q], u + 1 + START)
                pe.wait_ge(oc_r[q], u + START)
                if c < LAST:
                    for h, n in halves(c):
                        last = mm(psO[0:DH, q], v[:, s, c - 1 + h], pT[:, q, h], start=(h == int(c == 0)), stop=(h == 1))
                else:
                    for b in range(NB):
                        rows = slice(b * 64, (b + 1) * 64)
                        mm(psO[0:DH, q, rows], vc[:, s, b], pT[:, q, 0, rows], start=True, stop=False)
                        last = mm(psO[0:DH, q, rows], vn[:, s, b], pT[0:TS, q, 1, rows], start=False, stop=True)
                last.then_inc(o_r[q], 1)

            with pe.Fori(0, NKV // 2) as i:
                for s in range(2):
                    scores(i, s, 0)
                    for c in range(NT):
                        if c < LAST:
                            scores(i, s, c + 1)
                        values(i, s, c)

        def columns(c):
            return slice(P, K2) if c == 0 else (slice(0, K2) if c < LAST else slice(0, P + TS))

        @block.scalar
        def _(act):
            with act.Fori(0, NKV // 2) as i:
                def exps(s, c):
                    q, u = tile_(s, c)
                    u = i * NT + u
                    ks = columns(c)
                    act.wait_ge(nm_r[q], u + 1 + START)
                    act.wait_ge(pt_r[q], u + START)
                    act.wait_ge(pn_r[q], u + START)
                    nc.scalar.activation(es[:, q], es[:, q], ACT.Exp).then_inc(es_r[q], 1)
                    for r in range(QH):
                        last = nc.scalar.activation(pr[:, q, r, ks], s_[:, q, r, ks], ACT.Exp, bias=nm[:, q, r:r + 1], scale=SCALE, accum_out=den[:, q, r:r + 1])
                    last.then_inc(p_r[q], 1)

                def outputs(s, c):
                    q, u = tile_(s, c)
                    u = i * NT + u
                    if c == 0:
                        act.wait_ge(o_st[s], i * 16 + START)
                    act.wait_ge(pt_r[q], u + 1 + START)
                    for h, n in halves(c):
                        last = nc.scalar.copy(pT[0:n, q, h], psT[0:n, h])
                    last.then_inc(ptc_r[q], 1)
                    act.wait_ge(o_r[q], u + 1 + START)
                    src = psO[0:DH, q]
                    if c < LAST:
                        ins = nc.scalar.copy(o[:, s, :, c * P:(c + 1) * P], src.rearrange("d (r t) -> d r t", r=QH))
                    else:
                        ins = nc.scalar.copy(o[:, s, :, SEQ:T].rearrange("d r (b t) -> d r b t", t=TS), src.rearrange("d (b r t) -> d r b t", r=QH, t=TS))
                    ins.then_inc(oc_r[q], 1)

                for s in range(2):
                    act.wait_ge(loaded[s], i * 96 + 96 + START)
                    nc.scalar.copy(qs[:, s].rearrange("d b (r t) -> d r b t", r=QH), qT[:, s, :, SEQ:T].rearrange("d r (b t) -> d r b t", t=TS)).then_inc(qs_r[s], 1)
                    exps(s, 0)
                    for c in range(NT):
                        if c < LAST:
                            exps(s, c + 1)
                        outputs(s, c)
                    for e in range(2):
                        k = s * NT + LAST - e
                        act.wait_ge(oc_r[k % 2], i * NT + k // 2 + 1 + START)
                    act.dma_start(heads(scr["attn"], (i * 2 + s) * 2, 2), o[:, s]).then_inc(o_st[s], 16)
            for s in range(2):
                act.wait_ge(o_st[s], NKV // 2 * 16 + START)

        @block.vector
        def _(dve):
            vv = nc.vector
            dve.wait_ge(small, 32 + START)
            with dve.Fori(0, NKV // 2) as i:
                ch = Steps(dve, chain, 2 * (2 + 4 * NT), i)
                for s in range(2):
                    g = i * 2 + s
                    ch.step(vv.tensor_copy(sink[:, s, 0], sink_p[:, ds(g, 1)].rearrange("p g r -> p (g r)")))
                    ch.link(vv.tensor_copy(sink[:, s, 1], sink_s[:, ds(g, 1)].to_broadcast([P, QH])))

                    def maxima(c):
                        q, u = tile_(s, c)
                        u = i * NT + u
                        ks = columns(c)
                        n = ks.stop - ks.start
                        dve.wait_ge(s_r[q], u + 1 + START)
                        dve.wait_ge(p_r[q], u + START)
                        if c < LAST:
                            ins = vv.tensor_tensor(s_[:, q, :, ks], psS[:, q, :, ks], amask[:, ks].unsqueeze(1).to_broadcast([P, QH, n]), ALU.add)
                        else:
                            ins = vv.tensor_copy(s_[:, q, :, ks], psS[:, q, :, ks])
                        ins.then_inc(m_r[q], 1)
                        dve.wait_ge(m_r[q], u + 1 + START)
                        ch.link(vv.tensor_reduce(mx[:, q], s_[:, q, :, ks], AX.X, ALU.max))
                        sk = sink[:, s, int(c == LAST)]
                        ch.link(vv.scalar_tensor_tensor(out=mx[:, q], in0=mx[:, q], scalar=SCALE, in1=sk, op0=ALU.mult, op1=ALU.max))
                        vv.tensor_tensor(es[:, q], sk, mx[:, q], ALU.subtract)
                        vv.tensor_scalar(nm[:, q], mx[:, q], -1.0, None, ALU.mult).then_inc(nm_r[q], 1)

                    def normalize(c):
                        q, u = tile_(s, c)
                        u = i * NT + u
                        ks = columns(c)
                        n = ks.stop - ks.start
                        dve.wait_ge(p_r[q], u + 1 + START)
                        dve.wait_ge(es_r[q], u + 1 + START)
                        ch.link(vv.tensor_tensor(den[:, q], den[:, q], es[:, q], ALU.add))
                        ch.link(vv.reciprocal(den[:, q], den[:, q]))
                        vv.tensor_tensor(pr[:, q, :, ks], pr[:, q, :, ks], den[:, q].unsqueeze(2).to_broadcast([P, QH, n]), ALU.mult).then_inc(pn_r[q], 1)

                    maxima(0)
                    for c in range(NT):
                        if c < LAST:
                            maxima(c + 1)
                        normalize(c)
                ch.close()


def load_tiles(sp, dst, src, n, loaded):
    for k in range(n):
        sp.dma_start(dst[:, k], src[k]).then_inc(loaded, 16)


def phase_merge(nc, io, per, scr):
    KS, KA = INNER // P, ATTN // P
    with ExitStack() as ctx:
        sb, pb, sem = open_(nc, ctx)
        ys, ya = sb("mg_ys", [P, KS, T]), sb("mg_ya", [P, KA, T])
        ws, wa = sb("mg_ws", [P, 2, KS, P]), sb("mg_wa", [P, 2, KA, P])
        gates = sb("mg_gates", [P, 2, T])
        out = sb("mg_out", [P, 2, T])
        ps = pb("mg_ps", [P, 2, TB])
        acts, w_in, g_in = sem("mg_acts"), sem("mg_win", 2), sem("mg_gin", 2)
        mm, used, stored, chain = sem("mg_mm", 2), sem("mg_used", 2), sem("mg_stored"), sem("mg_chain")
        block = begin(nc, ctx)

        @block.sync
        def _(sp):
            load_tiles(sp, ys, scr["ynorm"], KS, acts)
            load_tiles(sp, ya, scr["attn"], KA, acts)
            one = lambda src, m: src[ds(m, 1)].rearrange("m p k c -> p (m k) c")
            with sp.Fori(0, KD // 2) as i:
                for s in range(2):
                    m = i * 2 + s
                    sp.wait_ge(mm[0], m + START)
                    sp.wait_ge(mm[1], m + START)
                    sp.dma_start(ws[:, s], one(io["w_ssm"], m)).then_inc(w_in[s], 16)
                    sp.dma_start(wa[:, s], one(io["w_attn"], m)).then_inc(w_in[s], 16)
                    sp.wait_ge(used[1], m + START)
                    for n in range(2):
                        sp.dma_start(gates[:, n], scr["plain"][ds(m + (TG + n * KD), 1)].rearrange("m p t -> p (m t)")).then_inc(g_in[s], 16)

        @block.tensor
        def _(pe):
            pe.wait_ge(acts, (KS + KA) * 16 + START)
            with pe.Fori(0, KD // 2) as i:
                for s in range(2):
                    m = i * 2 + s
                    pe.wait_ge(w_in[s], i * 32 + 32 + START)
                    for n, (w, y, k) in enumerate(((ws, ys, KS), (wa, ya, KA))):
                        pe.wait_ge(used[n], m + START)
                        product(nc, ps[:, n], w[:, s], y, k).then_inc(mm[n], 1)

        @block.vector
        def _(dve):
            v = nc.vector
            with dve.Fori(0, KD // 2) as i:
                for s in range(2):
                    m = i * 2 + s
                    dve.wait_ge(g_in[s], i * 32 + 32 + START)
                    for n in range(2):
                        dve.wait_ge(mm[n], m + 1 + START)
                        if n == 0:
                            dve.wait_ge(stored, m * 16 + START)
                        v.tensor_tensor(out[:, n], ps[:, n, 0:T], gates[:, n], ALU.mult).then_inc(used[n], 1)
                    dve.wait_ge(used[0], m + 1 + START)
                    dve.wait_ge(used[1], m + 1 + START)
                    v.tensor_tensor(out[:, 0], out[:, 0], out[:, 1], ALU.add).then_inc(chain, 1)

        @block.scalar
        def _(act):
            with act.Fori(0, KD) as m:
                act.wait_ge(chain, m + 1 + START)
                act.dma_start(scr["merged"][ds(m, 1)].rearrange("m p t -> p (m t)"), out[:, 0]).then_inc(stored, 16)
            act.wait_ge(stored, KD * 16 + START)


def phase_out(nc, io, per, scr):
    with ExitStack() as ctx:
        sb, pb, sem = open_(nc, ctx)
        y, x = sb("ou_y", [P, KD, T]), sb("ou_x", [P, KD, T])
        w = sb("ou_w", [P, 2, KD, P])
        g1 = sb("ou_gate", [P, 2, NC_])
        t, o = sb("ou_t", [P, 2, T]), sb("ou_o", [P, 2, T])
        ps = pb("ou_ps", [P, 2, TB])
        acts, w_in, mm, used, done, stored = sem("ou_acts"), sem("ou_win", 2), sem("ou_mm", 2), sem("ou_used", 2), sem("ou_done", 2), sem("ou_stored", 2)
        gate_r = sem("ou_gate_r")
        block = begin(nc, ctx)

        @block.sync
        def _(sp):
            load_tiles(sp, y, scr["merged"], KD, acts)
            sp.dma_start(x[:], io["x"][:]).then_inc(acts, 16)
            with sp.Fori(0, KD // 2) as i:
                for s in range(2):
                    sp.wait_ge(mm[s], i + START)
                    sp.dma_start(w[:, s], io["w_out"][ds(i * 2 + s, 1)].rearrange("m p k c -> p (m k) c")).then_inc(w_in[s], 16)

        @block.tensor
        def _(pe):
            pe.wait_ge(acts, (KD + 1) * 16 + START)
            with pe.Fori(0, KD // 2) as i:
                for s in range(2):
                    pe.wait_ge(w_in[s], i * 16 + 16 + START)
                    pe.wait_ge(used[s], i + START)
                    product(nc, ps[:, s], w[:, s], y, KD).then_inc(mm[s], 1)

        @block.vector
        def _(dve):
            v = nc.vector
            dve.wait_ge(acts, (KD + 1) * 16 + START)
            with dve.Fori(0, KD // 2) as i:
                for s in range(2):
                    m = i * 2 + s
                    v.tensor_copy(g1[:, s], per["mod"][:, ds(m + 2 * KD, 1)].rearrange("p m c -> p (m c)")).then_inc(gate_r, 1)
                    dve.wait_ge(gate_r, m + 1 + START)
                    dve.wait_ge(mm[s], i + 1 + START)
                    dve.wait_ge(stored[s], i * 16 + START)
                    v.tensor_scalar(t[:, s, 0:SEQ], ps[:, s, 0:SEQ], g1[:, s, 0:1], None, ALU.mult)
                    v.tensor_tensor(samples(t[:, s]), samples(ps[:, s]), g1[:, s, 1:NC_].unsqueeze(2).to_broadcast([P, NB, TS]), ALU.mult).then_inc(used[s], 1)
                    dve.wait_ge(used[s], i + 1 + START)
                    v.tensor_tensor(o[:, s], t[:, s], x[:, ds(m, 1)].rearrange("p m t -> p (m t)"), ALU.add).then_inc(done[s], 1)

        @block.scalar
        def _(act):
            with act.Fori(0, KD // 2) as i:
                for s in range(2):
                    act.wait_ge(done[s], i + 1 + START)
                    act.dma_start(scr["x1"][ds(i * 2 + s, 1)].rearrange("m p t -> p (m t)"), o[:, s]).then_inc(stored[s], 16)
            for s in range(2):
                act.wait_ge(stored[s], KD // 2 * 16 + START)


def phase_peer(nc, io, per, scr):
    with ExitStack() as ctx:
        h2 = ctx.enter_context(nc.sbuf_tensor("h2", [P, KD, T], F32))
        with ExitStack() as ctx2:
            picks = ctx2.enter_context(nc.sbuf_tensor("picks", [P, 3, T], F32))
            with nc.sbuf_tensor("top_v", [P, NT, 2 * PH, TOPK], F32) as top_v, nc.sbuf_tensor("top_i", [P, NT, 2 * PH, TOPK], F32) as top_i:
                phase_norm2(nc, io, per, scr, h2)
                phase_keys(nc, io, per, h2, top_v, top_i)
                phase_picks(nc, io, per, top_v, top_i, picks)
            phase_gates(nc, io, per, scr, picks)
        phase_experts(nc, io, per, scr, h2)


def phase_norm2(nc, io, per, scr, h2):
    with ExitStack() as ctx:
        sb, pb, sem = open_(nc, ctx)
        x = sb("n2_x", [P, KD, T])
        sq, tmp, rstd = sb("n2_sq", [P, 2, T]), sb("n2_tmp", [P, 2, T]), sb("n2_rstd", [P, T])
        ps = pb("n2_ps", [P, TB])
        x_in = sem("n2_x_in")
        sems = [sem(f"n2_{n}") for n in ("squared", "summed", "rooted", "chain")]
        block = begin(nc, ctx)

        @block.sync
        def _(sp):
            load_tiles(sp, x, scr["x1"], KD, x_in)
        norm_engines(nc, block, per, x, x_in, KD * 16, sq, ps, rstd, sems, modulated(nc, per, x, rstd, h2, 1, 3 * KD, tmp))


def top16(v, ch, vals, idx, spare, src):
    ch.link(v.max(vals[:, 0:8], src))
    ch.step(v.max_index(idx[:, 0:8], vals[:, 0:8], src))
    ch.link(v.match_replace(spare, vals[:, 0:8], src, NEG))
    ch.link(v.max(vals[:, 8:16], spare))
    ch.link(v.max_index(idx[:, 8:16], vals[:, 8:16], spare))


def phase_keys(nc, io, per, h2, top_v, top_i):
    with ExitStack() as ctx:
        sb, pb, sem = open_(nc, ctx)
        w, keys = sb("ky_w", [P, 2, KD, P]), sb("ky_keys", [P, 2, N_KEYS])
        q = sb("ky_q", [P, 2, T])
        val, idx = sb("ky_val", [P, 2, NT, TOPK]), sb("ky_idx", [P, 2, NT, TOPK], U32)
        spare = sb("ky_spare", [P, N_KEYS])
        score = sb("ky_score", [P, 2, NT, N_KEYS])
        ps, psk = pb("ky_ps", [P, TB]), pb("ky_psk", [P, TB])
        w_in, mm, q_r, sc_mm, sc_r, done = (sem("ky_" + n, 2) for n in ("win", "mm", "qr", "scmm", "scr", "done"))
        chain = sem("ky_chain")
        block = begin(nc, ctx)

        @block.sync
        def _(sp):
            with sp.Fori(0, PH) as i:
                for s in range(2):
                    sp.wait_ge(sc_mm[s], i + START)
                    sp.dma_start(w[:, s], io["w_query"][ds(i * 2 + s, 1)].rearrange("m p k c -> p (m k) c")).then_inc(w_in[s], 16)
                    sp.dma_start(keys[:, s], io["keys"][ds(i * 2 + s, 1)].rearrange("m d k -> d (m k)")).then_inc(w_in[s], 16)

        @block.tensor
        def _(pe):
            with pe.Fori(0, PH) as i:
                for s in range(2):
                    pe.wait_ge(w_in[s], i * 32 + 32 + START)
                    pe.wait_ge(q_r[1 - s], i + s + START)
                    product(nc, ps, w[:, s], h2, KD).then_inc(mm[s], 1)
                    pe.wait_ge(q_r[s], i + 1 + START)
                    pe.wait_ge(sc_r[1 - s], i + s + START)
                    for t in range(NT):
                        last = nc.tensor.matmul(psk[:, t * P:(t + 1) * P], q[:, s, t * P:(t + 1) * P], keys[:, s], start=True, stop=True)
                    last.then_inc(sc_mm[s], 1)

        @block.scalar
        def _(act):
            with act.Fori(0, PH) as i:
                for s in range(2):
                    act.wait_ge(mm[s], i + 1 + START)
                    act.wait_ge(sc_mm[s], i + START)
                    nc.scalar.copy(q[:, s], ps[:, 0:T]).then_inc(q_r[s], 1)

        @block.vector
        def _(dve):
            v = nc.vector
            with dve.Fori(0, PH) as i:
                ch = Steps(dve, chain)
                for s in range(2):
                    dve.wait_ge(sc_mm[s], i + 1 + START)
                    v.tensor_copy(score[:, s].rearrange("p t k -> p (t k)"), psk[:, 0:T]).then_inc(sc_r[s], 1)
                    dve.wait_ge(sc_r[s], i + 1 + START)
                    ch.link(v.memset(spare[:], NEG))
                    for t in range(NT):
                        top16(v, ch, val[:, s, t], idx[:, s, t], spare[:], score[:, s, t])
                    m = i * 2 + s
                    v.tensor_copy(top_v[:, :, ds(m, 1)].rearrange("p t m k -> p t (m k)"), val[:, s])
                    v.tensor_copy(top_i[:, :, ds(m, 1)].rearrange("p t m k -> p t (m k)"), idx[:, s]).then_inc(done[s], 1)
                    dve.wait_ge(done[s], i + 1 + START)
                ch.link(v.memset(spare[:], NEG))
                dve.sem_clear(chain)
                dve.sem_inc(chain, START)


def phase_picks(nc, io, per, top_v, top_i, picks):
    KK = TOPK * TOPK
    with ExitStack() as ctx:
        sb, pb, sem = open_(nc, ctx)
        sv, si = sb("pk_sv", [P, 2 * PH, TOPK]), sb("pk_si", [P, 2 * PH, TOPK])
        comb, spare = sb("pk_comb", [P, PH, KK]), sb("pk_spare", [P, 2, KK])
        fv, fi = sb("pk_fv", [P, PH, TOPK]), sb("pk_fi", [P, PH, TOPK], U32)
        half_u, half = sb("pk_half_u", [P, 2, HK], U32), sb("pk_half", [P, 2, HK])
        hot = sb("pk_hot", [P, HK, TOPK])
        out = sb("pk_out", [P, 3, HK])
        e, den = sb("pk_e", [P, PH, TOPK]), sb("pk_den", [P, PH])
        ps = pb("pk_ps", [P, 3, P])
        chain, e_in, e_out, o_r, tr, copied = (sem("pk_" + n) for n in ("chain", "ein", "eout", "or", "tr", "copied"))
        block = begin(nc, ctx)
        ident = per["const"][:, C_ID:C_ID + P]
        iota = per["const"][:, C_IOTA:C_IOTA + TOPK]

        @block.vector
        def _(dve):
            v = nc.vector
            with dve.Fori(0, NT) as t:
                ch = Steps(dve, chain)
                ch.step(v.tensor_copy(sv[:], top_v[:, ds(t, 1)].rearrange("p t m k -> p (t m) k")))
                ch.link(v.tensor_copy(si[:], top_i[:, ds(t, 1)].rearrange("p t m k -> p (t m) k")))
                halves = lambda x, n: x[:].rearrange("p (h n) k -> p n h k", n=2)[:, n]
                ch.link(v.tensor_tensor(comb[:].rearrange("p h (a b) -> p h a b", a=TOPK), halves(sv, 0).unsqueeze(3).to_broadcast([P, PH, TOPK, TOPK]),
                                        halves(sv, 1).unsqueeze(2).to_broadcast([P, PH, TOPK, TOPK]), ALU.add))
                for h in range(PH):
                    top16(v, ch, fv[:, h], fi[:, h], spare[:, h % 2], comb[:, h])
                dve.wait_ge(e_out, t + START)
                v.tensor_tensor(e[:], fv[:], fv[:, :, 0:1].to_broadcast([P, PH, TOPK]), ALU.subtract).then_inc(e_in, 1)
                picked = fi[:].rearrange("p h k -> p (h k)")
                ch.step(v.tensor_scalar(half_u[:, 0], picked, 4, None, ALU.logical_shift_right))
                ch.link(v.tensor_scalar(half_u[:, 1], picked, TOPK - 1, None, ALU.bitwise_and))
                ch.link(v.tensor_copy(half[:], half_u[:]))
                dve.wait_ge(tr, t + START)
                for n in range(2):
                    ch.link(v.tensor_tensor(hot[:], half[:, n].unsqueeze(2).to_broadcast([P, HK, TOPK]), iota.unsqueeze(1).to_broadcast([P, HK, TOPK]), ALU.is_equal))
                    hv = hot[:].rearrange("p (h k) a -> p h k a", h=PH)
                    ch.link(v.tensor_tensor(hv, hv, halves(si, n).unsqueeze(2).to_broadcast([P, PH, TOPK, TOPK]), ALU.mult))
                    ch.link(v.tensor_reduce(out[:, n], hot[:], AX.X, ALU.add))
                dve.wait_ge(e_out, t + 1 + START)
                ch.link(v.tensor_reduce(den[:], e[:], AX.X, ALU.add))
                ch.link(v.reciprocal(den[:], den[:]))
                v.tensor_tensor(out[:, 2].rearrange("p (h k) -> p h k", h=PH), e[:], den[:].unsqueeze(2).to_broadcast([P, PH, TOPK]), ALU.mult).then_inc(o_r, 1)
                dve.sem_clear(chain)
                dve.sem_inc(chain, START)

        @block.tensor
        def _(pe):
            with pe.Fori(0, NT) as t:
                pe.wait_ge(o_r, t + 1 + START)
                pe.wait_ge(copied, t + START)
                for n in range(3):
                    last = nc.tensor.transpose(ps[:, n], out[:, n], ident)
                last.then_inc(tr, 1)

        @block.scalar
        def _(act):
            with act.Fori(0, NT) as t:
                act.wait_ge(e_in, t + 1 + START)
                act.wait_ge(o_r, t + START)
                nc.scalar.activation(e[:], e[:], ACT.Exp).then_inc(e_out, 1)
                act.wait_ge(tr, t + 1 + START)
                nc.scalar.copy(picks[:, :, ds(t * P, P)], ps[:]).then_inc(copied, 1)


def phase_gates(nc, io, per, scr, picks):
    B = 8
    NBAT = P // B
    with ExitStack() as ctx:
        sb, pb, sem = open_(nc, ctx)
        cur = sb("gt_cur", [P, 2, 3, B])
        one1, one2 = sb("gt_one1", [P, 2, B, P]), sb("gt_one2", [P, 2, B, P])
        stage = sb("gt_stage", [P, N_KEYS, P])
        ps = pb("gt_ps", [P, 2, B * P])
        cur_r, hot_r, mm, ev, stored = sem("gt_cur_r", 2), sem("gt_hot", 2), sem("gt_mm", 2), sem("gt_ev", 2), sem("gt_stored")
        block = begin(nc, ctx)
        iota = per["const"][:, C_IOTA:C_IOTA + P]

        @block.vector
        def _(dve):
            v = nc.vector
            with dve.Fori(0, NT * NBAT // 2) as i:
                for s in range(2):
                    v.tensor_copy(cur[:, s], picks[:, :, ds((i * 2 + s) * B, B)]).then_inc(cur_r[s], 1)
                    dve.wait_ge(cur_r[s], i + 1 + START)
                    dve.wait_ge(mm[s], i + START)
                    for b in range(B):
                        v.tensor_scalar(one1[:, s, b], iota, cur[:, s, 0, b:b + 1], None, ALU.is_equal)
                        last = v.tensor_scalar(one2[:, s, b], iota, cur[:, s, 1, b:b + 1], cur[:, s, 2, b:b + 1], ALU.is_equal, ALU.mult)
                    last.then_inc(hot_r[s], 1)

        @block.tensor
        def _(pe):
            with pe.Fori(0, NT * NBAT // 2) as i:
                for s in range(2):
                    pe.wait_ge(hot_r[s], i + 1 + START)
                    pe.wait_ge(ev[s], i + START)
                    for b in range(B):
                        last = nc.tensor.matmul(ps[:, s, b * P:(b + 1) * P], one1[:, s, b], one2[:, s, b], start=True, stop=True)
                    last.then_inc(mm[s], 1)

        @block.scalar
        def _(act):
            with act.Fori(0, NT) as t:
                act.wait_ge(stored, t * 16 + START)
                for j in range(NBAT):
                    s = j % 2
                    act.wait_ge(mm[s], t * (NBAT // 2) + j // 2 + 1 + START)
                    nc.scalar.copy(stage[:, :, j * B:(j + 1) * B].rearrange("p k t -> p t k"), ps[:, s].rearrange("p (t k) -> p t k", t=B)).then_inc(ev[s], 1)
                for s in range(2):
                    act.wait_ge(ev[s], (t + 1) * (NBAT // 2) + START)
                act.dma_start(scr["gate"][:, :, ds(t * P, P)], stage[:]).then_inc(stored, 16)
            act.wait_ge(stored, NT * 16 + START)


def phase_experts(nc, io, per, scr, h2):
    E = 4
    TURNS = N_KEYS // E // 2
    SUMS = (3 * KD // 2, 3 * KD // 2 - 1)
    with ExitStack() as ctx:
        sb, pb, sem = open_(nc, ctx)
        acc = sb("ex_acc", [P, KD, T])
        with ExitStack() as ctx2:
            sb2, pb2, _ = open_(nc, ctx2)
            u, vv = sb2("ex_u", [P, 2, KD, P]), sb2("ex_v", [P, 2, E, D])
            gate = sb2("ex_gate", [P, 2, T])
            act_ = sb2("ex_act", [P, 2, T])
            g = sb2("ex_g", [P, 2, E, T])
            ps, pv = pb2("ex_ps", [P, 2, TB]), pb2("ex_pv", [P, 2, 512])
            u_in, v_in, g_in, mm, gelu_r, g_r, used, sum_mm, sum_r = (sem("ex_" + n, 2) for n in ("uin", "vin", "gin", "mm", "gelur", "gr", "used", "summm", "sumr"))
            zero = sem("ex_zero")
            block = begin(nc, ctx2)

            @block.sync
            def _(sp):
                with sp.Fori(0, TURNS) as i:
                    for s in range(2):
                        sp.wait_ge(used[s], i + START)
                        sp.dma_start(vv[:, s], io["expert_v"][ds((i * 2 + s) * E, E)].rearrange("e p d -> p e d")).then_inc(v_in[s], 16)
                        for e in range(E):
                            k, z = (i * 2 + s) * E + e, e % 2
                            n = (i * 2 + s) * (E // 2) + e // 2
                            sp.wait_ge(mm[z], n + START)
                            sp.dma_start(u[:, z], io["expert_u"][ds(k, 1)].rearrange("e p k c -> p (e k) c")).then_inc(u_in[z], 16)
                            sp.wait_ge(g_r[z], n + START)
                            sp.dma_start(gate[:, z], scr["gate"][:, ds(k, 1)].rearrange("p e t -> p (e t)")).then_inc(g_in[z], 16)

            @block.tensor
            def _(pe):
                with pe.Fori(0, TURNS) as i:
                    for s in range(2):
                        for e in range(E):
                            z, n = e % 2, (i * 2 + s) * (E // 2) + e // 2
                            pe.wait_ge(u_in[z], n * 16 + 16 + START)
                            pe.wait_ge(gelu_r[z], n + START)
                            product(nc, ps[:, z], u[:, z], h2, KD).then_inc(mm[z], 1)
                        pe.wait_ge(v_in[s], i * 16 + 16 + START)
                        for z in range(2):
                            pe.wait_ge(g_r[z], (i * 2 + s + 1) * (E // 2) + START)
                        for d in range(KD):
                            for c, (a, w) in enumerate(COLS):
                                j = d * 3 + c
                                if j == 1:
                                    pe.wait_ge(used[1 - s], i + s + START)
                                else:
                                    pe.wait_ge(sum_r[j % 2], (i * 2 + s) * SUMS[j % 2] + j // 2 + START)
                                for e in range(E):
                                    last = nc.tensor.matmul(pv[:, j % 2, 0:w], vv[:, s, e, d * P:(d + 1) * P], g[:, s, e, a:a + w], start=(e == 0), stop=(e == E - 1))
                                last.then_inc(sum_mm[j % 2], 1)

            @block.scalar
            def _(act):
                with act.Fori(0, TURNS * 2) as b:
                    for e in range(E):
                        z, n = e % 2, b * (E // 2) + e // 2
                        act.wait_ge(mm[z], n + 1 + START)
                        act.wait_ge(g_r[z], n + START)
                        nc.scalar.activation(act_[:, z], ps[:, z, 0:T], ACT.Gelu_apprx_tanh).then_inc(gelu_r[z], 1)

            @block.vector
            def _(dve):
                v = nc.vector
                v.memset(acc[:], 0.0).then_inc(zero, 1)
                dve.wait_ge(zero, 1 + START)
                with dve.Fori(0, TURNS) as i:
                    for s in range(2):
                        dve.wait_ge(used[s], i + START)
                        for e in range(E):
                            z, n = e % 2, (i * 2 + s) * (E // 2) + e // 2
                            dve.wait_ge(gelu_r[z], n + 1 + START)
                            dve.wait_ge(g_in[z], n * 16 + 16 + START)
                            v.tensor_tensor(g[:, s, e], act_[:, z], gate[:, z], ALU.mult).then_inc(g_r[z], 1)
                        for d in range(KD):
                            for c, (a, w) in enumerate(COLS):
                                j = d * 3 + c
                                n = (i * 2 + s) * (3 * KD // 2) + j // 2
                                dve.wait_ge(sum_mm[j % 2], n + 1 + START)
                                v.tensor_tensor(acc[:, d, a:a + w], acc[:, d, a:a + w], pv[:, j % 2, 0:w], ALU.add).then_inc(used[s] if j == 3 * KD - 1 else sum_r[j % 2], 1)
        finish_output(nc, io, per, scr, acc)


def finish_output(nc, io, per, scr, acc):
    with ExitStack() as ctx:
        sb, pb, sem = open_(nc, ctx)
        x = sb("fo_x", [P, KD, T])
        fg = sb("fo_g", [P, KD])
        sq, rstd, y = sb("fo_sq", [P, 2, T]), sb("fo_rstd", [P, T]), sb("fo_y", [P, 2, T])
        ps = pb("fo_ps", [P, TB])
        x_in, x_r, y_st, y_r = sem("fo_xin"), sem("fo_xr"), sem("fo_yst", 2), sem("fo_yr")
        pre = sem("fo_pre")
        squared, summed, rooted, chain = (sem("fo_" + n) for n in ("sq", "sum", "root", "chain"))
        block = begin(nc, ctx)
        ones = per["const"][:, C_ONE:C_ONE + P]

        @block.sync
        def _(sp):
            load_tiles(sp, x, scr["x1"], KD, x_in)
            sp.dma_start(fg[:], io["final_g"][:]).then_inc(x_in, 16)
            for k in range(KD):
                sp.wait_ge(y_r, k + 1 + START)
                sp.dma_start(io["y"][k], y[:, k % 2]).then_inc(y_st[k % 2], 16)
            for s in range(2):
                sp.wait_ge(y_st[s], KD // 2 * 16 + START)

        @block.vector
        def _(dve):
            v, mod = nc.vector, per["mod"]
            dve.wait_ge(x_in, (KD + 1) * 16 + START)
            for k in range(KD):
                v.tensor_scalar(acc[:, k, 0:SEQ], acc[:, k, 0:SEQ], mod[:, 5 * KD + k, 0:1], None, ALU.mult)
                v.tensor_tensor(samples(acc[:, k]), samples(acc[:, k]), per_token(mod[:, 5 * KD:6 * KD], k), ALU.mult).then_inc(pre, 1)
            for k in range(KD):
                dve.wait_ge(pre, k + 1 + START)
                v.tensor_tensor(x[:, k], x[:, k], acc[:, k], ALU.add).then_inc(x_r, 1)
            dve.wait_ge(rooted, 1 + START)
            v.reciprocal(rstd[:], rstd[:]).then_inc(chain, 1)
            dve.wait_ge(chain, 1 + START)
            for k in range(KD):
                if k >= 2:
                    dve.wait_ge(y_st[k % 2], k // 2 * 16 + START)
                v.scalar_tensor_tensor(out=y[:, k % 2], in0=x[:, k], scalar=fg[:, k:k + 1], in1=rstd[:], op0=ALU.mult, op1=ALU.mult).then_inc(y_r, 1)

        @block.scalar
        def _(act):
            for k in range(KD):
                act.wait_ge(x_r, k + 1 + START)
                if k >= 2:
                    act.wait_ge(summed, k - 1 + START)
                nc.scalar.activation(sq[:, k % 2], x[:, k], ACT.Square).then_inc(squared, 1)
            act.wait_ge(summed, KD + START)
            nc.scalar.activation(rstd[:], ps[:, 0:T], ACT.Sqrt, bias=per["eps"][:, 0:1], scale=1.0 / D).then_inc(rooted, 1)

        @block.tensor
        def _(pe):
            for k in range(KD):
                pe.wait_ge(squared, k + 1 + START)
                for a, n in COLS:
                    last = nc.tensor.matmul(ps[:, a:a + n], ones, sq[:, k % 2, a:a + n], start=(k == 0), stop=(k == KD - 1))
                last.then_inc(summed, 1)


def build(nc, io, outs):
    io = dict(io, **outs)
    with ExitStack() as ctx:
        sb, pb, sem = open_(nc, ctx)
        dram = lambda name, shape: nc.dram_tensor(name, shape, F32, kind="Internal").ap()
        scr = {
            "plain": dram("scr_plain", [NPLAIN, P, T]), "xbc": dram("scr_xbc", [MX, P, T]),
            "vd": dram("scr_vd", [P, NT, KV + H]), "ynorm": dram("scr_ynorm", [INNER // P, P, T]),
            "attn": dram("scr_attn", [ATTN // P, P, T]), "merged": dram("scr_merged", [KD, P, T]),
            "x1": dram("scr_x1", [KD, P, T]), "gate": dram("scr_gate", [P, N_KEYS, T]),
        }
        per = {"const": sb("const", [P, C_N]), "mod": sb("mod", [P, 6 * KD, NC_]),
               "gain": sb("gain", [P, 2, KD, NC_]), "eps": sb("eps", [P, 1])}
        nc.vector.memset(per["eps"][:], EPS)
        phase_modulation(nc, io, per)
        with nc.sbuf_tensor("h1", [P, KD, T], F32) as h1:
            phase_norm1(nc, io, per, h1)
            phase_projection(nc, io, per, h1, scr)
        phase_ssd(nc, io, per, scr)
        phase_attention(nc, io, per, scr)
        phase_merge(nc, io, per, scr)
        phase_out(nc, io, per, scr)
        phase_peer(nc, io, per, scr)



def kernel(**inputs):
    import numpy as np
    import concourse.bacc as bacc
    from concourse.bass_utils import run_bass_kernel_spmd

    a = {k: np.asarray(v) for k, v in inputs.items()}

    def col(v, m):
        return v.reshape((m, P) + v.shape[1:]).swapaxes(0, 1)

    def tiles(w):
        return w.reshape(w.shape[0] // P, P, w.shape[1] // P, P).transpose(2, 1, 0, 3)

    def constants():
        i = np.arange(P)
        out = np.zeros((P, C_N), np.float32)
        out[:, C_ID:C_ID + P] = np.eye(P)
        out[:, C_ONE:C_ONE + P] = 1
        for n, size in enumerate((P, TS)):
            same = i[:, None] // size == i[None] // size
            upto = same & (i[:, None] <= i[None])
            out[:, C_TRI + n * P:C_TRI + (n + 1) * P] = upto
            out[:, C_STRI + n * P:C_STRI + (n + 1) * P] = same & (i[:, None] > i[None])
            out[:, C_NEG + n * P:C_NEG + (n + 1) * P] = np.where(upto, 0, NEG)
        q, k = i[:, None] // CHUNK, np.arange(2 * P)[None] // CHUNK
        out[:, C_AM:C_AM + 2 * P] = np.where((k >= q) & (k <= q + 2), 0, NEG)
        out[:, C_IOTA:C_IOTA + P] = i[None]
        out[:, C_BM:C_BM + NB] = i[:, None] // TS == np.arange(NB)[None]
        return out

    w_in = a["w_in"][0]
    off_xbc, off_dt = INNER, INNER + CONV
    off_q = off_dt + H
    off_k, off_v, off_g = off_q + ATTN, off_q + ATTN + KV, off_q + ATTN + 2 * KV
    cols = lambda s, n: w_in[:, s:s + n]
    sinks = a["attn_sinks"][0].reshape(NKV, QH)
    arrays = {
        "const": constants(),
        "x": col(np.concatenate([a["x_prompt"][0], a["x_sample"].reshape(-1, D)]).T, KD),
        "c": col(np.concatenate([a["c_prompt"], a["c_sample"]]).T, KD),
        "ada_w": tiles(a["ada_w"][0]), "ada_b": col(a["ada_b"][0], 6 * KD),
        "norm_g": np.stack([col(a["norm1_g"][0], KD), col(a["norm2_g"][0], KD)], 1),
        "final_g": col(a["final_g"], KD),
        "w_main": tiles(np.concatenate([cols(0, INNER), cols(off_g, 2 * D), cols(off_q, ATTN), cols(off_k, KV), cols(off_xbc, CONV)], 1)),
        "w_vdt": col(np.concatenate([cols(off_v, KV), cols(off_dt, H)], 1), KD),
        "conv_hist": col(a["state_conv"][0].transpose(2, 0, 1), MX),
        "conv_w": col(np.concatenate([a["conv_w"][0], a["conv_b"]]).T, MX),
        "ssm_in": a["state_ssm"][0].reshape(NB, G, R * HD, N).transpose(1, 3, 0, 2),
        "dt_rows": np.broadcast_to(np.stack([a["dt_bias"][0], a["a_log"][0]]), (P, 2, H)),
        "d_skip": np.repeat(a["d_skip"][0].reshape(H // 2, 2), HD, 1).T.reshape(P, G, 2),
        "ssm_g": col(a["ssm_norm_g"][0], INNER // P).reshape(P, G, 2),
        "k_cache": a["cache_attn_k"][0].transpose(2, 3, 0, 1),
        "v_cache": a["cache_attn_v"][0].transpose(2, 1, 0, 3),
        "sink_prompt": np.broadcast_to(sinks[None], (P, NKV, QH)),
        "sink_sample": np.broadcast_to(sinks.T[None, :, None], (2, QH, TS, NKV)).reshape(P, NKV),
        "w_ssm": tiles(a["w_branch_ssm"][0]), "w_attn": tiles(a["w_branch_attn"][0]), "w_out": tiles(a["w_out"][0]),
        "w_query": tiles(a["peer_wq"][0]),
        "keys": a["peer_keys"][0].reshape(2 * PH, N_KEYS, P).transpose(0, 2, 1),
        "expert_u": a["peer_u"][0].reshape(N_KEYS, N_KEYS, KD, P).transpose(1, 3, 2, 0),
        "expert_v": a["peer_v"][0].reshape(N_KEYS, N_KEYS, D).transpose(1, 0, 2),
    }
    out_shapes = {
        "y": [KD, P, T], "k_prompt": [MK, P, P], "v_prompt": [P, KV], "k_sample": [MK, P, P], "v_sample": [P, KV],
        "conv_prompt": [P, MX, TAPS - 1], "conv_sample": [P, MX, NB * (TAPS - 1)],
        "ssm_prompt": [G, N, R * HD], "ssm_sample": [G, N, NB, R * HD],
    }
    nc = bacc.Bacc("TRN2", target_bir_lowering=False, num_devices=1)
    feed, io = {}, {}
    for name, v in arrays.items():
        feed["in_" + name] = np.ascontiguousarray(v)
        io[name] = nc.dram_tensor("in_" + name, feed["in_" + name].shape, F32, kind="ExternalInput").ap()
    outs = {n: nc.dram_tensor("out_" + n, s, F32, kind="ExternalOutput").ap() for n, s in out_shapes.items()}
    build(nc, io, outs)
    r = run_bass_kernel_spmd(nc, [feed], core_ids=[0]).results[0]
    o = {n: np.asarray(r["out_" + n]) for n in out_shapes}
    y = o["y"].reshape(D, T).T
    uncol = lambda v: v.swapaxes(0, 1).reshape((-1,) + v.shape[2:])
    return (
        np.ascontiguousarray(y[:SEQ]).reshape(1, SEQ, D), np.ascontiguousarray(y[SEQ:]).reshape(NB, TS, D),
        o["k_prompt"].reshape(KV, P).T.reshape(1, 1, P, NKV, DH), o["v_prompt"].reshape(1, 1, P, NKV, DH),
        uncol(o["conv_prompt"]).T.reshape(1, 1, TAPS - 1, CONV),
        o["ssm_prompt"].transpose(0, 2, 1).reshape(1, 1, H, HD, N),
        o["k_sample"].reshape(KV, NB, TS).transpose(1, 2, 0).reshape(1, NB, TS, NKV, DH),
        o["v_sample"].reshape(1, NB, TS, NKV, DH),
        uncol(o["conv_sample"]).reshape(CONV, NB, TAPS - 1).transpose(1, 2, 0)[None],
        o["ssm_sample"].transpose(2, 0, 3, 1).reshape(1, NB, H, HD, N),
    )
```

```python
import concourse.bass as bass
from concourse import mybir
from contextlib import ExitStack

P = 128
D = 1024
KD = D // P
SEQ = 1024
NB, TS = 8, 16
T = SEQ + NB * TS
NT = T // P
NC_ = 1 + NB
EPS = 1e-6
COLS = ((0, 512), (512, 512), (1024, 128))
TB = 1536
CW = T // 3

H, HD, N = 32, 64, 128
G, R = 8, 4
INNER, CONV = H * HD, H * HD + 2 * G * N
TAPS = 4
NKV, QH, DH = 4, 4, 64
ATTN, KV = NKV * QH * DH, NKV * DH
PAST, CHUNK, N_KEYS = 128, 64, 128
PH, TOPK = 8, 16
HK = PH * TOPK
MZ, MG, MQ, MK, MX = INNER // P, 2 * D // P, ATTN // P, KV // P, CONV // P
TZ, TG, TQ = 0, MZ, MZ + MG
TK = TQ + MQ
NPLAIN = TK + MK
NEG = -1e30

F32 = mybir.dt.float32
F32R = mybir.dt.float32r
U32 = mybir.dt.uint32
ALU = mybir.AluOpType
ACT = mybir.ActivationFunctionType
AX = mybir.AxisListType
ds = bass.ds
START = 1

C_ID, C_ONE, C_TRI, C_STRI, C_NEG, C_AM, C_IOTA, C_BM = 0, 128, 256, 512, 768, 1024, 1280, 1408
C_N = C_BM + NB


class Steps:

    def __init__(self, eng, sem, per_turn=0, turn=0, before=0):
        self.eng, self.sem, self.per_turn, self.turn = eng, sem, per_turn, turn
        self.before = self.n = before

    def step(self, ins):
        ins.then_inc(self.sem, 1)
        self.n += 1

    def wait(self):
        self.eng.wait_ge(self.sem, self.turn * self.per_turn + self.n + START)

    def link(self, ins):
        self.step(ins)
        self.wait()

    def close(self):
        assert self.n - self.before == self.per_turn, (self.n - self.before, self.per_turn)


def open_(nc, ctx):
    held = []

    def clear():
        if held:
            nc.clear_and_free_semaphores(held)
            nc.all_engine_barrier()
    ctx.callback(clear)

    def sb(name, shape, dt=F32):
        return ctx.enter_context(nc.sbuf_tensor(name, shape, dt))

    def pb(name, shape):
        return ctx.enter_context(nc.psum_tensor(name, shape, F32))

    def sem(name, n=None):
        got = [nc.alloc_semaphore(name if n is None else f"{name}{i}") for i in range(n or 1)]
        held.extend(got)
        for s in got:
            nc.gpsimd.sem_inc(s, START)
        return got[0] if n is None else got
    return sb, pb, sem


def begin(nc, ctx):
    nc.all_engine_barrier()
    return ctx.enter_context(nc.Block())


def phase_modulation(nc, io, per):
    M = 6 * KD
    MB = 4
    with ExitStack() as ctx:
        sb, pb, sem = open_(nc, ctx)
        c = sb("cond", [P, KD, NC_])
        cs = sb("cond_silu", [P, KD, NC_])
        bias = sb("ada_bias", [P, M])
        g1 = sb("norm_gains", [P, 2, KD])
        w = sb("ada_ring", [P, 2, MB, KD, P])
        raw = sb("mod_raw", [P, M, NC_])
        ps = pb("mod_psum", [P, 2, 512])
        consts_in, small_in, c_silu = sem("mod_consts_in"), sem("mod_small_in"), sem("mod_c_silu")
        w_in, mm, copied = sem("mod_w_in", 2), sem("mod_mm", 2), sem("mod_copied", 2)
        added = sem("mod_added")
        block = begin(nc, ctx)

        @block.sync
        def _(sp):
            sp.dma_start(c[:], io["c"][:]).then_inc(small_in, 16)
            sp.dma_start(bias[:], io["ada_b"][:]).then_inc(small_in, 16)
            sp.dma_start(g1[:], io["norm_g"][:]).then_inc(small_in, 16)
            sp.dma_start(per["const"][:], io["const"][:]).then_inc(consts_in, 16)
            with sp.Fori(0, M // MB // 2) as i:
                for s in range(2):
                    sp.wait_ge(mm[s], i + START)
                    sp.dma_start(w[:, s], io["ada_w"][ds((i * 2 + s) * MB, MB)].rearrange("m p k c -> p m (k c)")).then_inc(w_in[s], 16)
            sp.wait_ge(consts_in, 16 + START)

        @block.scalar
        def _(act):
            act.wait_ge(small_in, 48 + START)
            nc.scalar.activation(cs[:], c[:], ACT.Silu).then_inc(c_silu, 1)

        @block.tensor
        def _(pe):
            pe.wait_ge(c_silu, 1 + START)
            with pe.Fori(0, M // MB // 2) as i:
                for s in range(2):
                    pe.wait_ge(w_in[s], i * 16 + 16 + START)
                    pe.wait_ge(copied[s], i + START)
                    for m in range(MB):
                        for k in range(KD):
                            last = nc.tensor.matmul(ps[:, s, m * NC_:(m + 1) * NC_], w[:, s, m, k], cs[:, k], start=(k == 0), stop=(k == KD - 1))
                    last.then_inc(mm[s], 1)

        @block.vector
        def _(dve):
            with dve.Fori(0, M // MB // 2) as i:
                for s in range(2):
                    dve.wait_ge(mm[s], i + 1 + START)
                    nc.vector.tensor_copy(raw[:, ds((i * 2 + s) * MB, MB)].rearrange("p m c -> p (m c)"), ps[:, s, 0:MB * NC_]).then_inc(copied[s], 1)
            for s in range(2):
                dve.wait_ge(copied[s], M // MB // 2 + START)
            dve.wait_ge(small_in, 48 + START)
            mod = per["mod"]
            nc.vector.tensor_tensor(mod[:], raw[:], bias[:].unsqueeze(2).to_broadcast([P, M, NC_]), ALU.add).then_inc(added, 1)
            dve.wait_ge(added, 1 + START)
            for n, first in ((0, KD), (1, 4 * KD)):
                sc = mod[:, first:first + KD]
                nc.vector.scalar_tensor_tensor(out=per["gain"][:, n], in0=sc, scalar=1.0,
                                               in1=g1[:, n].unsqueeze(2).to_broadcast([P, KD, NC_]), op0=ALU.add, op1=ALU.mult)


def per_token(v, k):
    return v[:, k, 1:NC_].unsqueeze(2).to_broadcast([P, NB, TS])


def samples(x):
    return x[:, SEQ:T].rearrange("p (b t) -> p b t", t=TS)


def norm_engines(nc, block, per, x, xs_ready, xs_value, sq, ps, rstd, sems, finish):
    squared, summed, rooted, chain = sems
    ones = per["const"][:, C_ONE:C_ONE + P]

    @block.scalar
    def _(act):
        act.wait_ge(xs_ready, xs_value + START)
        for k in range(KD):
            if k >= 2:
                act.wait_ge(summed, k - 1 + START)
            nc.scalar.activation(sq[:, k % 2], x[:, k], ACT.Square).then_inc(squared, 1)
        act.wait_ge(summed, KD + START)
        nc.scalar.activation(rstd[:], ps[:, 0:T], ACT.Sqrt, bias=per["eps"][:, 0:1], scale=1.0 / D).then_inc(rooted, 1)

    @block.tensor
    def _(pe):
        for k in range(KD):
            pe.wait_ge(squared, k + 1 + START)
            for a, n in COLS:
                last = nc.tensor.matmul(ps[:, a:a + n], ones, sq[:, k % 2, a:a + n], start=(k == 0), stop=(k == KD - 1))
            last.then_inc(summed, 1)

    @block.vector
    def _(dve):
        ch = Steps(dve, chain)
        dve.wait_ge(rooted, 1 + START)
        ch.link(nc.vector.reciprocal(rstd[:], rstd[:]))
        for k in range(KD):
            finish(dve, k, ch)


def modulated(nc, per, x, rstd, hi, lo, which, shift_at, tmp, out):
    def finish(dve, k, ch):
        gain, mod = per["gain"][:, which], per["mod"]
        b = k % 2
        ch.link(nc.vector.tensor_tensor(tmp[:, b], x[:, k], rstd[:], ALU.mult))
        ch.step(nc.vector.tensor_scalar(out[:, b, 0:SEQ], tmp[:, b, 0:SEQ], gain[:, k, 0:1], mod[:, shift_at + k, 0:1], ALU.mult, ALU.add))
        ch.link(nc.vector.tensor_tensor(samples(out[:, b]), samples(tmp[:, b]), per_token(gain, k), ALU.mult))
        ch.link(nc.vector.tensor_tensor(samples(out[:, b]), samples(out[:, b]), per_token(mod[:, shift_at:shift_at + KD], k), ALU.add))
        ch.link(nc.vector.tensor_copy(hi[:, k], out[:, b]))
        ch.step(nc.vector.tensor_tensor(lo[:, k], out[:, b], hi[:, k].bitcast(F32), ALU.subtract))
    return finish


def phase_norm1(nc, io, per, hi, lo):
    with ExitStack() as ctx:
        sb, pb, sem = open_(nc, ctx)
        x = sb("n1_x", [P, KD, T])
        sq, tmp, rstd, out = sb("n1_sq", [P, 2, T]), sb("n1_tmp", [P, 2, T]), sb("n1_rstd", [P, T]), sb("n1_out", [P, 2, T])
        ps = pb("n1_ps", [P, TB])
        x_in = sem("n1_x_in")
        sems = [sem(f"n1_{n}") for n in ("squared", "summed", "rooted", "chain")]
        block = begin(nc, ctx)

        @block.sync
        def _(sp):
            sp.dma_start(x[:], io["x"][:]).then_inc(x_in, 16)
        norm_engines(nc, block, per, x, x_in, 16, sq, ps, rstd, sems, modulated(nc, per, x, rstd, hi, lo, 0, 0, tmp, out))


def product(nc, ps, w, x, kt):
    for k in range(kt):
        for a, n in COLS:
            last = nc.tensor.matmul(ps[:, a:a + n], w[:, k], x[:, k, a:a + n], start=(k == 0), stop=(k == kt - 1))
    return last


def banks(ps):
    return ps[:, :, 0:CW]


def cut(x):
    return x.rearrange("p (c w) -> p c w", w=CW)


SPLIT = ((0, 0), (0, 1), (1, 0))


def product3(nc, ps, w, x, kt):
    for k in range(kt):
        for a, b in SPLIT:
            for c in range(3):
                last = nc.tensor.matmul(ps[:, c, 0:CW], w[a][:, k], x[b][:, k, c * CW:(c + 1) * CW],
                                        start=(k == 0 and (a, b) == SPLIT[0]), stop=(k == kt - 1 and (a, b) == SPLIT[-1]))
    return last


def phase_projection(nc, io, per, h, scr):
    runs = ((TZ, MZ, ACT.Silu), (TG, MG, ACT.Sigmoid), (TQ, MQ + MK, ACT.Copy))
    turns = NPLAIN // 2
    XT = MX // 2
    PADP, PADS = TAPS - 1 + SEQ, TAPS - 1 + TS
    with ExitStack() as ctx:
        sb, pb, sem = open_(nc, ctx)
        w = sb("pr_w", [P, 2, KD, P])
        w2 = [sb("pr_w_" + n, [P, 2, KD, P], F32R) for n in ("hi", "lo")]
        wvd2 = [sb("pr_wvd_" + n, [P, KD, KV + H], F32R) for n in ("hi", "lo")]
        o = sb("pr_out", [P, 2, T])
        raw = sb("pr_raw", [P, 2, PADP + NB * PADS])
        acc = sb("pr_acc", [P, 2, T])
        acc2 = sb("pr_acc2", [P, 2, T])
        hist = sb("pr_hist", [P, MX, NB * (TAPS - 1)])
        cw = sb("pr_convw", [P, MX, TAPS + 1])
        cwt = sb("pr_convw_tile", [P, 2, TAPS + 1])
        tail_p, tail_s = sb("pr_tail_p", [P, MX, TAPS - 1]), sb("pr_tail_s", [P, MX, NB * (TAPS - 1)])
        wvd = sb("pr_wvd", [P, KD, KV + H])
        vd = sb("pr_vd", [P, NT, KV + H])
        ps = pb("pr_ps", [P, 2, 3, 512])
        pv = pb("pr_pv", [P, 2, 512])
        small_in, wvd_in = sem("pr_small_in"), sem("pr_wvd_in")
        w_hi, w_lo, wvd_hi, wvd_lo = sem("pr_w_hi", 2), sem("pr_w_lo", 2), sem("pr_wvd_hi"), sem("pr_wvd_lo")
        w_in, mm = sem("pr_w_in", 2), sem("pr_mm", 2)
        evac, stored = sem("pr_evac", 2), sem("pr_stored", 2)
        vmm, vcopied, vstored = sem("pr_vmm"), sem("pr_vcopied"), sem("pr_vstored")
        conv_ready, silu_done, tail_done = sem("pr_conv", 2), sem("pr_silu", 2), sem("pr_tails", 2)
        kept = sem("pr_kept")
        chains = sem("pr_chain")
        block = begin(nc, ctx)

        @block.sync
        def _(sp):
            sp.dma_start(wvd[:], io["w_vdt"][:]).then_inc(wvd_in, 16)
            sp.dma_start(hist[:], io["conv_hist"][:]).then_inc(small_in, 16)
            sp.dma_start(cw[:], io["conv_w"][:]).then_inc(small_in, 16)
            with sp.Fori(0, turns + XT) as i:
                for s in range(2):
                    sp.wait_ge(w_lo[s], i + START)
                    sp.dma_start(w[:, s], io["w_main"][ds(i * 2 + s, 1)].rearrange("m p k c -> p (m k) c")).then_inc(w_in[s], 16)
            sp.wait_ge(vcopied, NT + START)
            sp.dma_start(scr["vd"][:], vd[:]).then_inc(vstored, 16)
            sp.dma_start(io["v_prompt"][:], vd[:, NT - 2, 0:KV]).then_inc(vstored, 16)
            sp.dma_start(io["v_sample"][:], vd[:, NT - 1, 0:KV]).then_inc(vstored, 16)
            for s in range(2):
                sp.wait_ge(tail_done[s], XT + START)
            sp.dma_start(io["conv_prompt"][:], tail_p[:]).then_inc(kept, 16)
            sp.dma_start(io["conv_sample"][:], tail_s[:]).then_inc(kept, 16)
            sp.wait_ge(vstored, 48 + START)
            sp.wait_ge(kept, 32 + START)

        @block.tensor
        def _(pe):
            pe.wait_ge(wvd_lo, 1 + START)
            for t in range(NT):
                if t >= 2:
                    pe.wait_ge(vcopied, t - 1 + START)
                for k in range(KD):
                    for a, b in SPLIT:
                        last = nc.tensor.matmul(pv[:, t % 2, 0:KV + H], h[a][:, k, t * P:(t + 1) * P], wvd2[b][:, k],
                                                start=(k == 0 and (a, b) == SPLIT[0]), stop=(k == KD - 1 and (a, b) == SPLIT[-1]))
                last.then_inc(vmm, 1)
            with pe.Fori(0, turns + XT) as i:
                for s in range(2):
                    pe.wait_ge(w_lo[s], i + 1 + START)
                    pe.wait_ge(evac[s], i + START)
                    product3(nc, ps[:, s], [x[:, s] for x in w2], h, KD).then_inc(mm[s], 1)

        def round_weights(act, i, s):
            act.wait_ge(w_in[s], i * 16 + 16 + START)
            act.wait_ge(mm[s], i + START)
            nc.scalar.copy(w2[0][:, s], w[:, s]).then_inc(w_hi[s], 1)

        def rest_of_weights(dve, i, s):
            dve.wait_ge(w_hi[s], i + 1 + START)
            nc.vector.tensor_tensor(w2[1][:, s], w[:, s], w2[0][:, s].bitcast(F32), ALU.subtract).then_inc(w_lo[s], 1)

        @block.scalar
        def _(act):
            act.wait_ge(wvd_in, 16 + START)
            nc.scalar.copy(wvd2[0][:], wvd[:]).then_inc(wvd_hi, 1)
            for s in range(2):
                round_weights(act, 0, s)
            for first, count, func in runs:
                f = first // 2
                with act.Fori(f, f + count // 2) as i:
                    for s in range(2):
                        act.wait_ge(mm[s], i + 1 + START)
                        act.wait_ge(stored[s], i * 16 + START)
                        nc.scalar.activation(cut(o[:, s]), banks(ps[:, s]), func).then_inc(evac[s], 1)
                        round_weights(act, i + 1, s)
                        act.wait_ge(evac[s], i + 1 + START)
                        act.dma_start(scr["plain"][ds(i * 2 + s, 1)].rearrange("m p t -> p (m t)"), o[:, s]).then_inc(stored[s], 16)
            def conv_tile(i, s, more):
                    act.wait_ge(mm[s], i + turns + 1 + START)
                    act.wait_ge(tail_done[s], i + START)
                    nc.scalar.copy(cut(raw[:, s, TAPS - 1:TAPS - 1 + 2 * CW]), ps[:, s, 0:2, 0:CW])
                    nc.scalar.copy(raw[:, s, TAPS - 1 + 2 * CW:PADP], ps[:, s, 2, 0:SEQ - 2 * CW])
                    nc.scalar.copy(raw[:, s, PADP:].rearrange("p (b t) -> p b t", t=PADS)[:, :, TAPS - 1:],
                                   ps[:, s, 2, SEQ - 2 * CW:CW].rearrange("p (b t) -> p b t", t=TS)).then_inc(evac[s], 1)
                    if more:
                        round_weights(act, i + (turns + 1), s)
                    act.wait_ge(conv_ready[s], i + 1 + START)
                    act.wait_ge(stored[s], (i + turns) * 16 + START)
                    nc.scalar.activation(o[:, s], acc2[:, s], ACT.Silu).then_inc(silu_done[s], 1)
                    act.wait_ge(silu_done[s], i + 1 + START)
                    act.dma_start(scr["xbc"][ds(i * 2 + s, 1)].rearrange("m p t -> p (m t)"), o[:, s]).then_inc(stored[s], 16)

            with act.Fori(0, XT - 1) as i:
                for s in range(2):
                    conv_tile(i, s, True)
            for s in range(2):
                conv_tile(XT - 1, s, False)
            for s in range(2):
                act.wait_ge(stored[s], (turns + XT) * 16 + START)

        @block.vector
        def _(dve):
            dve.wait_ge(wvd_hi, 1 + START)
            nc.vector.tensor_tensor(wvd2[1][:], wvd[:], wvd2[0][:].bitcast(F32), ALU.subtract).then_inc(wvd_lo, 1)
            for s in range(2):
                rest_of_weights(dve, 0, s)
            for t in range(NT):
                dve.wait_ge(vmm, t + 1 + START)
                nc.vector.tensor_copy(vd[:, t], pv[:, t % 2, 0:KV + H]).then_inc(vcopied, 1)
            Steps(dve, chains).step(nc.vector.memset(raw[:, :, 0:TAPS - 1], 0.0))
            dve.wait_ge(small_in, 32 + START)
            with dve.Fori(1, turns + 1) as i:
                for s in range(2):
                    rest_of_weights(dve, i, s)

            def convolve(i, more):
                ch = Steps(dve, chains, 12, i, before=1)
                for s in range(2):
                    if more:
                        rest_of_weights(dve, i + (turns + 1), s)
                    rp, rs = raw[:, s, 0:PADP], raw[:, s, PADP:].rearrange("p (b t) -> p b t", t=PADS)
                    dve.wait_ge(evac[s], i + turns + 1 + START)
                    m = i * 2 + s
                    ch.step(nc.vector.tensor_copy(rs[:, :, 0:TAPS - 1], hist[:, ds(m, 1)].rearrange("p m (b t) -> p (m b) t", t=TAPS - 1)))
                    ch.link(nc.vector.tensor_copy(cwt[:, s], cw[:, ds(m, 1)].rearrange("p m j -> p (m j)")))
                    dve.wait_ge(silu_done[s], i + START)
                    views = ((rp, lambda j: rp[:, j:j + SEQ], lambda a: a[:, s, 0:SEQ]),
                             (rs, lambda j: rs[:, :, j:j + TS], lambda a: samples(a[:, s])))
                    bufs = (acc, acc2, acc, acc2)
                    for j in range(TAPS):
                        for _, src, dst in views:
                            if j == 0:
                                ins = nc.vector.tensor_scalar(dst(bufs[0]), src(0), cwt[:, s, 0:1], cwt[:, s, TAPS:TAPS + 1], ALU.mult, ALU.add)
                            else:
                                ins = nc.vector.scalar_tensor_tensor(out=dst(bufs[j]), in0=src(j), scalar=cwt[:, s, j:j + 1], in1=dst(bufs[j - 1]), op0=ALU.mult, op1=ALU.add)
                        if j < TAPS - 1:
                            ch.link(ins)
                        else:
                            ins.then_inc(conv_ready[s], 1)
                    ch.step(nc.vector.tensor_copy(tail_p[:, ds(m, 1)].rearrange("p m t -> p (m t)"), rp[:, SEQ:PADP]))
                    nc.vector.tensor_copy(tail_s[:, ds(m, 1)].rearrange("p m (b t) -> p (m b) t", t=TAPS - 1), rs[:, :, TS:PADS]).then_inc(tail_done[s], 1)
                    ch.wait()
                ch.close()

            with dve.Fori(0, XT - 1) as i:
                convolve(i, True)
            convolve(XT - 1, False)


def phase_decay(nc, io, per, scr, vec):
    NP8 = NT - 1
    with ExitStack() as ctx:
        sb, pb, sem = open_(nc, ctx)
        raw, rows = sb("dc_raw", [P, NT, H]), sb("dc_rows", [P, 2, H])
        t1, t2 = sb("dc_t1", [P, NT, H]), sb("dc_t2", [P, NT, H])
        rate = sb("dc_rate", [P, H])
        dt, na, a, toend = (sb("dc_" + n, [P, NT, H]) for n in ("dt", "na", "a", "toend"))
        ps = pb("dc_ps", [P, 2, 512])
        loaded, chain, exped, logged, summed, ended = (sem("dc_" + n) for n in ("in", "chain", "exp", "log", "sum", "end"))
        block = begin(nc, ctx)
        tri = [per["const"][:, C_TRI + n * P:C_TRI + (n + 1) * P] for n in range(2)]
        stri = [per["const"][:, C_STRI + n * P:C_STRI + (n + 1) * P] for n in range(2)]

        @block.sync
        def _(sp):
            sp.dma_start(raw[:], scr["vd"][:, :, KV:KV + H]).then_inc(loaded, 16)
            sp.dma_start(rows[:], io["dt_rows"][:]).then_inc(loaded, 16)

        @block.vector
        def _(dve):
            v, ch = nc.vector, Steps(dve, chain)
            dve.wait_ge(loaded, 32 + START)
            ch.link(v.tensor_tensor(raw[:], raw[:], rows[:, 0].unsqueeze(1).to_broadcast([P, NT, H]), ALU.add))
            ch.link(v.tensor_scalar(t1[:], raw[:], -1.0, None, ALU.mult))
            ch.link(v.tensor_tensor(t1[:], t1[:], raw[:], ALU.min))
            dve.wait_ge(logged, 1 + START)
            ch.link(v.scalar_tensor_tensor(out=dt[:], in0=raw[:], scalar=0.0, in1=t2[:], op0=ALU.max, op1=ALU.add))
            ch.link(v.tensor_tensor(na[:], dt[:], rate[:].unsqueeze(1).to_broadcast([P, NT, H]), ALU.mult))
            ch.link(v.tensor_scalar(a[:], na[:], -1.0, None, ALU.mult))
            dve.wait_ge(ended, 1 + START)
            ch.link(v.tensor_tensor(toend[:], toend[:], dt[:], ALU.mult))
            dve.wait_ge(summed, 1 + START)
            by_group = lambda x: x[:].rearrange("p t (g r) -> p t g r", g=G)
            for n, x in ((0, a), (2, dt), (3, toend)):
                ch.link(v.tensor_copy(vec[:, :, n].rearrange("p g t r -> p t g r"), by_group(x)))
            ch.link(v.tensor_copy(vec[:, :, 1].rearrange("p g t r -> p t g r"), ps[:, 0, 0:NT * H].rearrange("p (t g r) -> p t g r", g=G, t=NT)))

        @block.scalar
        def _(act):
            act.wait_ge(loaded, 32 + START)
            nc.scalar.activation(rate[:], rows[:, 1], ACT.Exp).then_inc(exped, 1)
            act.wait_ge(chain, 3 + START)
            nc.scalar.activation(t2[:], t1[:], ACT.Exp).then_inc(exped, 1)
            act.wait_ge(exped, 2 + START)
            nc.scalar.activation(t2[:], t2[:], ACT.Ln, bias=1.0).then_inc(logged, 1)
            act.wait_ge(summed, 1 + START)
            nc.scalar.activation(toend[:], ps[:, 1, 0:NT * H].rearrange("p (t h) -> p t h", t=NT), ACT.Exp).then_inc(ended, 1)

        @block.tensor
        def _(pe):
            pe.wait_ge(chain, 6 + START)
            for b, (m, x) in enumerate(((tri, na), (stri, a))):
                nc.tensor.matmul(ps[:, b, 0:NP8 * H], m[0], x[:, 0:NP8].rearrange("p t h -> p (t h)"), start=True, stop=True)
                last = nc.tensor.matmul(ps[:, b, NP8 * H:NT * H], m[1], x[:, NP8], start=True, stop=True)
            last.then_inc(summed, 1)


def phase_ssd(nc, io, per, scr):
    with ExitStack() as ctx0:
        vec = ctx0.enter_context(nc.sbuf_tensor("decay_vec", [P, G, 4, NT, R], F32))
        phase_decay(nc, io, per, scr, vec)
        ssd_groups(nc, io, per, scr, vec)


def ssd_groups(nc, io, per, scr, vec):
    LAST = NT - 1
    CH = 18
    W = R * HD
    with ExitStack() as ctx:
        sb, pb, sem = open_(nc, ctx)
        xT, bT, cT, zT = sb("sd_xT", [P, 2, 2, T]), sb("sd_bT", [P, 2, T]), sb("sd_cT", [P, 2, T]), sb("sd_zT", [P, 2, 2, T])
        h0 = sb("sd_h0", [P, NB, W])
        hp = sb("sd_h", [P, W])
        vg = sb("sd_vec", [P, 2, 4, NT, R])
        skip, gain = sb("sd_skip", [P, G, 2]), sb("sd_gain", [P, G, 2])
        sg = sb("sd_skip_gain", [P, 2, 2, 2])
        y, sq, rs = sb("sd_y", [P, 2, 2, T]), sb("sd_sq", [P, 2, T]), sb("sd_rs", [P, T])
        xdt, xe, bk = sb("sd_xdt", [P, 2, W]), sb("sd_xe", [P, 2, W]), sb("sd_bk", [P, 2, N])
        seg, dec, ea, mt, cts = (sb("sd_" + n, [P, 2, R, P]) for n in ("seg", "dec", "ea", "mt", "cts"))
        xeb = sb("sd_xeb", [P, 2, W])
        psT = pb("sd_psT", [P, 2, 512])
        psA = pb("sd_psA", [P, 2, 512])
        psY = pb("sd_psY", [P, 2, 512])
        psR = pb("sd_psR", [P, 2, 512])
        x_in, h_in = sem("sd_in", 2), sem("sd_h_in")
        small = sem("sd_small")
        vg_ready = sem("sd_vg", 2)
        tr, cum = sem("sd_tr", 2), sem("sd_cum", 2)
        xdt_r, bk_r, seg_r, ea_r, dec_r, mt_r, cts_r = (sem("sd_" + n, 2) for n in ("xdtr", "bkr", "segr", "ear", "decr", "mtr", "ctsr"))
        y_r, s_r, y_read, h_done = (sem("sd_" + n, 2) for n in ("yr", "sr", "yread", "hdone"))
        xeb_r, sb_r, sb_done = (sem("sd_" + n, 2) for n in ("xebr", "sbr", "sbdone"))
        sq_r, var_r, root_r = (sem("sd_" + n) for n in ("sqr", "varr", "rootr"))
        y_out, y_st, hs_st, hp_st = sem("sd_yout", 2), sem("sd_yst", 2), sem("sd_hsst"), sem("sd_hpst")
        yg_r = sem("sd_yg")
        chain = sem("sd_chain")
        block = begin(nc, ctx)
        ident, ones = per["const"][:, C_ID:C_ID + P], per["const"][:, C_ONE:C_ONE + P]
        tri = [per["const"][:, C_TRI + n * P:C_TRI + (n + 1) * P] for n in range(2)]
        neg = [per["const"][:, C_NEG + n * P:C_NEG + (n + 1) * P] for n in range(2)]

        def chunk(s, c):
            k = s * NT + c
            return k % 2, k // 2, int(c == LAST), slice(c * P, (c + 1) * P)

        def previous(i, s, c):
            k = s * NT + c - 1
            return k % 2, i * (CH // 2) + k // 2 + 1

        SEMS_OF = (NB // 2, NB // 2 - 1)

        def sample_states_done(eng, i, s):
            q, u, _, _ = chunk(s, LAST)
            for e in range(2):
                eng.wait_ge(sb_done[e], (i * 2 + s + 1) * SEMS_OF[e] + START)
            eng.wait_ge(h_done[q], i * (CH // 2) + u + 1 + START)

        @block.sync
        def _(sp):
            sp.dma_start(skip[:], io["d_skip"][:]).then_inc(small, 16)
            sp.dma_start(gain[:], io["ssm_g"][:]).then_inc(small, 16)
            with sp.Fori(0, G // 2) as i:
                for s in range(2):
                    g = i * 2 + s
                    sp.wait_ge(y_out[s], i + START)
                    tile_of = lambda src, m: src[ds(m, 1)].rearrange("m p t -> p (m t)")
                    for j in range(2):
                        sp.dma_start(xT[:, s, j], tile_of(scr["xbc"], g * 2 + j)).then_inc(x_in[s], 16)
                        sp.dma_start(zT[:, s, j], tile_of(scr["plain"], g * 2 + (TZ + j))).then_inc(x_in[s], 16)
                    sp.dma_start(bT[:, s], tile_of(scr["xbc"], g + INNER // P)).then_inc(x_in[s], 16)
                    sp.dma_start(cT[:, s], tile_of(scr["xbc"], g + (INNER // P + G))).then_inc(x_in[s], 16)
                    sp.wait_ge(hs_st, g * 16 + START)
                    sp.dma_start(h0[:], io["ssm_in"][ds(g, 1)].rearrange("g n b w -> n (g b) w")).then_inc(h_in, 16)

        @block.tensor
        def _(pe):
            mm = nc.tensor.matmul

            def prepare(i, s, c):
                q, u, ms, at = chunk(s, c)
                u = i * (CH // 2) + u
                if c == 0:
                    pe.wait_ge(x_in[s], i * 96 + 96 + START)
                    pe.wait_ge(vg_ready[s], i + 1 + START)
                pe.wait_ge(xdt_r[q], u + START)
                pe.wait_ge(bk_r[q], u + START)
                pe.wait_ge(mt_r[q], u + START)
                for j in range(2):
                    nc.tensor.transpose(psT[:, q, j * P:(j + 1) * P], xT[:, s, j, at], ident)
                nc.tensor.transpose(psT[:, q, 2 * P:3 * P], bT[:, s, at], ident)
                mm(psT[:, q, 3 * P:4 * P], bT[:, s, at], cT[:, s, at], start=True, stop=True).then_inc(tr[q], 1)
                pe.wait_ge(seg_r[q], u + START)
                pe.wait_ge(ea_r[q], u + START)
                for r in range(R):
                    last = mm(psA[:, q, r * P:(r + 1) * P], vg[:, s, 0, c, r:r + 1].to_broadcast([P, P]), tri[ms], start=True, stop=True)
                last.then_inc(cum[q], 1)

            def scan(i, s, c):
                q, u, ms, at = chunk(s, c)
                u = i * (CH // 2) + u
                pe.wait_ge(mt_r[q], u + 1 + START)
                pe.wait_ge(xdt_r[q], u + 1 + START)
                pe.wait_ge(cts_r[q], u + 1 + START)
                pe.wait_ge(y_read[q], u + START)
                pe.wait_ge(h_done[q], u + START)
                if c == LAST:
                    pe.wait_ge(h_in, i * 32 + (s + 1) * 16 + START)
                elif c > 0:
                    pq, n = previous(i, s, c)
                    pe.wait_ge(h_done[pq], n + START)
                for r in range(R):
                    o = psY[HD * (r % 2):HD * (r % 2) + HD, q, (r // 2) * P:(r // 2 + 1) * P]
                    if c == LAST:
                        for b in range(NB):
                            t = slice(b * TS, (b + 1) * TS)
                            mm(o[:, t], h0[:, b, r * HD:(r + 1) * HD], cts[:, q, r, t], start=(b == 0), stop=False, skip_group_check=True)
                    elif c > 0:
                        mm(o, hp[:, r * HD:(r + 1) * HD], cts[:, q, r], start=True, stop=False)
                    last = mm(o, xdt[:, q, r * HD:(r + 1) * HD], mt[:, q, r], start=(c == 0), stop=True, skip_group_check=(c == LAST))
                last.then_inc(y_r[q], 1)
                pe.wait_ge(bk_r[q], u + 1 + START)
                if c < LAST:
                    mm(psY[:, q, 256:512], bk[:, q], xe[:, q], start=True, stop=True).then_inc(s_r[q], 1)
                    return
                for b in range(NB):
                    e, n = b % 2, b // 2
                    pe.wait_ge(xeb_r[e], i * NB + s * (NB // 2) + n + 1 + START)
                    if n == 0:
                        pe.wait_ge(root_r, i * 6 + s * 3 + START)
                    pe.wait_ge(sb_done[e], (i * 2 + s) * SEMS_OF[e] + n + START)
                    last = mm(psR[:, e, 0:W], bk[:, q], xeb[:, e], start=True, stop=True)
                    last.then_inc(s_r[q] if b == NB - 1 else sb_r[e], 1)

            with pe.Fori(0, G // 2) as i:
                for s in range(2):
                    prepare(i, s, 0)
                    for c in range(NT):
                        if c < LAST:
                            prepare(i, s, c + 1)
                        scan(i, s, c)
                    pe.wait_ge(sq_r, i * 2 + s + 1 + START)
                    sample_states_done(pe, i, s)
                    for n, (a, w) in enumerate(COLS):
                        if n == 2:
                            pe.wait_ge(root_r, i * 6 + s * 3 + 1 + START)
                        for j in range(2):
                            last = mm(psR[:, n % 2, 0:w], ones, sq[:, j, a:a + w], start=(j == 0), stop=(j == 1))
                        last.then_inc(var_r, 1)

        @block.scalar
        def _(act):
            with act.Fori(0, G // 2) as i:
                for s in range(2):
                    for c in range(NT):
                        q, u, ms, at = chunk(s, c)
                        u = i * (CH // 2) + u
                        act.wait_ge(tr[q], u + 1 + START)
                        act.wait_ge(s_r[q], u + START)
                        act.wait_ge(xdt_r[q], u + 1 + START)
                        nc.scalar.copy(bk[:, q], psT[:, q, 2 * P:3 * P]).then_inc(bk_r[q], 1)
                        act.wait_ge(cum[q], u + 1 + START)
                        act.wait_ge(cts_r[q], u + START)
                        act.wait_ge(h_done[q], u + START)
                        act.wait_ge(seg_r[q], u + 1 + START)
                        nc.scalar.activation(ea[:, q].rearrange("p r l -> p (r l)"), psA[:, q], ACT.Exp).then_inc(ea_r[q], 1)
                        act.wait_ge(mt_r[q], u + START)
                        for r in range(R):
                            last = nc.scalar.activation(dec[:, q, r], seg[:, q, r], ACT.Exp, bias=vg[:, s, 1, c, r:r + 1])
                        last.then_inc(dec_r[q], 1)
                    act.wait_ge(yg_r, i * 2 + s + 1 + START)
                    act.wait_ge(var_r, i * 6 + s * 3 + START)
                    nc.scalar.activation(sq[:], y[:, s], ACT.Square).then_inc(sq_r, 1)
                    act.wait_ge(y_out[1 - s], i + s + START)
                    for n, (a, w) in enumerate(COLS):
                        act.wait_ge(var_r, i * 6 + s * 3 + n + 1 + START)
                        nc.scalar.activation(rs[:, a:a + w], psR[:, n % 2, 0:w], ACT.Sqrt, bias=per["eps"][:, 0:1], scale=1.0 / W).then_inc(root_r, 1)
                    act.wait_ge(y_out[s], i + 1 + START)
                    act.dma_start(scr["ynorm"][ds((i * 2 + s) * 2, 2)].rearrange("m p t -> p m t"), y[:, s]).then_inc(y_st[s], 16)
                    sample_states_done(act, i, s)
                    act.dma_start(io["ssm_sample"][ds(i * 2 + s, 1)].rearrange("g n b w -> n (g b) w"), h0[:]).then_inc(hs_st, 16)
                    act.dma_start(io["ssm_prompt"][ds(i * 2 + s, 1)].rearrange("g n w -> n (g w)"), hp[:]).then_inc(hp_st, 16)
            for s in range(2):
                act.wait_ge(y_st[s], G // 2 * 16 + START)
            act.wait_ge(hs_st, G * 16 + START)
            act.wait_ge(hp_st, G * 16 + START)

        @block.gpsimd
        def _(pool):
            with pool.Fori(0, G // 2) as i:
                for s in range(2):
                    for c in range(NT):
                        q, u, ms, at = chunk(s, c)
                        u = i * (CH // 2) + u
                        pool.wait_ge(ea_r[q], u + 1 + START)
                        pool.wait_ge(y_r[q], u + START)
                        if c == 0:
                            pool.wait_ge(x_in[s], i * 96 + 96 + START)
                        nc.gpsimd.tensor_tensor(cts[:, q], cT[:, s, at].unsqueeze(1).to_broadcast([P, R, P]), ea[:, q], ALU.mult).then_inc(cts_r[q], 1)

        @block.vector
        def _(dve):
            v = nc.vector
            PER = 2 * (2 + (LAST - 1) + NB + 1)
            dve.wait_ge(small, 32 + START)
            with dve.Fori(0, G // 2) as i:
                ch = Steps(dve, chain, PER, i)
                for s in range(2):
                    g = i * 2 + s
                    v.tensor_copy(vg[:, s].rearrange("p k t r -> p (k t r)"), vec[:, ds(g, 1)].rearrange("p g k t r -> p (g k t r)")).then_inc(vg_ready[s], 1)
                    ch.link(v.tensor_copy(sg[:, s, 0], skip[:, ds(g, 1)].rearrange("p g j -> p (g j)")))
                    ch.link(v.tensor_copy(sg[:, s, 1], gain[:, ds(g, 1)].rearrange("p g j -> p (g j)")))
                    dve.wait_ge(vg_ready[s], i + 1 + START)
                    dve.wait_ge(x_in[s], i * 96 + 96 + START)
                    dve.wait_ge(y_st[s], i * 16 + START)

                    def before(c):
                        q, u, ms, at = chunk(s, c)
                        u = i * (CH // 2) + u
                        scaled = lambda out, kind: v.tensor_tensor(
                            out[:, q].rearrange("p (r d) -> p r d", d=HD), psT[:, q, 0:W].rearrange("p (r d) -> p r d", d=HD),
                            vg[:, s, kind, c].unsqueeze(2).to_broadcast([P, R, HD]), ALU.mult)
                        dve.wait_ge(cum[q], u + 1 + START)
                        v.tensor_tensor(seg[:, q], psA[:, q].rearrange("p (r l) -> p r l", r=R),
                                        neg[ms].unsqueeze(1).to_broadcast([P, R, P]), ALU.add).then_inc(seg_r[q], 1)
                        dve.wait_ge(tr[q], u + 1 + START)
                        dve.wait_ge(s_r[q], u + START)
                        scaled(xdt, 2)
                        scaled(xe, 3).then_inc(xdt_r[q], 1)

                    def masked(c):
                        q, u, ms, at = chunk(s, c)
                        u = i * (CH // 2) + u
                        dve.wait_ge(dec_r[q], u + 1 + START)
                        dve.wait_ge(bk_r[q], u + 1 + START)
                        dve.wait_ge(y_r[q], u + START)
                        v.tensor_tensor(mt[:, q], dec[:, q], psT[:, q, 3 * P:4 * P].unsqueeze(1).to_broadcast([P, R, P]), ALU.mult).then_inc(mt_r[q], 1)

                    def after(c):
                        q, u, ms, at = chunk(s, c)
                        u = i * (CH // 2) + u
                        dve.wait_ge(y_r[q], u + 1 + START)
                        if c < LAST:
                            dve.wait_ge(s_r[q], u + 1 + START)
                        for j in range(2):
                            ins = v.scalar_tensor_tensor(out=y[:, s, j, at], in0=xT[:, s, j, at], scalar=sg[:, s, 0, j:j + 1],
                                                         in1=psY[:, q, j * P:(j + 1) * P], op0=ALU.mult, op1=ALU.add)
                        ins.then_inc(y_read[q], 1)
                        if c == 0:
                            dve.wait_ge(hp_st, g * 16 + START)
                            v.tensor_copy(hp[:], psY[:, q, 256:512]).then_inc(h_done[q], 1)
                        elif c < LAST:
                            hv = hp[:].rearrange("p (r d) -> p r d", d=HD)
                            pq, n = previous(i, s, c)
                            dve.wait_ge(h_done[pq], n + START)
                            ch.link(v.tensor_tensor(hv, hv, ea[:, q, :, P - 1:P].to_broadcast([P, R, HD]), ALU.mult))
                            v.tensor_tensor(hp[:], hp[:], psY[:, q, 256:512], ALU.add).then_inc(h_done[q], 1)
                        else:
                            dve.wait_ge(xdt_r[q], u + 1 + START)
                            dve.wait_ge(h_in, g * 16 + 16 + START)

                            def rows_of(b):
                                e, n = b % 2, b // 2
                                dve.wait_ge(sb_r[e], g * SEMS_OF[e] + n + START)
                                v.tensor_scalar(xeb[:, e], xe[:, q], per["const"][:, C_BM + b:C_BM + b + 1], None, ALU.mult).then_inc(xeb_r[e], 1)

                            def update(b):
                                e, n = b % 2, b // 2
                                hv = h0[:, b].rearrange("p (r d) -> p r d", d=HD)
                                ch.link(v.tensor_tensor(hv, hv, ea[:, q, :, b * TS + TS - 1:(b + 1) * TS].to_broadcast([P, R, HD]), ALU.mult))
                                if b < NB - 1:
                                    dve.wait_ge(sb_r[e], g * SEMS_OF[e] + n + 1 + START)
                                else:
                                    dve.wait_ge(s_r[q], u + 1 + START)
                                v.tensor_tensor(h0[:, b], h0[:, b], psR[:, e, 0:W], ALU.add).then_inc(h_done[q] if b == NB - 1 else sb_done[e], 1)

                            rows_of(0)
                            for b in range(NB):
                                if b < NB - 1:
                                    rows_of(b + 1)
                                update(b)

                    before(0)
                    masked(0)
                    for c in range(NT):
                        if c < LAST:
                            before(c + 1)
                        after(c)
                        if c < LAST:
                            masked(c + 1)
                    q, u, _, _ = chunk(s, LAST)
                    dve.wait_ge(y_read[q], i * (CH // 2) + u + 1 + START)
                    v.tensor_tensor(y[:, s], y[:, s], zT[:, s], ALU.mult).then_inc(yg_r, 1)
                    dve.wait_ge(root_r, g * 3 + 3 + START)
                    ch.link(v.reciprocal(rs[:], rs[:]))
                    dve.wait_ge(yg_r, g + 1 + START)
                    for j in range(2):
                        ins = v.scalar_tensor_tensor(out=y[:, s, j], in0=y[:, s, j], scalar=sg[:, s, 1, j:j + 1], in1=rs[:], op0=ALU.mult, op1=ALU.mult)
                    ins.then_inc(y_out[s], 1)
                ch.close()


def phase_attention(nc, io, per, scr):
    SCALE = DH ** -0.5
    LAST = NT - 1
    K2 = 2 * P
    with ExitStack() as ctx:
        sb, pb, sem = open_(nc, ctx)
        qT, kT = sb("at_qT", [DH, 2, QH, T]), sb("at_kT", [DH, 2, T])
        v, vn = sb("at_v", [P, 2, NT, DH]), sb("at_vnew", [TS, 2, NB, DH])
        kc, vc = sb("at_kc", [DH, 2, NB, P]), sb("at_vc", [P, 2, NB, DH])
        sink_p, sink_s = sb("at_sink_p", [P, NKV, QH]), sb("at_sink_s", [P, NKV])
        sink = sb("at_sink", [P, 2, 2, QH])
        s_ = sb("at_s", [P, 2, QH, K2])
        pr = sb("at_p", [P, 2, QH, K2])
        pT = sb("at_pT", [P, 2, 2, QH * P])
        qs = sb("at_qs", [DH, 2, NB, QH * TS])
        mx, nm, es, den = (sb("at_" + n, [P, 2, QH]) for n in ("mx", "nm", "es", "den"))
        o = sb("at_o", [DH, 2, QH, T])
        psS = pb("at_psS", [P, 2, QH, K2])
        psT = pb("at_psT", [P, 2, QH * P])
        psO = pb("at_psO", [P, 2, QH * P])
        small, loaded, qs_r = sem("at_small"), sem("at_in", 2), sem("at_qsr", 2)
        s_r, m_r, nm_r, es_r, p_r, pn_r, pt_r, ptc_r, o_r, oc_r = (
            sem("at_" + n, 2) for n in ("sr", "mr", "nmr", "esr", "pr", "pnr", "ptr", "ptcr", "or", "ocr"))
        chain, o_st, copied = sem("at_chain"), sem("at_ost", 2), sem("at_kout")
        block = begin(nc, ctx)
        ident = per["const"][:, C_ID:C_ID + P]
        amask = per["const"][:, C_AM:C_AM + K2]
        heads = lambda x, a, n: x[ds(a, n)].rearrange("m (h d) t -> d (m h) t", d=DH)

        def tile_(s, c):
            k = s * NT + c
            return k % 2, k // 2

        def halves(c):
            return ((1, P),) if c == 0 else ((0, P), (1, P if c < LAST else TS))

        @block.sync
        def _(sp):
            sp.dma_start(sink_p[:], io["sink_prompt"][:]).then_inc(small, 16)
            sp.dma_start(sink_s[:], io["sink_sample"][:]).then_inc(small, 16)
            for n, t in (("k_prompt", NT - 2), ("k_sample", LAST)):
                sp.dma_start(io[n][:], scr["plain"][TK:TK + MK, :, t * P:(t + 1) * P]).then_inc(copied, 16)
            with sp.Fori(0, NKV // 2) as i:
                for s in range(2):
                    g = i * 2 + s
                    sp.wait_ge(o_st[s], i * 16 + START)
                    sp.dma_start(qT[:, s], heads(scr["plain"], TQ + g * 2, 2)).then_inc(loaded[s], 16)
                    sp.dma_start(kT[:, s], scr["plain"][ds(TK + i, 1)][:, s * DH:(s + 1) * DH].rearrange("m d t -> d (m t)")).then_inc(loaded[s], 16)
                    sp.dma_start(v[:, s], scr["vd"][:, :, ds(g * DH, DH)]).then_inc(loaded[s], 16)
                    sp.dma_start(vn[:, s], scr["vd"][:, LAST, ds(g * DH, DH)].rearrange("(b t) d -> t b d", t=TS)).then_inc(loaded[s], 16)
                    sp.dma_start(kc[:, s], io["k_cache"][ds(g, 1)].rearrange("g d b k -> d (g b) k")).then_inc(loaded[s], 16)
                    sp.dma_start(vc[:, s], io["v_cache"][ds(g, 1)].rearrange("g k b d -> k (g b) d")).then_inc(loaded[s], 16)
            sp.wait_ge(copied, 32 + START)

        @block.tensor
        def _(pe):
            mm = nc.tensor.matmul

            def scores(i, s, c):
                q, u = tile_(s, c)
                u = i * NT + u
                if c == 0:
                    pe.wait_ge(loaded[s], i * 96 + 96 + START)
                pe.wait_ge(m_r[q], u + START)
                if c < LAST:
                    lo = P if c == 0 else 0
                    for r in range(QH):
                        last = mm(psS[:, q, r, lo:K2], qT[:, s, r, c * P:(c + 1) * P], kT[:, s, (c - 1) * P + lo:(c + 1) * P], start=True, stop=True)
                else:
                    pe.wait_ge(qs_r[s], i + 1 + START)
                    for b in range(NB):
                        at = slice(SEQ + b * TS, SEQ + (b + 1) * TS)
                        rows, n = (slice(0, P), 2) if b % 2 == 0 else (slice(64, P), 1)
                        own = qs[:, s, b:b + n].rearrange("d b m -> d (b m)")
                        mm(psS[rows, q, b // 2, 0:P], own, kc[:, s, b], start=True, stop=True)
                        last = mm(psS[rows, q, b // 2, P:P + TS], own, kT[:, s, at], start=True, stop=True)
                last.then_inc(s_r[q], 1)

            def turned(i, s, c):
                q, u = tile_(s, c)
                u = i * NT + u
                pe.wait_ge(pn_r[q], u + 1 + START)
                k = s * NT + c
                pe.wait_ge(ptc_r[(k - 1) % 2], i * NT + (k + 1) // 2 + START)
                for h, n in halves(c):
                    for r in range(QH):
                        last = nc.tensor.transpose(psT[0:n, h, r * P:(r + 1) * P], pr[:, q, r, h * P:h * P + n], ident)
                last.then_inc(pt_r[q], 1)

            def values(i, s, c):
                q, u = tile_(s, c)
                u = i * NT + u
                pe.wait_ge(ptc_r[q], u + 1 + START)
                pe.wait_ge(oc_r[q], u + START)
                if c < LAST:
                    for h, n in halves(c):
                        last = mm(psO[0:DH, q], v[:, s, c - 1 + h], pT[:, q, h], start=(h == int(c == 0)), stop=(h == 1))
                else:
                    for b in range(NB):
                        rows = slice(b * 64, (b + 1) * 64)
                        mm(psO[0:DH, q, rows], vc[:, s, b], pT[:, q, 0, rows], start=True, stop=False)
                        last = mm(psO[0:DH, q, rows], vn[:, s, b], pT[0:TS, q, 1, rows], start=False, stop=True)
                last.then_inc(o_r[q], 1)

            with pe.Fori(0, NKV // 2) as i:
                for s in range(2):
                    scores(i, s, 0)
                    scores(i, s, 1)
                    for c in range(NT):
                        turned(i, s, c)
                        if c < LAST - 1:
                            scores(i, s, c + 2)
                        values(i, s, c)

        def columns(c):
            return slice(P, K2) if c == 0 else (slice(0, K2) if c < LAST else slice(0, P + TS))

        @block.scalar
        def _(act):
            with act.Fori(0, NKV // 2) as i:
                def exps(s, c):
                    q, u = tile_(s, c)
                    u = i * NT + u
                    ks = columns(c)
                    act.wait_ge(nm_r[q], u + 1 + START)
                    act.wait_ge(pt_r[q], u + START)
                    act.wait_ge(pn_r[q], u + START)
                    nc.scalar.activation(es[:, q], es[:, q], ACT.Exp).then_inc(es_r[q], 1)
                    for r in range(QH):
                        last = nc.scalar.activation(pr[:, q, r, ks], s_[:, q, r, ks], ACT.Exp, bias=nm[:, q, r:r + 1], scale=SCALE, accum_out=den[:, q, r:r + 1])
                    last.then_inc(p_r[q], 1)

                def turned(s, c):
                    q, u = tile_(s, c)
                    u = i * NT + u
                    act.wait_ge(pt_r[q], u + 1 + START)
                    act.wait_ge(o_r[q], u + START)
                    for h, n in halves(c):
                        last = nc.scalar.copy(pT[0:n, q, h], psT[0:n, h])
                    last.then_inc(ptc_r[q], 1)

                def outputs(s, c):
                    q, u = tile_(s, c)
                    u = i * NT + u
                    if c == 0:
                        act.wait_ge(o_st[s], i * 16 + START)
                    act.wait_ge(o_r[q], u + 1 + START)
                    src = psO[0:DH, q]
                    if c < LAST:
                        ins = nc.scalar.copy(o[:, s, :, c * P:(c + 1) * P], src.rearrange("d (r t) -> d r t", r=QH))
                    else:
                        ins = nc.scalar.copy(o[:, s, :, SEQ:T].rearrange("d r (b t) -> d r b t", t=TS), src.rearrange("d (b r t) -> d r b t", r=QH, t=TS))
                    ins.then_inc(oc_r[q], 1)

                for s in range(2):
                    act.wait_ge(loaded[s], i * 96 + 96 + START)
                    nc.scalar.copy(qs[:, s].rearrange("d b (r t) -> d r b t", r=QH), qT[:, s, :, SEQ:T].rearrange("d r (b t) -> d r b t", t=TS)).then_inc(qs_r[s], 1)
                    exps(s, 0)
                    for c in range(NT):
                        turned(s, c)
                        if c < LAST:
                            exps(s, c + 1)
                        outputs(s, c)
                    for e in range(2):
                        k = s * NT + LAST - e
                        act.wait_ge(oc_r[k % 2], i * NT + k // 2 + 1 + START)
                    act.dma_start(heads(scr["attn"], (i * 2 + s) * 2, 2), o[:, s]).then_inc(o_st[s], 16)
            for s in range(2):
                act.wait_ge(o_st[s], NKV // 2 * 16 + START)

        @block.vector
        def _(dve):
            vv = nc.vector
            dve.wait_ge(small, 32 + START)
            with dve.Fori(0, NKV // 2) as i:
                ch = Steps(dve, chain, 2 * (2 + 4 * NT), i)
                for s in range(2):
                    g = i * 2 + s
                    ch.step(vv.tensor_copy(sink[:, s, 0], sink_p[:, ds(g, 1)].rearrange("p g r -> p (g r)")))
                    ch.link(vv.tensor_copy(sink[:, s, 1], sink_s[:, ds(g, 1)].to_broadcast([P, QH])))

                    def maxima(c):
                        q, u = tile_(s, c)
                        u = i * NT + u
                        ks = columns(c)
                        n = ks.stop - ks.start
                        dve.wait_ge(s_r[q], u + 1 + START)
                        dve.wait_ge(p_r[q], u + START)
                        if c < LAST:
                            ins = vv.tensor_tensor(s_[:, q, :, ks], psS[:, q, :, ks], amask[:, ks].unsqueeze(1).to_broadcast([P, QH, n]), ALU.add)
                        else:
                            ins = vv.tensor_copy(s_[:, q, :, ks], psS[:, q, :, ks])
                        ins.then_inc(m_r[q], 1)
                        dve.wait_ge(m_r[q], u + 1 + START)
                        ch.link(vv.tensor_reduce(mx[:, q], s_[:, q, :, ks], AX.X, ALU.max))
                        sk = sink[:, s, int(c == LAST)]
                        ch.link(vv.scalar_tensor_tensor(out=mx[:, q], in0=mx[:, q], scalar=SCALE, in1=sk, op0=ALU.mult, op1=ALU.max))
                        vv.tensor_tensor(es[:, q], sk, mx[:, q], ALU.subtract)
                        vv.tensor_scalar(nm[:, q], mx[:, q], -1.0, None, ALU.mult).then_inc(nm_r[q], 1)

                    def normalize(c):
                        q, u = tile_(s, c)
                        u = i * NT + u
                        ks = columns(c)
                        n = ks.stop - ks.start
                        dve.wait_ge(p_r[q], u + 1 + START)
                        dve.wait_ge(es_r[q], u + 1 + START)
                        ch.link(vv.tensor_tensor(den[:, q], den[:, q], es[:, q], ALU.add))
                        ch.link(vv.reciprocal(den[:, q], den[:, q]))
                        vv.tensor_tensor(pr[:, q, :, ks], pr[:, q, :, ks], den[:, q].unsqueeze(2).to_broadcast([P, QH, n]), ALU.mult).then_inc(pn_r[q], 1)

                    maxima(0)
                    maxima(1)
                    for c in range(NT):
                        normalize(c)
                        if c < LAST - 1:
                            maxima(c + 2)
                ch.close()


def load_tiles(sp, dst, src, n, loaded):
    for k in range(n):
        sp.dma_start(dst[:, k], src[k]).then_inc(loaded, 16)


def phase_merge(nc, io, per, scr):
    KS, KA = INNER // P, ATTN // P
    with ExitStack() as ctx:
        sb, pb, sem = open_(nc, ctx)
        ys, ya = sb("mg_ys", [P, KS, T]), sb("mg_ya", [P, KA, T])
        ws, wa = sb("mg_ws", [P, 2, KS, P]), sb("mg_wa", [P, 2, KA, P])
        gates = sb("mg_gates", [P, 2, T])
        out = sb("mg_out", [P, 2, T])
        ps = pb("mg_ps", [P, 2, TB])
        acts, w_in, g_in = sem("mg_acts"), sem("mg_win", 2), sem("mg_gin", 2)
        mm, used, stored, chain = sem("mg_mm", 2), sem("mg_used", 2), sem("mg_stored"), sem("mg_chain")
        block = begin(nc, ctx)

        @block.sync
        def _(sp):
            load_tiles(sp, ys, scr["ynorm"], KS, acts)
            load_tiles(sp, ya, scr["attn"], KA, acts)
            one = lambda src, m: src[ds(m, 1)].rearrange("m p k c -> p (m k) c")
            with sp.Fori(0, KD // 2) as i:
                for s in range(2):
                    m = i * 2 + s
                    sp.wait_ge(mm[0], m + START)
                    sp.wait_ge(mm[1], m + START)
                    sp.dma_start(ws[:, s], one(io["w_ssm"], m)).then_inc(w_in[s], 16)
                    sp.dma_start(wa[:, s], one(io["w_attn"], m)).then_inc(w_in[s], 16)
                    sp.wait_ge(used[1], m + START)
                    for n in range(2):
                        sp.dma_start(gates[:, n], scr["plain"][ds(m + (TG + n * KD), 1)].rearrange("m p t -> p (m t)")).then_inc(g_in[s], 16)

        @block.tensor
        def _(pe):
            pe.wait_ge(acts, (KS + KA) * 16 + START)
            with pe.Fori(0, KD // 2) as i:
                for s in range(2):
                    m = i * 2 + s
                    pe.wait_ge(w_in[s], i * 32 + 32 + START)
                    for n, (w, y, k) in enumerate(((ws, ys, KS), (wa, ya, KA))):
                        pe.wait_ge(used[n], m + START)
                        product(nc, ps[:, n], w[:, s], y, k).then_inc(mm[n], 1)

        @block.vector
        def _(dve):
            v = nc.vector
            with dve.Fori(0, KD // 2) as i:
                for s in range(2):
                    m = i * 2 + s
                    dve.wait_ge(g_in[s], i * 32 + 32 + START)
                    for n in range(2):
                        dve.wait_ge(mm[n], m + 1 + START)
                        if n == 0:
                            dve.wait_ge(stored, m * 16 + START)
                        v.tensor_tensor(out[:, n], ps[:, n, 0:T], gates[:, n], ALU.mult).then_inc(used[n], 1)
                    dve.wait_ge(used[0], m + 1 + START)
                    dve.wait_ge(used[1], m + 1 + START)
                    v.tensor_tensor(out[:, 0], out[:, 0], out[:, 1], ALU.add).then_inc(chain, 1)

        @block.scalar
        def _(act):
            with act.Fori(0, KD) as m:
                act.wait_ge(chain, m + 1 + START)
                act.dma_start(scr["merged"][ds(m, 1)].rearrange("m p t -> p (m t)"), out[:, 0]).then_inc(stored, 16)
            act.wait_ge(stored, KD * 16 + START)


def phase_out(nc, io, per, scr):
    with ExitStack() as ctx:
        sb, pb, sem = open_(nc, ctx)
        y, x = sb("ou_y", [P, KD, T]), sb("ou_x", [P, KD, T])
        w = sb("ou_w", [P, 2, KD, P])
        g1 = sb("ou_gate", [P, 2, NC_])
        t, o = sb("ou_t", [P, 2, T]), sb("ou_o", [P, 2, T])
        ps = pb("ou_ps", [P, 2, TB])
        acts, w_in, mm, used, done, stored = sem("ou_acts"), sem("ou_win", 2), sem("ou_mm", 2), sem("ou_used", 2), sem("ou_done", 2), sem("ou_stored", 2)
        gate_r = sem("ou_gate_r")
        block = begin(nc, ctx)

        @block.sync
        def _(sp):
            load_tiles(sp, y, scr["merged"], KD, acts)
            sp.dma_start(x[:], io["x"][:]).then_inc(acts, 16)
            with sp.Fori(0, KD // 2) as i:
                for s in range(2):
                    sp.wait_ge(mm[s], i + START)
                    sp.dma_start(w[:, s], io["w_out"][ds(i * 2 + s, 1)].rearrange("m p k c -> p (m k) c")).then_inc(w_in[s], 16)

        @block.tensor
        def _(pe):
            pe.wait_ge(acts, (KD + 1) * 16 + START)
            with pe.Fori(0, KD // 2) as i:
                for s in range(2):
                    pe.wait_ge(w_in[s], i * 16 + 16 + START)
                    pe.wait_ge(used[s], i + START)
                    product(nc, ps[:, s], w[:, s], y, KD).then_inc(mm[s], 1)

        @block.vector
        def _(dve):
            v = nc.vector
            dve.wait_ge(acts, (KD + 1) * 16 + START)
            with dve.Fori(0, KD // 2) as i:
                for s in range(2):
                    m = i * 2 + s
                    v.tensor_copy(g1[:, s], per["mod"][:, ds(m + 2 * KD, 1)].rearrange("p m c -> p (m c)")).then_inc(gate_r, 1)
                    dve.wait_ge(gate_r, m + 1 + START)
                    dve.wait_ge(mm[s], i + 1 + START)
                    dve.wait_ge(stored[s], i * 16 + START)
                    v.tensor_scalar(t[:, s, 0:SEQ], ps[:, s, 0:SEQ], g1[:, s, 0:1], None, ALU.mult)
                    v.tensor_tensor(samples(t[:, s]), samples(ps[:, s]), g1[:, s, 1:NC_].unsqueeze(2).to_broadcast([P, NB, TS]), ALU.mult).then_inc(used[s], 1)
                    dve.wait_ge(used[s], i + 1 + START)
                    v.tensor_tensor(o[:, s], t[:, s], x[:, ds(m, 1)].rearrange("p m t -> p (m t)"), ALU.add).then_inc(done[s], 1)

        @block.scalar
        def _(act):
            with act.Fori(0, KD // 2) as i:
                for s in range(2):
                    act.wait_ge(done[s], i + 1 + START)
                    act.dma_start(scr["x1"][ds(i * 2 + s, 1)].rearrange("m p t -> p (m t)"), o[:, s]).then_inc(stored[s], 16)
            for s in range(2):
                act.wait_ge(stored[s], KD // 2 * 16 + START)


def phase_peer(nc, io, per, scr):
    with ExitStack() as ctx:
        h2 = [ctx.enter_context(nc.sbuf_tensor("h2_" + n, [P, KD, T], F32R)) for n in ("hi", "lo")]
        with ExitStack() as ctx2:
            picks = ctx2.enter_context(nc.sbuf_tensor("picks", [P, 3, T], F32))
            with nc.sbuf_tensor("top_v", [P, NT, 2 * PH, TOPK], F32) as top_v, nc.sbuf_tensor("top_i", [P, NT, 2 * PH, TOPK], F32) as top_i:
                phase_norm2(nc, io, per, scr, h2)
                phase_keys(nc, io, per, h2, top_v, top_i)
                phase_picks(nc, io, per, top_v, top_i, picks)
            phase_gates(nc, io, per, scr, picks)
        phase_experts(nc, io, per, scr, h2)


def phase_norm2(nc, io, per, scr, h2):
    with ExitStack() as ctx:
        sb, pb, sem = open_(nc, ctx)
        x = sb("n2_x", [P, KD, T])
        sq, tmp, rstd, out = sb("n2_sq", [P, 2, T]), sb("n2_tmp", [P, 2, T]), sb("n2_rstd", [P, T]), sb("n2_out", [P, 2, T])
        ps = pb("n2_ps", [P, TB])
        x_in = sem("n2_x_in")
        sems = [sem(f"n2_{n}") for n in ("squared", "summed", "rooted", "chain")]
        block = begin(nc, ctx)

        @block.sync
        def _(sp):
            load_tiles(sp, x, scr["x1"], KD, x_in)
        norm_engines(nc, block, per, x, x_in, KD * 16, sq, ps, rstd, sems, modulated(nc, per, x, rstd, h2[0], h2[1], 1, 3 * KD, tmp, out))


def top16(v, ch, vals, idx, spare, src):
    ch.link(v.max(vals[:, 0:8], src))
    ch.step(v.max_index(idx[:, 0:8], vals[:, 0:8], src))
    ch.link(v.match_replace(spare, vals[:, 0:8], src, NEG))
    ch.link(v.max(vals[:, 8:16], spare))
    ch.link(v.max_index(idx[:, 8:16], vals[:, 8:16], spare))


def phase_keys(nc, io, per, h2, top_v, top_i):
    with ExitStack() as ctx:
        sb, pb, sem = open_(nc, ctx)
        w, keys = sb("ky_w", [P, 2, KD, P]), sb("ky_keys", [P, 2, N_KEYS])
        w2 = [sb("ky_w_" + n, [P, 2, KD, P], F32R) for n in ("hi", "lo")]
        q = sb("ky_q", [P, 2, T])
        val, idx = sb("ky_val", [P, 2, NT, TOPK]), sb("ky_idx", [P, 2, NT, TOPK], U32)
        spare = sb("ky_spare", [P, N_KEYS])
        score = sb("ky_score", [P, 2, NT, N_KEYS])
        ps, psk = pb("ky_ps", [P, 3, 512]), pb("ky_psk", [P, TB])
        w_hi, w_lo = sem("ky_whi", 2), sem("ky_wlo", 2)
        w_in, mm, q_r, sc_mm, sc_r, done = (sem("ky_" + n, 2) for n in ("win", "mm", "qr", "scmm", "scr", "done"))
        chain = sem("ky_chain")
        block = begin(nc, ctx)

        @block.sync
        def _(sp):
            with sp.Fori(0, PH) as i:
                for s in range(2):
                    sp.wait_ge(sc_mm[s], i + START)
                    sp.dma_start(w[:, s], io["w_query"][ds(i * 2 + s, 1)].rearrange("m p k c -> p (m k) c")).then_inc(w_in[s], 16)
                    sp.dma_start(keys[:, s], io["keys"][ds(i * 2 + s, 1)].rearrange("m d k -> d (m k)")).then_inc(w_in[s], 16)

        @block.tensor
        def _(pe):
            with pe.Fori(0, PH) as i:
                for s in range(2):
                    pe.wait_ge(w_lo[s], i + 1 + START)
                    pe.wait_ge(q_r[1 - s], i + s + START)
                    product3(nc, ps, [x[:, s] for x in w2], h2, KD).then_inc(mm[s], 1)
                    pe.wait_ge(q_r[s], i + 1 + START)
                    pe.wait_ge(sc_r[1 - s], i + s + START)
                    for t in range(NT):
                        last = nc.tensor.matmul(psk[:, t * P:(t + 1) * P], q[:, s, t * P:(t + 1) * P], keys[:, s], start=True, stop=True)
                    last.then_inc(sc_mm[s], 1)

        @block.scalar
        def _(act):
            with act.Fori(0, PH) as i:
                for s in range(2):
                    act.wait_ge(w_in[s], i * 32 + 32 + START)
                    act.wait_ge(mm[s], i + START)
                    nc.scalar.copy(w2[0][:, s], w[:, s]).then_inc(w_hi[s], 1)
                    if s == 1:
                        for e in range(2):
                            act.wait_ge(mm[e], i + 1 + START)
                            act.wait_ge(sc_mm[e], i + START)
                            nc.scalar.copy(cut(q[:, e]), banks(ps)).then_inc(q_r[e], 1)

        @block.vector
        def _(dve):
            v = nc.vector
            with dve.Fori(0, PH) as i:
                ch = Steps(dve, chain)
                for s in range(2):
                    dve.wait_ge(w_hi[s], i + 1 + START)
                    v.tensor_tensor(w2[1][:, s], w[:, s], w2[0][:, s].bitcast(F32), ALU.subtract).then_inc(w_lo[s], 1)
                for s in range(2):
                    dve.wait_ge(sc_mm[s], i + 1 + START)
                    v.tensor_copy(score[:, s].rearrange("p t k -> p (t k)"), psk[:, 0:T]).then_inc(sc_r[s], 1)
                    dve.wait_ge(sc_r[s], i + 1 + START)
                    ch.link(v.memset(spare[:], NEG))
                    for t in range(NT):
                        top16(v, ch, val[:, s, t], idx[:, s, t], spare[:], score[:, s, t])
                    m = i * 2 + s
                    v.tensor_copy(top_v[:, :, ds(m, 1)].rearrange("p t m k -> p t (m k)"), val[:, s])
                    v.tensor_copy(top_i[:, :, ds(m, 1)].rearrange("p t m k -> p t (m k)"), idx[:, s]).then_inc(done[s], 1)
                    dve.wait_ge(done[s], i + 1 + START)
                ch.link(v.memset(spare[:], NEG))
                dve.sem_clear(chain)
                dve.sem_inc(chain, START)


def phase_picks(nc, io, per, top_v, top_i, picks):
    KK = TOPK * TOPK
    with ExitStack() as ctx:
        sb, pb, sem = open_(nc, ctx)
        sv, si = sb("pk_sv", [P, 2 * PH, TOPK]), sb("pk_si", [P, 2 * PH, TOPK])
        comb, spare = sb("pk_comb", [P, PH, KK]), sb("pk_spare", [P, 2, KK])
        fv, fi = sb("pk_fv", [P, PH, TOPK]), sb("pk_fi", [P, PH, TOPK], U32)
        half_u, half = sb("pk_half_u", [P, 2, HK], U32), sb("pk_half", [P, 2, HK])
        hot = sb("pk_hot", [P, HK, TOPK])
        out = sb("pk_out", [P, 3, HK])
        e, den = sb("pk_e", [P, PH, TOPK]), sb("pk_den", [P, PH])
        ps = pb("pk_ps", [P, 3, P])
        chain, e_in, e_out, o_r, tr, copied = (sem("pk_" + n) for n in ("chain", "ein", "eout", "or", "tr", "copied"))
        block = begin(nc, ctx)
        ident = per["const"][:, C_ID:C_ID + P]
        iota = per["const"][:, C_IOTA:C_IOTA + TOPK]

        @block.vector
        def _(dve):
            v = nc.vector
            with dve.Fori(0, NT) as t:
                ch = Steps(dve, chain)
                ch.step(v.tensor_copy(sv[:], top_v[:, ds(t, 1)].rearrange("p t m k -> p (t m) k")))
                ch.link(v.tensor_copy(si[:], top_i[:, ds(t, 1)].rearrange("p t m k -> p (t m) k")))
                halves = lambda x, n: x[:].rearrange("p (h n) k -> p n h k", n=2)[:, n]
                ch.link(v.tensor_tensor(comb[:].rearrange("p h (a b) -> p h a b", a=TOPK), halves(sv, 0).unsqueeze(3).to_broadcast([P, PH, TOPK, TOPK]),
                                        halves(sv, 1).unsqueeze(2).to_broadcast([P, PH, TOPK, TOPK]), ALU.add))
                for h in range(PH):
                    top16(v, ch, fv[:, h], fi[:, h], spare[:, h % 2], comb[:, h])
                dve.wait_ge(e_out, t + START)
                v.tensor_tensor(e[:], fv[:], fv[:, :, 0:1].to_broadcast([P, PH, TOPK]), ALU.subtract).then_inc(e_in, 1)
                picked = fi[:].rearrange("p h k -> p (h k)")
                ch.step(v.tensor_scalar(half_u[:, 0], picked, 4, None, ALU.logical_shift_right))
                ch.link(v.tensor_scalar(half_u[:, 1], picked, TOPK - 1, None, ALU.bitwise_and))
                ch.link(v.tensor_copy(half[:], half_u[:]))
                dve.wait_ge(tr, t + START)
                for n in range(2):
                    ch.link(v.tensor_tensor(hot[:], half[:, n].unsqueeze(2).to_broadcast([P, HK, TOPK]), iota.unsqueeze(1).to_broadcast([P, HK, TOPK]), ALU.is_equal))
                    hv = hot[:].rearrange("p (h k) a -> p h k a", h=PH)
                    ch.link(v.tensor_tensor(hv, hv, halves(si, n).unsqueeze(2).to_broadcast([P, PH, TOPK, TOPK]), ALU.mult))
                    ch.link(v.tensor_reduce(out[:, n], hot[:], AX.X, ALU.add))
                dve.wait_ge(e_out, t + 1 + START)
                ch.link(v.tensor_reduce(den[:], e[:], AX.X, ALU.add))
                ch.link(v.reciprocal(den[:], den[:]))
                v.tensor_tensor(out[:, 2].rearrange("p (h k) -> p h k", h=PH), e[:], den[:].unsqueeze(2).to_broadcast([P, PH, TOPK]), ALU.mult).then_inc(o_r, 1)
                dve.sem_clear(chain)
                dve.sem_inc(chain, START)

        @block.tensor
        def _(pe):
            with pe.Fori(0, NT) as t:
                pe.wait_ge(o_r, t + 1 + START)
                pe.wait_ge(copied, t + START)
                for n in range(3):
                    last = nc.tensor.transpose(ps[:, n], out[:, n], ident)
                last.then_inc(tr, 1)

        @block.scalar
        def _(act):
            with act.Fori(0, NT) as t:
                act.wait_ge(e_in, t + 1 + START)
                act.wait_ge(o_r, t + START)
                nc.scalar.activation(e[:], e[:], ACT.Exp).then_inc(e_out, 1)
                act.wait_ge(tr, t + 1 + START)
                nc.scalar.copy(picks[:, :, ds(t * P, P)], ps[:]).then_inc(copied, 1)


def phase_gates(nc, io, per, scr, picks):
    B = 8
    NBAT = P // B
    with ExitStack() as ctx:
        sb, pb, sem = open_(nc, ctx)
        cur = sb("gt_cur", [P, 2, 3, B])
        one1, one2 = sb("gt_one1", [P, 2, B, P]), sb("gt_one2", [P, 2, B, P])
        stage = sb("gt_stage", [P, N_KEYS, P])
        ps = pb("gt_ps", [P, 2, B * P])
        cur_r, hot_r, mm, ev, stored = sem("gt_cur_r", 2), sem("gt_hot", 2), sem("gt_mm", 2), sem("gt_ev", 2), sem("gt_stored")
        block = begin(nc, ctx)
        iota = per["const"][:, C_IOTA:C_IOTA + P]

        @block.vector
        def _(dve):
            v = nc.vector
            with dve.Fori(0, NT * NBAT // 2) as i:
                for s in range(2):
                    v.tensor_copy(cur[:, s], picks[:, :, ds((i * 2 + s) * B, B)]).then_inc(cur_r[s], 1)
                    dve.wait_ge(cur_r[s], i + 1 + START)
                    dve.wait_ge(mm[s], i + START)
                    for b in range(B):
                        v.tensor_scalar(one1[:, s, b], iota, cur[:, s, 0, b:b + 1], None, ALU.is_equal)
                        last = v.tensor_scalar(one2[:, s, b], iota, cur[:, s, 1, b:b + 1], cur[:, s, 2, b:b + 1], ALU.is_equal, ALU.mult)
                    last.then_inc(hot_r[s], 1)

        @block.tensor
        def _(pe):
            with pe.Fori(0, NT * NBAT // 2) as i:
                for s in range(2):
                    pe.wait_ge(hot_r[s], i + 1 + START)
                    pe.wait_ge(ev[s], i + START)
                    for b in range(B):
                        last = nc.tensor.matmul(ps[:, s, b * P:(b + 1) * P], one1[:, s, b], one2[:, s, b], start=True, stop=True)
                    last.then_inc(mm[s], 1)

        @block.scalar
        def _(act):
            with act.Fori(0, NT) as t:
                act.wait_ge(stored, t * 16 + START)
                for j in range(NBAT):
                    s = j % 2
                    act.wait_ge(mm[s], t * (NBAT // 2) + j // 2 + 1 + START)
                    nc.scalar.copy(stage[:, :, j * B:(j + 1) * B].rearrange("p k t -> p t k"), ps[:, s].rearrange("p (t k) -> p t k", t=B)).then_inc(ev[s], 1)
                for s in range(2):
                    act.wait_ge(ev[s], (t + 1) * (NBAT // 2) + START)
                act.dma_start(scr["gate"][:, :, ds(t * P, P)], stage[:]).then_inc(stored, 16)
            act.wait_ge(stored, NT * 16 + START)


def phase_experts(nc, io, per, scr, h2):
    E = 2
    BATCHES = N_KEYS // E
    SUMS = 3 * KD // 2
    with ExitStack() as ctx:
        sb, pb, sem = open_(nc, ctx)
        acc = sb("ex_acc", [P, KD, T])
        with ExitStack() as ctx2:
            sb2, pb2, _ = open_(nc, ctx2)
            pair = lambda name, shape: [sb2(name + n, shape, F32R) for n in ("_hi", "_lo")]
            u, vv = sb2("ex_u", [P, E, KD, P]), sb2("ex_v", [P, E, D])
            u2, v2, g2 = pair("ex_u", [P, E, KD, P]), pair("ex_v", [P, E, D]), pair("ex_g", [P, E, T])
            gate = sb2("ex_gate", [P, E, T])
            act_ = sb2("ex_act", [P, E, T])
            ps, pv = pb2("ex_ps", [P, E, 3, 512]), pb2("ex_pv", [P, 2, 512])
            u_in, v_in, gate_in, mm = (sem("ex_" + n, E) for n in ("uin", "vin", "gatein", "mm"))
            u_hi, u_lo, v_hi, v_lo = (sem("ex_" + n, E) for n in ("uhi", "ulo", "vhi", "vlo"))
            gelu_r, gated, g_hi, g_lo = (sem("ex_" + n, E) for n in ("gelur", "gated", "ghi", "glo"))
            sum_mm, sum_r = sem("ex_summm", 2), sem("ex_sumr", 2)
            zero = sem("ex_zero")
            block = begin(nc, ctx2)

            @block.sync
            def _(sp):
                with sp.Fori(0, BATCHES) as b:
                    for e in range(E):
                        sp.wait_ge(u_lo[e], b + START)
                        sp.dma_start(u[:, e], io["expert_u"][ds(b * E + e, 1)].rearrange("e p k c -> p (e k) c")).then_inc(u_in[e], 16)
                    for e in range(E):
                        sp.wait_ge(gated[e], b + START)
                        sp.dma_start(gate[:, e], scr["gate"][:, ds(b * E + e, 1)].rearrange("p e t -> p (e t)")).then_inc(gate_in[e], 16)
                        sp.wait_ge(v_lo[e], b + START)
                        sp.dma_start(vv[:, e], io["expert_v"][ds(b * E + e, 1)].rearrange("e p d -> p (e d)")).then_inc(v_in[e], 16)

            @block.tensor
            def _(pe):
                def u_products(b):
                    for e in range(E):
                        pe.wait_ge(u_lo[e], b + 1 + START)
                        pe.wait_ge(gelu_r[e], b + START)
                        product3(nc, ps[:, e], [x[:, e] for x in u2], h2, KD).then_inc(mm[e], 1)

                def v_products(b):
                    for e in range(E):
                        pe.wait_ge(v_lo[e], b + 1 + START)
                        pe.wait_ge(g_lo[e], b + 1 + START)
                    for d in range(KD):
                        for c in range(3):
                            j = d * 3 + c
                            pe.wait_ge(sum_r[j % 2], b * SUMS + j // 2 + START)
                            for e in range(E):
                                for x, y in SPLIT:
                                    last = nc.tensor.matmul(pv[:, j % 2, 0:CW], v2[x][:, e, d * P:(d + 1) * P], g2[y][:, e, c * CW:(c + 1) * CW],
                                                            start=(e == 0 and (x, y) == SPLIT[0]), stop=(e == E - 1 and (x, y) == SPLIT[-1]))
                            last.then_inc(sum_mm[j % 2], 1)

                u_products(0)
                with pe.Fori(0, BATCHES - 1) as b:
                    u_products(b + 1)
                    v_products(b)
                v_products(BATCHES - 1)

            @block.scalar
            def _(act):
                def round_u(b, e):
                    act.wait_ge(u_in[e], b * 16 + 16 + START)
                    act.wait_ge(mm[e], b + START)
                    nc.scalar.copy(u2[0][:, e], u[:, e]).then_inc(u_hi[e], 1)

                def gelu(b, e):
                    act.wait_ge(mm[e], b + 1 + START)
                    act.wait_ge(g_lo[e], b + START)
                    nc.scalar.activation(cut(act_[:, e]), banks(ps[:, e]), ACT.Gelu_apprx_tanh).then_inc(gelu_r[e], 1)

                def round_g_and_v(b):
                    for z in range(2):
                        act.wait_ge(sum_mm[z], b * SUMS + START)
                    for e in range(E):
                        act.wait_ge(gated[e], b + 1 + START)
                        nc.scalar.copy(g2[0][:, e], act_[:, e]).then_inc(g_hi[e], 1)
                        act.wait_ge(v_in[e], b * 16 + 16 + START)
                        nc.scalar.copy(v2[0][:, e], vv[:, e]).then_inc(v_hi[e], 1)

                def batch(b, more):
                    for e in range(E):
                        gelu(b, e)
                        if more:
                            round_u(b + 1, e)
                    round_g_and_v(b)

                for e in range(E):
                    round_u(0, e)
                with act.Fori(0, BATCHES - 1) as b:
                    batch(b, True)
                batch(BATCHES - 1, False)

            @block.vector
            def _(dve):
                v = nc.vector

                def rest_of_u(b, e):
                    dve.wait_ge(u_hi[e], b + 1 + START)
                    v.tensor_tensor(u2[1][:, e], u[:, e], u2[0][:, e].bitcast(F32), ALU.subtract).then_inc(u_lo[e], 1)

                def apply_gate(b, e):
                    dve.wait_ge(gelu_r[e], b + 1 + START)
                    dve.wait_ge(gate_in[e], b * 16 + 16 + START)
                    v.tensor_tensor(act_[:, e], act_[:, e], gate[:, e], ALU.mult).then_inc(gated[e], 1)

                def rest_of_g_and_v(b):
                    for e in range(E):
                        dve.wait_ge(g_hi[e], b + 1 + START)
                        v.tensor_tensor(g2[1][:, e], act_[:, e], g2[0][:, e].bitcast(F32), ALU.subtract).then_inc(g_lo[e], 1)
                        dve.wait_ge(v_hi[e], b + 1 + START)
                        v.tensor_tensor(v2[1][:, e], vv[:, e], v2[0][:, e].bitcast(F32), ALU.subtract).then_inc(v_lo[e], 1)

                def add_sums(b, first, end):
                    for j in range(first, end):
                        a = (j % 3) * CW
                        dve.wait_ge(sum_mm[j % 2], b * SUMS + j // 2 + 1 + START)
                        v.tensor_tensor(acc[:, j // 3, a:a + CW], acc[:, j // 3, a:a + CW], pv[:, j % 2, 0:CW], ALU.add).then_inc(sum_r[j % 2], 1)

                v.memset(acc[:], 0.0).then_inc(zero, 1)
                dve.wait_ge(zero, 1 + START)
                for e in range(E):
                    rest_of_u(0, e)
                apply_gate(0, 0)
                rest_of_u(1, 0)
                apply_gate(0, 1)
                rest_of_u(1, 1)
                rest_of_g_and_v(0)

                def batch(b, more):
                    apply_gate(b + 1, 0)
                    if more:
                        rest_of_u(b + 2, 0)
                    add_sums(b, 0, 6)
                    apply_gate(b + 1, 1)
                    add_sums(b, 6, 10)
                    if more:
                        rest_of_u(b + 2, 1)
                    add_sums(b, 10, 3 * KD)
                    rest_of_g_and_v(b + 1)

                with dve.Fori(0, BATCHES - 2) as b:
                    batch(b, True)
                batch(BATCHES - 2, False)
                add_sums(BATCHES - 1, 0, 3 * KD)
        finish_output(nc, io, per, scr, acc)


def finish_output(nc, io, per, scr, acc):
    with ExitStack() as ctx:
        sb, pb, sem = open_(nc, ctx)
        x = sb("fo_x", [P, KD, T])
        fg = sb("fo_g", [P, KD])
        sq, rstd, y = sb("fo_sq", [P, 2, T]), sb("fo_rstd", [P, T]), sb("fo_y", [P, 2, T])
        ps = pb("fo_ps", [P, TB])
        x_in, x_r, y_st, y_r = sem("fo_xin"), sem("fo_xr"), sem("fo_yst", 2), sem("fo_yr")
        pre = sem("fo_pre")
        squared, summed, rooted, chain = (sem("fo_" + n) for n in ("sq", "sum", "root", "chain"))
        block = begin(nc, ctx)
        ones = per["const"][:, C_ONE:C_ONE + P]

        @block.sync
        def _(sp):
            load_tiles(sp, x, scr["x1"], KD, x_in)
            sp.dma_start(fg[:], io["final_g"][:]).then_inc(x_in, 16)
            for k in range(KD):
                sp.wait_ge(y_r, k + 1 + START)
                sp.dma_start(io["y"][k], y[:, k % 2]).then_inc(y_st[k % 2], 16)
            for s in range(2):
                sp.wait_ge(y_st[s], KD // 2 * 16 + START)

        @block.vector
        def _(dve):
            v, mod = nc.vector, per["mod"]
            dve.wait_ge(x_in, (KD + 1) * 16 + START)
            for k in range(KD):
                v.tensor_scalar(acc[:, k, 0:SEQ], acc[:, k, 0:SEQ], mod[:, 5 * KD + k, 0:1], None, ALU.mult)
                v.tensor_tensor(samples(acc[:, k]), samples(acc[:, k]), per_token(mod[:, 5 * KD:6 * KD], k), ALU.mult).then_inc(pre, 1)
            for k in range(KD):
                dve.wait_ge(pre, k + 1 + START)
                v.tensor_tensor(x[:, k], x[:, k], acc[:, k], ALU.add).then_inc(x_r, 1)
            dve.wait_ge(rooted, 1 + START)
            v.reciprocal(rstd[:], rstd[:]).then_inc(chain, 1)
            dve.wait_ge(chain, 1 + START)
            for k in range(KD):
                if k >= 2:
                    dve.wait_ge(y_st[k % 2], k // 2 * 16 + START)
                v.scalar_tensor_tensor(out=y[:, k % 2], in0=x[:, k], scalar=fg[:, k:k + 1], in1=rstd[:], op0=ALU.mult, op1=ALU.mult).then_inc(y_r, 1)

        @block.scalar
        def _(act):
            for k in range(KD):
                act.wait_ge(x_r, k + 1 + START)
                if k >= 2:
                    act.wait_ge(summed, k - 1 + START)
                nc.scalar.activation(sq[:, k % 2], x[:, k], ACT.Square).then_inc(squared, 1)
            act.wait_ge(summed, KD + START)
            nc.scalar.activation(rstd[:], ps[:, 0:T], ACT.Sqrt, bias=per["eps"][:, 0:1], scale=1.0 / D).then_inc(rooted, 1)

        @block.tensor
        def _(pe):
            for k in range(KD):
                pe.wait_ge(squared, k + 1 + START)
                for a, n in COLS:
                    last = nc.tensor.matmul(ps[:, a:a + n], ones, sq[:, k % 2, a:a + n], start=(k == 0), stop=(k == KD - 1))
                last.then_inc(summed, 1)


def build(nc, io, outs):
    io = dict(io, **outs)
    with ExitStack() as ctx:
        sb, pb, sem = open_(nc, ctx)
        dram = lambda name, shape: nc.dram_tensor(name, shape, F32, kind="Internal").ap()
        scr = {
            "plain": dram("scr_plain", [NPLAIN, P, T]), "xbc": dram("scr_xbc", [MX, P, T]),
            "vd": dram("scr_vd", [P, NT, KV + H]), "ynorm": dram("scr_ynorm", [INNER // P, P, T]),
            "attn": dram("scr_attn", [ATTN // P, P, T]), "merged": dram("scr_merged", [KD, P, T]),
            "x1": dram("scr_x1", [KD, P, T]), "gate": dram("scr_gate", [P, N_KEYS, T]),
        }
        per = {"const": sb("const", [P, C_N]), "mod": sb("mod", [P, 6 * KD, NC_]),
               "gain": sb("gain", [P, 2, KD, NC_]), "eps": sb("eps", [P, 1])}
        nc.vector.memset(per["eps"][:], EPS)
        phase_modulation(nc, io, per)
        with nc.sbuf_tensor("h_hi", [P, KD, T], F32R) as hi, nc.sbuf_tensor("h_lo", [P, KD, T], F32R) as lo:
            phase_norm1(nc, io, per, hi, lo)
            phase_projection(nc, io, per, (hi, lo), scr)
        phase_ssd(nc, io, per, scr)
        phase_attention(nc, io, per, scr)
        phase_merge(nc, io, per, scr)
        phase_out(nc, io, per, scr)
        phase_peer(nc, io, per, scr)



def kernel(**inputs):
    import numpy as np
    import concourse.bacc as bacc
    from concourse.bass_utils import run_bass_kernel_spmd

    a = {k: np.asarray(v) for k, v in inputs.items()}

    def col(v, m):
        return v.reshape((m, P) + v.shape[1:]).swapaxes(0, 1)

    def tiles(w):
        return w.reshape(w.shape[0] // P, P, w.shape[1] // P, P).transpose(2, 1, 0, 3)

    def constants():
        i = np.arange(P)
        out = np.zeros((P, C_N), np.float32)
        out[:, C_ID:C_ID + P] = np.eye(P)
        out[:, C_ONE:C_ONE + P] = 1
        for n, size in enumerate((P, TS)):
            same = i[:, None] // size == i[None] // size
            upto = same & (i[:, None] <= i[None])
            out[:, C_TRI + n * P:C_TRI + (n + 1) * P] = upto
            out[:, C_STRI + n * P:C_STRI + (n + 1) * P] = same & (i[:, None] > i[None])
            out[:, C_NEG + n * P:C_NEG + (n + 1) * P] = np.where(upto, 0, NEG)
        q, k = i[:, None] // CHUNK, np.arange(2 * P)[None] // CHUNK
        out[:, C_AM:C_AM + 2 * P] = np.where((k >= q) & (k <= q + 2), 0, NEG)
        out[:, C_IOTA:C_IOTA + P] = i[None]
        out[:, C_BM:C_BM + NB] = i[:, None] // TS == np.arange(NB)[None]
        return out

    w_in = a["w_in"][0]
    off_xbc, off_dt = INNER, INNER + CONV
    off_q = off_dt + H
    off_k, off_v, off_g = off_q + ATTN, off_q + ATTN + KV, off_q + ATTN + 2 * KV
    cols = lambda s, n: w_in[:, s:s + n]
    sinks = a["attn_sinks"][0].reshape(NKV, QH)
    arrays = {
        "const": constants(),
        "x": col(np.concatenate([a["x_prompt"][0], a["x_sample"].reshape(-1, D)]).T, KD),
        "c": col(np.concatenate([a["c_prompt"], a["c_sample"]]).T, KD),
        "ada_w": tiles(a["ada_w"][0]), "ada_b": col(a["ada_b"][0], 6 * KD),
        "norm_g": np.stack([col(a["norm1_g"][0], KD), col(a["norm2_g"][0], KD)], 1),
        "final_g": col(a["final_g"], KD),
        "w_main": tiles(np.concatenate([cols(0, INNER), cols(off_g, 2 * D), cols(off_q, ATTN), cols(off_k, KV), cols(off_xbc, CONV)], 1)),
        "w_vdt": col(np.concatenate([cols(off_v, KV), cols(off_dt, H)], 1), KD),
        "conv_hist": col(a["state_conv"][0].transpose(2, 0, 1), MX),
        "conv_w": col(np.concatenate([a["conv_w"][0], a["conv_b"]]).T, MX),
        "ssm_in": a["state_ssm"][0].reshape(NB, G, R * HD, N).transpose(1, 3, 0, 2),
        "dt_rows": np.broadcast_to(np.stack([a["dt_bias"][0], a["a_log"][0]]), (P, 2, H)),
        "d_skip": np.repeat(a["d_skip"][0].reshape(H // 2, 2), HD, 1).T.reshape(P, G, 2),
        "ssm_g": col(a["ssm_norm_g"][0], INNER // P).reshape(P, G, 2),
        "k_cache": a["cache_attn_k"][0].transpose(2, 3, 0, 1),
        "v_cache": a["cache_attn_v"][0].transpose(2, 1, 0, 3),
        "sink_prompt": np.broadcast_to(sinks[None], (P, NKV, QH)),
        "sink_sample": np.broadcast_to(sinks.T[None, :, None], (2, QH, TS, NKV)).reshape(P, NKV),
        "w_ssm": tiles(a["w_branch_ssm"][0]), "w_attn": tiles(a["w_branch_attn"][0]), "w_out": tiles(a["w_out"][0]),
        "w_query": tiles(a["peer_wq"][0]),
        "keys": a["peer_keys"][0].reshape(2 * PH, N_KEYS, P).transpose(0, 2, 1),
        "expert_u": a["peer_u"][0].reshape(N_KEYS, N_KEYS, KD, P).transpose(1, 3, 2, 0),
        "expert_v": a["peer_v"][0].reshape(N_KEYS, N_KEYS, D).transpose(1, 0, 2),
    }
    out_shapes = {
        "y": [KD, P, T], "k_prompt": [MK, P, P], "v_prompt": [P, KV], "k_sample": [MK, P, P], "v_sample": [P, KV],
        "conv_prompt": [P, MX, TAPS - 1], "conv_sample": [P, MX, NB * (TAPS - 1)],
        "ssm_prompt": [G, N, R * HD], "ssm_sample": [G, N, NB, R * HD],
    }
    nc = bacc.Bacc("TRN2", target_bir_lowering=False, num_devices=1)
    feed, io = {}, {}
    for name, v in arrays.items():
        feed["in_" + name] = np.ascontiguousarray(v)
        io[name] = nc.dram_tensor("in_" + name, feed["in_" + name].shape, F32, kind="ExternalInput").ap()
    outs = {n: nc.dram_tensor("out_" + n, s, F32, kind="ExternalOutput").ap() for n, s in out_shapes.items()}
    build(nc, io, outs)
    r = run_bass_kernel_spmd(nc, [feed], core_ids=[0]).results[0]
    o = {n: np.asarray(r["out_" + n]) for n in out_shapes}
    y = o["y"].reshape(D, T).T
    uncol = lambda v: v.swapaxes(0, 1).reshape((-1,) + v.shape[2:])
    return (
        np.ascontiguousarray(y[:SEQ]).reshape(1, SEQ, D), np.ascontiguousarray(y[SEQ:]).reshape(NB, TS, D),
        o["k_prompt"].reshape(KV, P).T.reshape(1, 1, P, NKV, DH), o["v_prompt"].reshape(1, 1, P, NKV, DH),
        uncol(o["conv_prompt"]).T.reshape(1, 1, TAPS - 1, CONV),
        o["ssm_prompt"].transpose(0, 2, 1).reshape(1, 1, H, HD, N),
        o["k_sample"].reshape(KV, NB, TS).transpose(1, 2, 0).reshape(1, NB, TS, NKV, DH),
        o["v_sample"].reshape(1, NB, TS, NKV, DH),
        uncol(o["conv_sample"]).reshape(CONV, NB, TAPS - 1).transpose(1, 2, 0)[None],
        o["ssm_sample"].transpose(2, 0, 3, 1).reshape(1, NB, H, HD, N),
    )
```

```python
import concourse.bass as bass
from concourse import mybir
from contextlib import ExitStack

P = 128
D = 1024
KD = D // P
SEQ = 1024
NB, TS = 8, 16
T = SEQ + NB * TS
NT = T // P
HALF = P // 2
NC_ = 1 + NB
EPS = 1e-6
COLS = ((0, 512), (512, 512), (1024, 128))
TB = 1536
CW = T // 3

H, HD, N = 32, 64, 128
G, R = 8, 4
INNER, CONV = H * HD, H * HD + 2 * G * N
TAPS = 4
NKV, QH, DH = 4, 4, 64
ATTN, KV = NKV * QH * DH, NKV * DH
PAST, CHUNK, N_KEYS = 128, 64, 128
PH, TOPK = 8, 16
HK = PH * TOPK
MZ, MG, MQ, MK, MX = INNER // P, 2 * D // P, ATTN // P, KV // P, CONV // P
TZ, TG, TQ = 0, MZ, MZ + MG
TK = TQ + MQ
NPLAIN = TK + MK
NEG = -1e30

F32 = mybir.dt.float32
F32R = mybir.dt.float32r
U32 = mybir.dt.uint32
ALU = mybir.AluOpType
ACT = mybir.ActivationFunctionType
AX = mybir.AxisListType
ds = bass.ds
START = 1

C_ID, C_ONE, C_TRI, C_STRI, C_NEG, C_AM, C_IOTA, C_BM = 0, 128, 256, 512, 768, 1024, 1280, 1408
C_N = C_BM + NB


class Steps:

    def __init__(self, eng, sem, per_turn=0, turn=0, before=0):
        self.eng, self.sem, self.per_turn, self.turn = eng, sem, per_turn, turn
        self.before = self.n = before

    def step(self, ins):
        ins.then_inc(self.sem, 1)
        self.n += 1

    def wait(self):
        self.eng.wait_ge(self.sem, self.turn * self.per_turn + self.n + START)

    def link(self, ins):
        self.step(ins)
        self.wait()

    def close(self):
        assert self.n - self.before == self.per_turn, (self.n - self.before, self.per_turn)


def open_(nc, ctx):
    held = []

    def clear():
        if held:
            nc.clear_and_free_semaphores(held)
            nc.all_engine_barrier()
    ctx.callback(clear)

    def sb(name, shape, dt=F32):
        return ctx.enter_context(nc.sbuf_tensor(name, shape, dt))

    def pb(name, shape):
        return ctx.enter_context(nc.psum_tensor(name, shape, F32))

    def sem(name, n=None):
        got = [nc.alloc_semaphore(name if n is None else f"{name}{i}") for i in range(n or 1)]
        held.extend(got)
        for s in got:
            nc.gpsimd.sem_inc(s, START)
        return got[0] if n is None else got
    return sb, pb, sem


def begin(nc, ctx):
    nc.all_engine_barrier()
    return ctx.enter_context(nc.Block())


def phase_modulation(nc, io, per):
    M = 2 * KD
    MB = 4
    with ExitStack() as ctx:
        sb, pb, sem = open_(nc, ctx)
        c = sb("cond", [P, KD, NC_])
        cs, bias, g1 = per["cond"], per["ada_b"], per["norm_g"]
        w = sb("ada_ring", [P, 2, MB, KD, P])
        raw = sb("mod_raw", [P, M, NC_])
        ps = pb("mod_psum", [P, 2, 512])
        consts_in, small_in, c_silu = sem("mod_consts_in"), sem("mod_small_in"), sem("mod_c_silu")
        w_in, mm, copied = sem("mod_w_in", 2), sem("mod_mm", 2), sem("mod_copied", 2)
        added = sem("mod_added")
        block = begin(nc, ctx)

        @block.sync
        def _(sp):
            sp.dma_start(c[:], io["c"][:]).then_inc(small_in, 16)
            sp.dma_start(bias[:], io["ada_b"][:]).then_inc(small_in, 16)
            sp.dma_start(g1[:], io["norm_g"][:]).then_inc(small_in, 16)
            sp.dma_start(per["const"][:], io["const"][:]).then_inc(consts_in, 16)
            with sp.Fori(0, M // MB // 2) as i:
                for s in range(2):
                    sp.wait_ge(mm[s], i + START)
                    sp.dma_start(w[:, s], io["ada_w"][ds((i * 2 + s) * MB, MB)].rearrange("m p k c -> p m (k c)")).then_inc(w_in[s], 16)
            sp.wait_ge(consts_in, 16 + START)

        @block.scalar
        def _(act):
            act.wait_ge(small_in, 48 + START)
            nc.scalar.activation(cs[:], c[:], ACT.Silu).then_inc(c_silu, 1)

        @block.tensor
        def _(pe):
            pe.wait_ge(c_silu, 1 + START)
            with pe.Fori(0, M // MB // 2) as i:
                for s in range(2):
                    pe.wait_ge(w_in[s], i * 16 + 16 + START)
                    pe.wait_ge(copied[s], i + START)
                    for m in range(MB):
                        for k in range(KD):
                            last = nc.tensor.matmul(ps[:, s, m * NC_:(m + 1) * NC_], w[:, s, m, k], cs[:, k], start=(k == 0), stop=(k == KD - 1))
                    last.then_inc(mm[s], 1)

        @block.vector
        def _(dve):
            with dve.Fori(0, M // MB // 2) as i:
                for s in range(2):
                    dve.wait_ge(mm[s], i + 1 + START)
                    nc.vector.tensor_copy(raw[:, ds((i * 2 + s) * MB, MB)].rearrange("p m c -> p (m c)"), ps[:, s, 0:MB * NC_]).then_inc(copied[s], 1)
            for s in range(2):
                dve.wait_ge(copied[s], M // MB // 2 + START)
            dve.wait_ge(small_in, 48 + START)
            finish_modulation(nc, dve, per, raw, 0, M, added)


def finish_modulation(nc, dve, per, raw, first, end, added):
    mod, n = per["mod"], end - first
    nc.vector.tensor_tensor(mod[:, first:end], raw[:], per["ada_b"][:, first:end].unsqueeze(2).to_broadcast([P, n, NC_]), ALU.add).then_inc(added, 1)
    dve.wait_ge(added, 1 + START)
    for which, at in ((0, KD), (1, 4 * KD)):
        if first <= at < end:
            nc.vector.scalar_tensor_tensor(out=per["gain"][:, which], in0=mod[:, at:at + KD], scalar=1.0,
                                           in1=per["norm_g"][:, which].unsqueeze(2).to_broadcast([P, KD, NC_]), op0=ALU.add, op1=ALU.mult)


def per_token(v, k):
    return v[:, k, 1:NC_].unsqueeze(2).to_broadcast([P, NB, TS])


def samples(x):
    return x[:, SEQ:T].rearrange("p (b t) -> p b t", t=TS)


def norm_engines(nc, block, per, x, xs_ready, xs_value, sq, ps, rstd, sems, finish):
    squared, summed, rooted, chain = sems
    ones = per["const"][:, C_ONE:C_ONE + P]

    @block.scalar
    def _(act):
        act.wait_ge(xs_ready, xs_value + START)
        for k in range(KD):
            if k >= 2:
                act.wait_ge(summed, k - 1 + START)
            nc.scalar.activation(sq[:, k % 2], x[:, k], ACT.Square).then_inc(squared, 1)
        act.wait_ge(summed, KD + START)
        nc.scalar.activation(rstd[:], ps[:, 0:T], ACT.Sqrt, bias=per["eps"][:, 0:1], scale=1.0 / D).then_inc(rooted, 1)

    @block.tensor
    def _(pe):
        for k in range(KD):
            pe.wait_ge(squared, k + 1 + START)
            for a, n in COLS:
                last = nc.tensor.matmul(ps[:, a:a + n], ones, sq[:, k % 2, a:a + n], start=(k == 0), stop=(k == KD - 1))
            last.then_inc(summed, 1)

    @block.vector
    def _(dve):
        ch = Steps(dve, chain)
        dve.wait_ge(rooted, 1 + START)
        ch.link(nc.vector.reciprocal(rstd[:], rstd[:]))
        for k in range(KD):
            finish(dve, k, ch)


def modulated(nc, per, x, rstd, hi, lo, which, shift_at, tmp, out):
    def finish(dve, k, ch):
        gain, mod = per["gain"][:, which], per["mod"]
        b = k % 2
        ch.link(nc.vector.tensor_tensor(tmp[:, b], x[:, k], rstd[:], ALU.mult))
        ch.step(nc.vector.tensor_scalar(out[:, b, 0:SEQ], tmp[:, b, 0:SEQ], gain[:, k, 0:1], mod[:, shift_at + k, 0:1], ALU.mult, ALU.add))
        ch.link(nc.vector.tensor_tensor(samples(out[:, b]), samples(tmp[:, b]), per_token(gain, k), ALU.mult))
        ch.link(nc.vector.tensor_tensor(samples(out[:, b]), samples(out[:, b]), per_token(mod[:, shift_at:shift_at + KD], k), ALU.add))
        ch.link(nc.vector.tensor_copy(hi[:, k], out[:, b]))
        ch.step(nc.vector.tensor_tensor(lo[:, k], out[:, b], hi[:, k].bitcast(F32), ALU.subtract))
    return finish


def phase_norm1(nc, io, per, hi, lo):
    with ExitStack() as ctx:
        sb, pb, sem = open_(nc, ctx)
        x = sb("n1_x", [P, KD, T])
        sq, tmp, rstd, out = sb("n1_sq", [P, 2, T]), sb("n1_tmp", [P, 2, T]), sb("n1_rstd", [P, T]), sb("n1_out", [P, 2, T])
        ps = pb("n1_ps", [P, TB])
        x_in = sem("n1_x_in")
        sems = [sem(f"n1_{n}") for n in ("squared", "summed", "rooted", "chain")]
        block = begin(nc, ctx)

        @block.sync
        def _(sp):
            sp.dma_start(x[:], io["x"][:]).then_inc(x_in, 16)
        norm_engines(nc, block, per, x, x_in, 16, sq, ps, rstd, sems, modulated(nc, per, x, rstd, hi, lo, 0, 0, tmp, out))


def banks(ps):
    return ps[:, :, 0:CW]


def cut(x):
    return x.rearrange("p (c w) -> p c w", w=CW)


SPLIT = ((0, 0), (0, 1), (1, 0))


def product3(nc, ps, w, x, kt):
    for k in range(kt):
        for a, b in SPLIT:
            for c in range(3):
                last = nc.tensor.matmul(ps[:, c, 0:CW], w[a][:, k], x[b][:, k, c * CW:(c + 1) * CW],
                                        start=(k == 0 and (a, b) == SPLIT[0]), stop=(k == kt - 1 and (a, b) == SPLIT[-1]))
    return last


def phase_projection(nc, io, per, h, scr):
    MOD, MODS = 2 * KD, 4 * KD
    runs = ((TZ, MZ, ACT.Silu), (TG, MG, ACT.Sigmoid), (TQ, MQ + MK, ACT.Copy))
    turns = NPLAIN // 2
    XT = MX // 2
    PADP, PADS = TAPS - 1 + SEQ, TAPS - 1 + TS
    with ExitStack() as ctx:
        sb, pb, sem = open_(nc, ctx)
        w = sb("pr_w", [P, 2, KD, P])
        w2 = [sb("pr_w_" + n, [P, 2, KD, P], F32R) for n in ("hi", "lo")]
        wvd2 = [sb("pr_wvd_" + n, [P, KD, KV + H], F32R) for n in ("hi", "lo")]
        o = sb("pr_out", [P, 2, T])
        raw = sb("pr_raw", [P, 2, PADP + NB * PADS])
        acc = sb("pr_acc", [P, 2, T])
        acc2 = sb("pr_acc2", [P, 2, T])
        hist = sb("pr_hist", [P, MX, NB * (TAPS - 1)])
        cw = sb("pr_convw", [P, MX, TAPS + 1])
        cwt = sb("pr_convw_tile", [P, 2, TAPS + 1])
        tail_p, tail_s = sb("pr_tail_p", [P, MX, TAPS - 1]), sb("pr_tail_s", [P, MX, NB * (TAPS - 1)])
        wvd = sb("pr_wvd", [P, KD, KV + H])
        vd = sb("pr_vd", [P, NT, KV + H])
        ps = pb("pr_ps", [P, 2, 3, 512])
        pv = pb("pr_pv", [P, 2, 512])
        wm, mod_raw = sb("pr_wmod", [P, 2, KD, P]), sb("pr_mod_raw", [P, MODS, NC_])
        wm_in, mod_mm, mod_r, mod_added = sem("pr_wmod_in", 2), sem("pr_mod_mm", 2), sem("pr_mod_r", 2), sem("pr_mod_added")
        pm = pv[:, :, KV + H:KV + H + NC_]
        small_in, wvd_in = sem("pr_small_in"), sem("pr_wvd_in")
        w_hi, w_lo, wvd_hi, wvd_lo = sem("pr_w_hi", 2), sem("pr_w_lo", 2), sem("pr_wvd_hi"), sem("pr_wvd_lo")
        w_in, mm = sem("pr_w_in", 2), sem("pr_mm", 2)
        evac, stored = sem("pr_evac", 2), sem("pr_stored", 2)
        vmm, vcopied, vstored = sem("pr_vmm"), sem("pr_vcopied"), sem("pr_vstored")
        conv_ready, silu_done, tail_done = sem("pr_conv", 2), sem("pr_silu", 2), sem("pr_tails", 2)
        kept = sem("pr_kept")
        chains = sem("pr_chain")
        block = begin(nc, ctx)

        @block.sync
        def _(sp):
            sp.dma_start(wvd[:], io["w_vdt"][:]).then_inc(wvd_in, 16)
            sp.dma_start(hist[:], io["conv_hist"][:]).then_inc(small_in, 16)
            sp.dma_start(cw[:], io["conv_w"][:]).then_inc(small_in, 16)
            def load(i, s):
                sp.wait_ge(w_lo[s], i + START)
                sp.dma_start(w[:, s], io["w_main"][ds(i * 2 + s, 1)].rearrange("m p k c -> p (m k) c")).then_inc(w_in[s], 16)

            with sp.Fori(0, MODS // 2) as i:
                for s in range(2):
                    load(i, s)
                    sp.wait_ge(mod_mm[s], i + START)
                    sp.dma_start(wm[:, s], io["ada_w"][ds(i * 2 + s + MOD, 1)].rearrange("m p k c -> p (m k) c")).then_inc(wm_in[s], 16)
            with sp.Fori(MODS // 2, turns + XT) as i:
                for s in range(2):
                    load(i, s)
            sp.wait_ge(vcopied, NT + START)
            sp.dma_start(scr["vd"][:], vd[:]).then_inc(vstored, 16)
            sp.dma_start(io["v_prompt"][:], vd[:, NT - 2, 0:KV]).then_inc(vstored, 16)
            sp.dma_start(io["v_sample"][:], vd[:, NT - 1, 0:KV]).then_inc(vstored, 16)
            for s in range(2):
                sp.wait_ge(tail_done[s], XT + START)
            sp.dma_start(io["conv_prompt"][:], tail_p[:]).then_inc(kept, 16)
            sp.dma_start(io["conv_sample"][:], tail_s[:]).then_inc(kept, 16)
            sp.wait_ge(vstored, 48 + START)
            sp.wait_ge(kept, 32 + START)

        @block.tensor
        def _(pe):
            pe.wait_ge(wvd_lo, 1 + START)
            for t in range(NT):
                if t >= 2:
                    pe.wait_ge(vcopied, t - 1 + START)
                for k in range(KD):
                    for a, b in SPLIT:
                        last = nc.tensor.matmul(pv[:, t % 2, 0:KV + H], h[a][:, k, t * P:(t + 1) * P], wvd2[b][:, k],
                                                start=(k == 0 and (a, b) == SPLIT[0]), stop=(k == KD - 1 and (a, b) == SPLIT[-1]))
                last.then_inc(vmm, 1)
            def tile(i, s):
                pe.wait_ge(w_lo[s], i + 1 + START)
                pe.wait_ge(evac[s], i + START)
                product3(nc, ps[:, s], [x[:, s] for x in w2], h, KD).then_inc(mm[s], 1)

            pe.wait_ge(vcopied, NT + START)
            with pe.Fori(0, MODS // 2) as i:
                for s in range(2):
                    tile(i, s)
                    pe.wait_ge(wm_in[s], i * 16 + 16 + START)
                    pe.wait_ge(mod_r[s], i + START)
                    for k in range(KD):
                        last = nc.tensor.matmul(pm[:, s], wm[:, s, k], per["cond"][:, k], start=(k == 0), stop=(k == KD - 1))
                    last.then_inc(mod_mm[s], 1)
            with pe.Fori(MODS // 2, turns + XT) as i:
                for s in range(2):
                    tile(i, s)

        def round_weights(act, i, s):
            act.wait_ge(w_in[s], i * 16 + 16 + START)
            act.wait_ge(mm[s], i + START)
            nc.scalar.copy(w2[0][:, s], w[:, s]).then_inc(w_hi[s], 1)

        def rest_of_weights(dve, i, s):
            dve.wait_ge(w_hi[s], i + 1 + START)
            nc.vector.tensor_tensor(w2[1][:, s], w[:, s], w2[0][:, s].bitcast(F32), ALU.subtract).then_inc(w_lo[s], 1)

        @block.scalar
        def _(act):
            act.wait_ge(wvd_in, 16 + START)
            nc.scalar.copy(wvd2[0][:], wvd[:]).then_inc(wvd_hi, 1)
            for s in range(2):
                round_weights(act, 0, s)
            for first, count, func in runs:
                f = first // 2
                with act.Fori(f, f + count // 2) as i:
                    for s in range(2):
                        act.wait_ge(mm[s], i + 1 + START)
                        act.wait_ge(stored[s], i * 16 + START)
                        nc.scalar.activation(cut(o[:, s]), banks(ps[:, s]), func).then_inc(evac[s], 1)
                        round_weights(act, i + 1, s)
                        act.wait_ge(evac[s], i + 1 + START)
                        act.dma_start(scr["plain"][ds(i * 2 + s, 1)].rearrange("m p t -> p (m t)"), o[:, s]).then_inc(stored[s], 16)

            def take_raw(i, s, more):
                act.wait_ge(mm[s], i + turns + 1 + START)
                act.wait_ge(tail_done[s], i + START)
                nc.scalar.copy(cut(raw[:, s, TAPS - 1:TAPS - 1 + 2 * CW]), ps[:, s, 0:2, 0:CW])
                nc.scalar.copy(raw[:, s, TAPS - 1 + 2 * CW:PADP], ps[:, s, 2, 0:SEQ - 2 * CW])
                nc.scalar.copy(raw[:, s, PADP:].rearrange("p (b t) -> p b t", t=PADS)[:, :, TAPS - 1:],
                               ps[:, s, 2, SEQ - 2 * CW:CW].rearrange("p (b t) -> p b t", t=TS)).then_inc(evac[s], 1)
                if more:
                    round_weights(act, i + (turns + 1), s)

            def give_xbc(i, s):
                act.wait_ge(conv_ready[s], i + 1 + START)
                act.wait_ge(stored[s], (i + turns) * 16 + START)
                nc.scalar.activation(o[:, s], acc2[:, s], ACT.Silu).then_inc(silu_done[s], 1)
                act.wait_ge(silu_done[s], i + 1 + START)
                act.dma_start(scr["xbc"][ds(i * 2 + s, 1)].rearrange("m p t -> p (m t)"), o[:, s]).then_inc(stored[s], 16)

            def conv_turn(i, more):
                take_raw(i, 1, True)
                give_xbc(i, 0)
                take_raw(i + 1, 0, more)
                give_xbc(i, 1)

            take_raw(0, 0, True)
            with act.Fori(0, XT - 2) as i:
                conv_turn(i, True)
            conv_turn(XT - 2, False)
            take_raw(XT - 1, 1, False)
            for s in range(2):
                give_xbc(XT - 1, s)
            for s in range(2):
                act.wait_ge(stored[s], (turns + XT) * 16 + START)

        @block.vector
        def _(dve):
            dve.wait_ge(wvd_hi, 1 + START)
            nc.vector.tensor_tensor(wvd2[1][:], wvd[:], wvd2[0][:].bitcast(F32), ALU.subtract).then_inc(wvd_lo, 1)
            for s in range(2):
                rest_of_weights(dve, 0, s)
            for t in range(NT):
                dve.wait_ge(vmm, t + 1 + START)
                nc.vector.tensor_copy(vd[:, t], pv[:, t % 2, 0:KV + H]).then_inc(vcopied, 1)
            Steps(dve, chains).step(nc.vector.memset(raw[:, :, 0:TAPS - 1], 0.0))
            dve.wait_ge(small_in, 32 + START)
            with dve.Fori(1, MODS // 2 + 1) as i:
                for s in range(2):
                    rest_of_weights(dve, i, s)
                    dve.wait_ge(mod_mm[s], i + START)
                    nc.vector.tensor_copy(mod_raw[:, ds(i * 2 + (s - 2), 1)].rearrange("p m c -> p (m c)"), pm[:, s]).then_inc(mod_r[s], 1)
            with dve.Fori(MODS // 2 + 1, turns + 1) as i:
                for s in range(2):
                    rest_of_weights(dve, i, s)
            for s in range(2):
                dve.wait_ge(mod_r[s], MODS // 2 + START)
            finish_modulation(nc, dve, per, mod_raw, MOD, MOD + MODS, mod_added)

            def convolve(i, more):
                ch = Steps(dve, chains, 12, i, before=1)
                for s in range(2):
                    if more:
                        rest_of_weights(dve, i + (turns + 1), s)
                    rp, rs = raw[:, s, 0:PADP], raw[:, s, PADP:].rearrange("p (b t) -> p b t", t=PADS)
                    dve.wait_ge(evac[s], i + turns + 1 + START)
                    m = i * 2 + s
                    ch.step(nc.vector.tensor_copy(rs[:, :, 0:TAPS - 1], hist[:, ds(m, 1)].rearrange("p m (b t) -> p (m b) t", t=TAPS - 1)))
                    ch.link(nc.vector.tensor_copy(cwt[:, s], cw[:, ds(m, 1)].rearrange("p m j -> p (m j)")))
                    dve.wait_ge(silu_done[s], i + START)
                    views = ((rp, lambda j: rp[:, j:j + SEQ], lambda a: a[:, s, 0:SEQ]),
                             (rs, lambda j: rs[:, :, j:j + TS], lambda a: samples(a[:, s])))
                    bufs = (acc, acc2, acc, acc2)
                    for j in range(TAPS):
                        for _, src, dst in views:
                            if j == 0:
                                ins = nc.vector.tensor_scalar(dst(bufs[0]), src(0), cwt[:, s, 0:1], cwt[:, s, TAPS:TAPS + 1], ALU.mult, ALU.add)
                            else:
                                ins = nc.vector.scalar_tensor_tensor(out=dst(bufs[j]), in0=src(j), scalar=cwt[:, s, j:j + 1], in1=dst(bufs[j - 1]), op0=ALU.mult, op1=ALU.add)
                        if j < TAPS - 1:
                            ch.link(ins)
                        else:
                            ins.then_inc(conv_ready[s], 1)
                    ch.step(nc.vector.tensor_copy(tail_p[:, ds(m, 1)].rearrange("p m t -> p (m t)"), rp[:, SEQ:PADP]))
                    nc.vector.tensor_copy(tail_s[:, ds(m, 1)].rearrange("p m (b t) -> p (m b) t", t=TAPS - 1), rs[:, :, TS:PADS]).then_inc(tail_done[s], 1)
                    ch.wait()
                ch.close()

            with dve.Fori(0, XT - 1) as i:
                convolve(i, True)
            convolve(XT - 1, False)


def phase_decay(nc, io, per, scr, vec):
    NP8 = NT - 1
    with ExitStack() as ctx:
        sb, pb, sem = open_(nc, ctx)
        raw, rows = sb("dc_raw", [P, NT, H]), sb("dc_rows", [P, 2, H])
        t1, t2 = sb("dc_t1", [P, NT, H]), sb("dc_t2", [P, NT, H])
        rate = sb("dc_rate", [P, H])
        dt, na, a, toend = (sb("dc_" + n, [P, NT, H]) for n in ("dt", "na", "a", "toend"))
        ps = pb("dc_ps", [P, 2, 512])
        loaded, chain, exped, logged, summed, ended = (sem("dc_" + n) for n in ("in", "chain", "exp", "log", "sum", "end"))
        block = begin(nc, ctx)
        tri = [per["const"][:, C_TRI + n * P:C_TRI + (n + 1) * P] for n in range(2)]
        stri = [per["const"][:, C_STRI + n * P:C_STRI + (n + 1) * P] for n in range(2)]

        @block.sync
        def _(sp):
            sp.dma_start(raw[:], scr["vd"][:, :, KV:KV + H]).then_inc(loaded, 16)
            sp.dma_start(rows[:], io["dt_rows"][:]).then_inc(loaded, 16)

        @block.vector
        def _(dve):
            v, ch = nc.vector, Steps(dve, chain)
            dve.wait_ge(loaded, 32 + START)
            ch.link(v.tensor_tensor(raw[:], raw[:], rows[:, 0].unsqueeze(1).to_broadcast([P, NT, H]), ALU.add))
            ch.link(v.tensor_scalar(t1[:], raw[:], -1.0, None, ALU.mult))
            ch.link(v.tensor_tensor(t1[:], t1[:], raw[:], ALU.min))
            dve.wait_ge(logged, 1 + START)
            ch.link(v.scalar_tensor_tensor(out=dt[:], in0=raw[:], scalar=0.0, in1=t2[:], op0=ALU.max, op1=ALU.add))
            ch.link(v.tensor_tensor(na[:], dt[:], rate[:].unsqueeze(1).to_broadcast([P, NT, H]), ALU.mult))
            ch.link(v.tensor_scalar(a[:], na[:], -1.0, None, ALU.mult))
            dve.wait_ge(ended, 1 + START)
            ch.link(v.tensor_tensor(toend[:], toend[:], dt[:], ALU.mult))
            dve.wait_ge(summed, 1 + START)
            by_group = lambda x: x[:].rearrange("p t (g r) -> p t g r", g=G)
            for n, x in ((0, a), (2, dt), (3, toend)):
                ch.link(v.tensor_copy(vec[:, :, n].rearrange("p g t r -> p t g r"), by_group(x)))
            ch.link(v.tensor_copy(vec[:, :, 1].rearrange("p g t r -> p t g r"), ps[:, 0, 0:NT * H].rearrange("p (t g r) -> p t g r", g=G, t=NT)))

        @block.scalar
        def _(act):
            act.wait_ge(loaded, 32 + START)
            nc.scalar.activation(rate[:], rows[:, 1], ACT.Exp).then_inc(exped, 1)
            act.wait_ge(chain, 3 + START)
            nc.scalar.activation(t2[:], t1[:], ACT.Exp).then_inc(exped, 1)
            act.wait_ge(exped, 2 + START)
            nc.scalar.activation(t2[:], t2[:], ACT.Ln, bias=1.0).then_inc(logged, 1)
            act.wait_ge(summed, 1 + START)
            nc.scalar.activation(toend[:], ps[:, 1, 0:NT * H].rearrange("p (t h) -> p t h", t=NT), ACT.Exp).then_inc(ended, 1)

        @block.tensor
        def _(pe):
            pe.wait_ge(chain, 6 + START)
            for b, (m, x) in enumerate(((tri, na), (stri, a))):
                nc.tensor.matmul(ps[:, b, 0:NP8 * H], m[0], x[:, 0:NP8].rearrange("p t h -> p (t h)"), start=True, stop=True)
                last = nc.tensor.matmul(ps[:, b, NP8 * H:NT * H], m[1], x[:, NP8], start=True, stop=True)
            last.then_inc(summed, 1)


def phase_ssd(nc, io, per, scr):
    with ExitStack() as ctx0:
        vec = ctx0.enter_context(nc.sbuf_tensor("decay_vec", [P, G, 4, NT, R], F32))
        phase_decay(nc, io, per, scr, vec)
        ssd_groups(nc, io, per, scr, vec)


def ssd_groups(nc, io, per, scr, vec):
    LAST = NT - 1
    CH = 18
    W = R * HD
    with ExitStack() as ctx:
        sb, pb, sem = open_(nc, ctx)
        xT, bT, cT, zT = sb("sd_xT", [P, 2, 2, T]), sb("sd_bT", [P, 2, T]), sb("sd_cT", [P, 2, T]), sb("sd_zT", [P, 2, 2, T])
        h0 = sb("sd_h0", [P, NB, W])
        hp = sb("sd_h", [P, W])
        vg = sb("sd_vec", [P, 2, 4, NT, R])
        skip, gain = sb("sd_skip", [P, G, 2]), sb("sd_gain", [P, G, 2])
        sg = sb("sd_skip_gain", [P, 2, 2, 2])
        y, sq, rs = sb("sd_y", [P, 2, 2, T]), sb("sd_sq", [P, 2, T]), sb("sd_rs", [P, T])
        xdt, xe, bk = sb("sd_xdt", [P, 2, W]), sb("sd_xe", [P, 2, W]), sb("sd_bk", [P, 2, N])
        seg, dec, ea, mt, cts = (sb("sd_" + n, [P, 2, R, P]) for n in ("seg", "dec", "ea", "mt", "cts"))
        xeb = sb("sd_xeb", [P, 2, W])
        psT = pb("sd_psT", [P, 2, 512])
        psA = pb("sd_psA", [P, 2, 512])
        psY = pb("sd_psY", [P, 2, 512])
        psR = pb("sd_psR", [P, 2, 512])
        x_in, h_in = sem("sd_in", 2), sem("sd_h_in")
        small = sem("sd_small")
        vg_ready = sem("sd_vg", 2)
        tr, cum = sem("sd_tr", 2), sem("sd_cum", 2)
        xdt_r, bk_r, seg_r, ea_r, dec_r, mt_r, cts_r = (sem("sd_" + n, 2) for n in ("xdtr", "bkr", "segr", "ear", "decr", "mtr", "ctsr"))
        y_r, s_r, y_read, h_done = (sem("sd_" + n, 2) for n in ("yr", "sr", "yread", "hdone"))
        xeb_r, sb_r, sb_done = (sem("sd_" + n, 2) for n in ("xebr", "sbr", "sbdone"))
        sq_r, var_r, root_r = (sem("sd_" + n) for n in ("sqr", "varr", "rootr"))
        y_out, y_st, hs_st, hp_st = sem("sd_yout", 2), sem("sd_yst", 2), sem("sd_hsst"), sem("sd_hpst")
        yg_r = sem("sd_yg")
        chain = sem("sd_chain")
        block = begin(nc, ctx)
        ident, ones = per["const"][:, C_ID:C_ID + P], per["const"][:, C_ONE:C_ONE + P]
        tri = [per["const"][:, C_TRI + n * P:C_TRI + (n + 1) * P] for n in range(2)]
        neg = [per["const"][:, C_NEG + n * P:C_NEG + (n + 1) * P] for n in range(2)]

        def chunk(s, c):
            k = s * NT + c
            return k % 2, k // 2, int(c == LAST), slice(c * P, (c + 1) * P)

        def previous(i, s, c):
            k = s * NT + c - 1
            return k % 2, i * (CH // 2) + k // 2 + 1

        SEMS_OF = (NB // 2, NB // 2 - 1)

        def sample_states_done(eng, i, s):
            q, u, _, _ = chunk(s, LAST)
            for e in range(2):
                eng.wait_ge(sb_done[e], (i * 2 + s + 1) * SEMS_OF[e] + START)
            eng.wait_ge(h_done[q], i * (CH // 2) + u + 1 + START)

        FINAL = (G // 2 - 1, 1)

        def over_groups(eng, group):
            group(0, 0, None)
            group(0, 1, (0, 0))
            with eng.Fori(1, G // 2) as i:
                group(i, 0, (i - 1, 1))
                group(i, 1, (i, 0))

        @block.sync
        def _(sp):
            sp.dma_start(skip[:], io["d_skip"][:]).then_inc(small, 16)
            sp.dma_start(gain[:], io["ssm_g"][:]).then_inc(small, 16)
            with sp.Fori(0, G // 2) as i:
                for s in range(2):
                    g = i * 2 + s
                    sp.wait_ge(y_out[s], i + START)
                    tile_of = lambda src, m: src[ds(m, 1)].rearrange("m p t -> p (m t)")
                    for j in range(2):
                        sp.dma_start(xT[:, s, j], tile_of(scr["xbc"], g * 2 + j)).then_inc(x_in[s], 16)
                        sp.dma_start(zT[:, s, j], tile_of(scr["plain"], g * 2 + (TZ + j))).then_inc(x_in[s], 16)
                    sp.dma_start(bT[:, s], tile_of(scr["xbc"], g + INNER // P)).then_inc(x_in[s], 16)
                    sp.dma_start(cT[:, s], tile_of(scr["xbc"], g + (INNER // P + G))).then_inc(x_in[s], 16)
                    sp.wait_ge(hs_st, g * 16 + START)
                    sp.dma_start(h0[:], io["ssm_in"][ds(g, 1)].rearrange("g n b w -> n (g b) w")).then_inc(h_in, 16)

        @block.tensor
        def _(pe):
            mm = nc.tensor.matmul

            def prepare(i, s, c):
                q, u, ms, at = chunk(s, c)
                u = i * (CH // 2) + u
                if c == 0:
                    pe.wait_ge(x_in[s], i * 96 + 96 + START)
                    pe.wait_ge(vg_ready[s], i + 1 + START)
                pe.wait_ge(xdt_r[q], u + START)
                pe.wait_ge(bk_r[q], u + START)
                pe.wait_ge(mt_r[q], u + START)
                for j in range(2):
                    nc.tensor.transpose(psT[:, q, j * P:(j + 1) * P], xT[:, s, j, at], ident)
                nc.tensor.transpose(psT[:, q, 2 * P:3 * P], bT[:, s, at], ident)
                mm(psT[:, q, 3 * P:4 * P], bT[:, s, at], cT[:, s, at], start=True, stop=True).then_inc(tr[q], 1)
                pe.wait_ge(seg_r[q], u + START)
                pe.wait_ge(ea_r[q], u + START)
                for r in range(R):
                    last = mm(psA[:, q, r * P:(r + 1) * P], vg[:, s, 0, c, r:r + 1].to_broadcast([P, P]), tri[ms], start=True, stop=True)
                last.then_inc(cum[q], 1)

            def scan(i, s, c):
                q, u, ms, at = chunk(s, c)
                u = i * (CH // 2) + u
                pe.wait_ge(mt_r[q], u + 1 + START)
                pe.wait_ge(xdt_r[q], u + 1 + START)
                pe.wait_ge(cts_r[q], u + 1 + START)
                pe.wait_ge(y_read[q], u + START)
                pe.wait_ge(h_done[q], u + START)
                if c == LAST:
                    pe.wait_ge(h_in, i * 32 + (s + 1) * 16 + START)
                elif c > 0:
                    pq, n = previous(i, s, c)
                    pe.wait_ge(h_done[pq], n + START)
                for r in range(R):
                    o = psY[HD * (r % 2):HD * (r % 2) + HD, q, (r // 2) * P:(r // 2 + 1) * P]
                    if c == LAST:
                        for b in range(NB):
                            t = slice(b * TS, (b + 1) * TS)
                            mm(o[:, t], h0[:, b, r * HD:(r + 1) * HD], cts[:, q, r, t], start=(b == 0), stop=False, skip_group_check=True)
                    elif c > 0:
                        mm(o, hp[:, r * HD:(r + 1) * HD], cts[:, q, r], start=True, stop=False)
                    last = mm(o, xdt[:, q, r * HD:(r + 1) * HD], mt[:, q, r], start=(c == 0), stop=True, skip_group_check=(c == LAST))
                last.then_inc(y_r[q], 1)
                pe.wait_ge(bk_r[q], u + 1 + START)
                if c < LAST:
                    mm(psY[:, q, 256:512], bk[:, q], xe[:, q], start=True, stop=True).then_inc(s_r[q], 1)
                    return
                for b in range(NB):
                    e, n = b % 2, b // 2
                    pe.wait_ge(xeb_r[e], i * NB + s * (NB // 2) + n + 1 + START)
                    if n == 0:
                        pe.wait_ge(root_r, i * 6 + s * 3 + START)
                    pe.wait_ge(sb_done[e], (i * 2 + s) * SEMS_OF[e] + n + START)
                    last = mm(psR[:, e, 0:W], bk[:, q], xeb[:, e], start=True, stop=True)
                    last.then_inc(s_r[q] if b == NB - 1 else sb_r[e], 1)

            def variances(i, s, first, end):
                if first == 0:
                    pe.wait_ge(sq_r, i * 2 + s + 1 + START)
                    sample_states_done(pe, i, s)
                for n in range(first, end):
                    a, w = COLS[n]
                    if n == 2:
                        pe.wait_ge(root_r, i * 6 + s * 3 + 1 + START)
                    for j in range(2):
                        last = mm(psR[:, n % 2, 0:w], ones, sq[:, j, a:a + w], start=(j == 0), stop=(j == 1))
                    last.then_inc(var_r, 1)

            def group(i, s, before):
                prepare(i, s, 0)
                for c in range(NT):
                    if c < LAST:
                        prepare(i, s, c + 1)
                    scan(i, s, c)
                    if before and c == 0:
                        variances(*before, 0, 2)
                    if before and c == 2:
                        variances(*before, 2, 3)

            over_groups(pe, group)
            variances(*FINAL, 0, 3)

        @block.scalar
        def _(act):
            def roots(i, s):
                act.wait_ge(y_out[1 - s], i + s + START)
                for n, (a, w) in enumerate(COLS):
                    act.wait_ge(var_r, i * 6 + s * 3 + n + 1 + START)
                    nc.scalar.activation(rs[:, a:a + w], psR[:, n % 2, 0:w], ACT.Sqrt, bias=per["eps"][:, 0:1], scale=1.0 / W).then_inc(root_r, 1)

            def store_y(i, s):
                act.wait_ge(y_out[s], i + 1 + START)
                act.dma_start(scr["ynorm"][ds((i * 2 + s) * 2, 2)].rearrange("m p t -> p m t"), y[:, s]).then_inc(y_st[s], 16)

            def group(i, s, before):
                for c in range(NT):
                    q, u, ms, at = chunk(s, c)
                    u = i * (CH // 2) + u
                    act.wait_ge(tr[q], u + 1 + START)
                    act.wait_ge(s_r[q], u + START)
                    act.wait_ge(xdt_r[q], u + 1 + START)
                    nc.scalar.copy(bk[:, q], psT[:, q, 2 * P:3 * P]).then_inc(bk_r[q], 1)
                    act.wait_ge(cum[q], u + 1 + START)
                    act.wait_ge(cts_r[q], u + START)
                    act.wait_ge(h_done[q], u + START)
                    act.wait_ge(seg_r[q], u + 1 + START)
                    nc.scalar.activation(ea[:, q].rearrange("p r l -> p (r l)"), psA[:, q], ACT.Exp).then_inc(ea_r[q], 1)
                    act.wait_ge(mt_r[q], u + START)
                    for r in range(R):
                        last = nc.scalar.activation(dec[:, q, r], seg[:, q, r], ACT.Exp, bias=vg[:, s, 1, c, r:r + 1])
                    last.then_inc(dec_r[q], 1)
                    if before and c == 2:
                        roots(*before)
                    if before and c == 5:
                        store_y(*before)
                act.wait_ge(yg_r, i * 2 + s + 1 + START)
                act.wait_ge(var_r, i * 6 + s * 3 + START)
                nc.scalar.activation(sq[:], y[:, s], ACT.Square).then_inc(sq_r, 1)
                sample_states_done(act, i, s)
                act.dma_start(io["ssm_sample"][ds(i * 2 + s, 1)].rearrange("g n b w -> n (g b) w"), h0[:]).then_inc(hs_st, 16)
                act.dma_start(io["ssm_prompt"][ds(i * 2 + s, 1)].rearrange("g n w -> n (g w)"), hp[:]).then_inc(hp_st, 16)

            over_groups(act, group)
            roots(*FINAL)
            store_y(*FINAL)
            for s in range(2):
                act.wait_ge(y_st[s], G // 2 * 16 + START)
            act.wait_ge(hs_st, G * 16 + START)
            act.wait_ge(hp_st, G * 16 + START)

        @block.gpsimd
        def _(pool):
            with pool.Fori(0, G // 2) as i:
                for s in range(2):
                    for c in range(NT):
                        q, u, ms, at = chunk(s, c)
                        u = i * (CH // 2) + u
                        pool.wait_ge(ea_r[q], u + 1 + START)
                        pool.wait_ge(y_r[q], u + START)
                        if c == 0:
                            pool.wait_ge(x_in[s], i * 96 + 96 + START)
                        nc.gpsimd.tensor_tensor(cts[:, q], cT[:, s, at].unsqueeze(1).to_broadcast([P, R, P]), ea[:, q], ALU.mult).then_inc(cts_r[q], 1)

        @block.vector
        def _(dve):
            v = nc.vector
            PER = 2 * (2 + (LAST - 1) + NB + 1)
            dve.wait_ge(small, 32 + START)

            def normalize(ch, i, s):
                g = i * 2 + s
                dve.wait_ge(root_r, g * 3 + 3 + START)
                ch.link(v.reciprocal(rs[:], rs[:]))
                dve.wait_ge(yg_r, g + 1 + START)
                for j in range(2):
                    ins = v.scalar_tensor_tensor(out=y[:, s, j], in0=y[:, s, j], scalar=sg[:, s, 1, j:j + 1], in1=rs[:], op0=ALU.mult, op1=ALU.mult)
                ins.then_inc(y_out[s], 1)

            def group(ch, i, s, last):
                g = i * 2 + s
                v.tensor_copy(vg[:, s].rearrange("p k t r -> p (k t r)"), vec[:, ds(g, 1)].rearrange("p g k t r -> p (g k t r)")).then_inc(vg_ready[s], 1)
                ch.link(v.tensor_copy(sg[:, s, 0], skip[:, ds(g, 1)].rearrange("p g j -> p (g j)")))
                ch.link(v.tensor_copy(sg[:, s, 1], gain[:, ds(g, 1)].rearrange("p g j -> p (g j)")))
                dve.wait_ge(vg_ready[s], i + 1 + START)
                dve.wait_ge(x_in[s], i * 96 + 96 + START)
                dve.wait_ge(y_st[s], i * 16 + START)

                def before(c):
                    q, u, ms, at = chunk(s, c)
                    u = i * (CH // 2) + u
                    scaled = lambda out, kind: v.tensor_tensor(
                        out[:, q].rearrange("p (r d) -> p r d", d=HD), psT[:, q, 0:W].rearrange("p (r d) -> p r d", d=HD),
                        vg[:, s, kind, c].unsqueeze(2).to_broadcast([P, R, HD]), ALU.mult)
                    dve.wait_ge(cum[q], u + 1 + START)
                    v.tensor_tensor(seg[:, q], psA[:, q].rearrange("p (r l) -> p r l", r=R),
                                    neg[ms].unsqueeze(1).to_broadcast([P, R, P]), ALU.add).then_inc(seg_r[q], 1)
                    dve.wait_ge(tr[q], u + 1 + START)
                    dve.wait_ge(s_r[q], u + START)
                    scaled(xdt, 2)
                    scaled(xe, 3).then_inc(xdt_r[q], 1)

                def masked(c):
                    q, u, ms, at = chunk(s, c)
                    u = i * (CH // 2) + u
                    dve.wait_ge(dec_r[q], u + 1 + START)
                    dve.wait_ge(bk_r[q], u + 1 + START)
                    dve.wait_ge(y_r[q], u + START)
                    v.tensor_tensor(mt[:, q], dec[:, q], psT[:, q, 3 * P:4 * P].unsqueeze(1).to_broadcast([P, R, P]), ALU.mult).then_inc(mt_r[q], 1)

                def after(c):
                    q, u, ms, at = chunk(s, c)
                    u = i * (CH // 2) + u
                    dve.wait_ge(y_r[q], u + 1 + START)
                    if c < LAST:
                        dve.wait_ge(s_r[q], u + 1 + START)
                    for j in range(2):
                        ins = v.scalar_tensor_tensor(out=y[:, s, j, at], in0=xT[:, s, j, at], scalar=sg[:, s, 0, j:j + 1],
                                                     in1=psY[:, q, j * P:(j + 1) * P], op0=ALU.mult, op1=ALU.add)
                    ins.then_inc(y_read[q], 1)
                    if c == 0:
                        dve.wait_ge(hp_st, g * 16 + START)
                        v.tensor_copy(hp[:], psY[:, q, 256:512]).then_inc(h_done[q], 1)
                    elif c < LAST:
                        hv = hp[:].rearrange("p (r d) -> p r d", d=HD)
                        pq, n = previous(i, s, c)
                        dve.wait_ge(h_done[pq], n + START)
                        ch.link(v.tensor_tensor(hv, hv, ea[:, q, :, P - 1:P].to_broadcast([P, R, HD]), ALU.mult))
                        v.tensor_tensor(hp[:], hp[:], psY[:, q, 256:512], ALU.add).then_inc(h_done[q], 1)
                    else:
                        dve.wait_ge(xdt_r[q], u + 1 + START)
                        dve.wait_ge(h_in, g * 16 + 16 + START)

                        def rows_of(b):
                            e, n = b % 2, b // 2
                            dve.wait_ge(sb_r[e], g * SEMS_OF[e] + n + START)
                            v.tensor_scalar(xeb[:, e], xe[:, q], per["const"][:, C_BM + b:C_BM + b + 1], None, ALU.mult).then_inc(xeb_r[e], 1)

                        def update(b):
                            e, n = b % 2, b // 2
                            hv = h0[:, b].rearrange("p (r d) -> p r d", d=HD)
                            ch.link(v.tensor_tensor(hv, hv, ea[:, q, :, b * TS + TS - 1:(b + 1) * TS].to_broadcast([P, R, HD]), ALU.mult))
                            if b < NB - 1:
                                dve.wait_ge(sb_r[e], g * SEMS_OF[e] + n + 1 + START)
                            else:
                                dve.wait_ge(s_r[q], u + 1 + START)
                            v.tensor_tensor(h0[:, b], h0[:, b], psR[:, e, 0:W], ALU.add).then_inc(h_done[q] if b == NB - 1 else sb_done[e], 1)

                        rows_of(0)
                        for b in range(NB):
                            if b < NB - 1:
                                rows_of(b + 1)
                            update(b)

                before(0)
                masked(0)
                for c in range(NT):
                    if c < LAST:
                        before(c + 1)
                    after(c)
                    if last and c == 3:
                        normalize(ch, *last)
                    if c < LAST:
                        masked(c + 1)
                q, u, _, _ = chunk(s, LAST)
                dve.wait_ge(y_read[q], i * (CH // 2) + u + 1 + START)
                v.tensor_tensor(y[:, s], y[:, s], zT[:, s], ALU.mult).then_inc(yg_r, 1)

            ch = Steps(dve, chain, PER - 1, 0)
            group(ch, 0, 0, None)
            group(ch, 0, 1, (0, 0))
            ch.close()
            with dve.Fori(1, G // 2) as i:
                ch = Steps(dve, chain, PER, i, before=-1)
                group(ch, i, 0, (i - 1, 1))
                group(ch, i, 1, (i, 0))
                ch.close()
            normalize(Steps(dve, chain, PER, G // 2, before=-1), *FINAL)


def phase_attention(nc, io, per, scr):
    SCALE = DH ** -0.5
    LAST = NT - 1
    K2 = 2 * P
    with ExitStack() as ctx:
        sb, pb, sem = open_(nc, ctx)
        qT, kT = sb("at_qT", [DH, 2, QH, T]), sb("at_kT", [DH, 2, T])
        v, vn = sb("at_v", [P, 2, NT, DH]), sb("at_vnew", [TS, 2, NB, DH])
        kc, vc = sb("at_kc", [DH, 2, NB, P]), sb("at_vc", [P, 2, NB, DH])
        sink_p, sink_s = sb("at_sink_p", [P, NKV, QH]), sb("at_sink_s", [P, NKV])
        sink = sb("at_sink", [P, 2, 2, QH])
        s_ = sb("at_s", [P, 2, QH, K2])
        pr = sb("at_p", [P, 2, QH, K2])
        pT = sb("at_pT", [P, 2, 2, QH * P])
        qs = sb("at_qs", [DH, 2, NB, QH * TS])
        mx, nm, es, den = (sb("at_" + n, [P, 2, QH]) for n in ("mx", "nm", "es", "den"))
        o = sb("at_o", [DH, 2, QH, T])
        psS = pb("at_psS", [P, 2, QH, K2])
        psT = pb("at_psT", [P, 2, QH * P])
        psO = pb("at_psO", [P, 2, QH * P])
        small, loaded, qs_r = sem("at_small"), sem("at_in", 2), sem("at_qsr", 2)
        s_r, m_r, nm_r, es_r, p_r, pn_r, pt_r, ptc_r, o_r, oc_r = (
            sem("at_" + n, 2) for n in ("sr", "mr", "nmr", "esr", "pr", "pnr", "ptr", "ptcr", "or", "ocr"))
        chain, o_st, copied = sem("at_chain"), sem("at_ost", 2), sem("at_kout")
        block = begin(nc, ctx)
        ident = per["const"][:, C_ID:C_ID + P]
        amask = per["const"][:, C_AM:C_AM + K2]
        heads = lambda x, a, n: x[ds(a, n)].rearrange("m (h d) t -> d (m h) t", d=DH)

        def tile_(s, c):
            k = s * NT + c
            return k % 2, k // 2

        def halves(c):
            return ((1, P),) if c == 0 else ((0, P), (1, P if c < LAST else TS))

        @block.sync
        def _(sp):
            sp.dma_start(sink_p[:], io["sink_prompt"][:]).then_inc(small, 16)
            sp.dma_start(sink_s[:], io["sink_sample"][:]).then_inc(small, 16)
            for n, t in (("k_prompt", NT - 2), ("k_sample", LAST)):
                sp.dma_start(io[n][:], scr["plain"][TK:TK + MK, :, t * P:(t + 1) * P]).then_inc(copied, 16)
            with sp.Fori(0, NKV // 2) as i:
                for s in range(2):
                    g = i * 2 + s
                    sp.wait_ge(o_st[s], i * 16 + START)
                    sp.dma_start(qT[:, s], heads(scr["plain"], TQ + g * 2, 2)).then_inc(loaded[s], 16)
                    sp.dma_start(kT[:, s], scr["plain"][ds(TK + i, 1)][:, s * DH:(s + 1) * DH].rearrange("m d t -> d (m t)")).then_inc(loaded[s], 16)
                    sp.dma_start(v[:, s], scr["vd"][:, :, ds(g * DH, DH)]).then_inc(loaded[s], 16)
                    sp.dma_start(vn[:, s], scr["vd"][:, LAST, ds(g * DH, DH)].rearrange("(b t) d -> t b d", t=TS)).then_inc(loaded[s], 16)
                    sp.dma_start(kc[:, s], io["k_cache"][ds(g, 1)].rearrange("g d b k -> d (g b) k")).then_inc(loaded[s], 16)
                    sp.dma_start(vc[:, s], io["v_cache"][ds(g, 1)].rearrange("g k b d -> k (g b) d")).then_inc(loaded[s], 16)
            sp.wait_ge(copied, 32 + START)

        @block.tensor
        def _(pe):
            mm = nc.tensor.matmul

            def scores(i, s, c):
                q, u = tile_(s, c)
                u = i * NT + u
                if c == 0:
                    pe.wait_ge(loaded[s], i * 96 + 96 + START)
                pe.wait_ge(m_r[q], u + START)
                if c < LAST:
                    lo = P if c == 0 else 0
                    for r in range(QH):
                        last = mm(psS[:, q, r, lo:K2], qT[:, s, r, c * P:(c + 1) * P], kT[:, s, (c - 1) * P + lo:(c + 1) * P], start=True, stop=True)
                else:
                    pe.wait_ge(qs_r[s], i + 1 + START)
                    for b in range(NB):
                        at = slice(SEQ + b * TS, SEQ + (b + 1) * TS)
                        rows, n = (slice(0, P), 2) if b % 2 == 0 else (slice(64, P), 1)
                        own = qs[:, s, b:b + n].rearrange("d b m -> d (b m)")
                        mm(psS[rows, q, b // 2, 0:P], own, kc[:, s, b], start=True, stop=True)
                        last = mm(psS[rows, q, b // 2, P:P + TS], own, kT[:, s, at], start=True, stop=True)
                last.then_inc(s_r[q], 1)

            def turned(i, s, c):
                q, u = tile_(s, c)
                u = i * NT + u
                pe.wait_ge(pn_r[q], u + 1 + START)
                k = s * NT + c
                pe.wait_ge(ptc_r[(k - 1) % 2], i * NT + (k + 1) // 2 + START)
                for h, n in halves(c):
                    for r in range(QH):
                        last = nc.tensor.transpose(psT[0:n, h, r * P:(r + 1) * P], pr[:, q, r, h * P:h * P + n], ident)
                last.then_inc(pt_r[q], 1)

            def values(i, s, c):
                q, u = tile_(s, c)
                u = i * NT + u
                pe.wait_ge(ptc_r[q], u + 1 + START)
                pe.wait_ge(oc_r[q], u + START)
                if c < LAST:
                    for h, n in halves(c):
                        last = mm(psO[0:DH, q], v[:, s, c - 1 + h], pT[:, q, h], start=(h == int(c == 0)), stop=(h == 1))
                else:
                    for b in range(NB):
                        rows = slice(b * 64, (b + 1) * 64)
                        mm(psO[0:DH, q, rows], vc[:, s, b], pT[:, q, 0, rows], start=True, stop=False)
                        last = mm(psO[0:DH, q, rows], vn[:, s, b], pT[0:TS, q, 1, rows], start=False, stop=True)
                last.then_inc(o_r[q], 1)

            with pe.Fori(0, NKV // 2) as i:
                for s in range(2):
                    scores(i, s, 0)
                    scores(i, s, 1)
                    for c in range(NT):
                        turned(i, s, c)
                        if c < LAST - 1:
                            scores(i, s, c + 2)
                        values(i, s, c)

        def columns(c):
            return slice(P, K2) if c == 0 else (slice(0, K2) if c < LAST else slice(0, P + TS))

        @block.scalar
        def _(act):
            with act.Fori(0, NKV // 2) as i:
                def exps(s, c):
                    q, u = tile_(s, c)
                    u = i * NT + u
                    ks = columns(c)
                    act.wait_ge(nm_r[q], u + 1 + START)
                    act.wait_ge(pt_r[q], u + START)
                    act.wait_ge(pn_r[q], u + START)
                    nc.scalar.activation(es[:, q], es[:, q], ACT.Exp).then_inc(es_r[q], 1)
                    for r in range(QH):
                        last = nc.scalar.activation(pr[:, q, r, ks], s_[:, q, r, ks], ACT.Exp, bias=nm[:, q, r:r + 1], scale=SCALE, accum_out=den[:, q, r:r + 1])
                    last.then_inc(p_r[q], 1)

                def turned(s, c):
                    q, u = tile_(s, c)
                    u = i * NT + u
                    act.wait_ge(pt_r[q], u + 1 + START)
                    act.wait_ge(o_r[q], u + START)
                    for h, n in halves(c):
                        last = nc.scalar.copy(pT[0:n, q, h], psT[0:n, h])
                    last.then_inc(ptc_r[q], 1)

                def outputs(s, c):
                    q, u = tile_(s, c)
                    u = i * NT + u
                    if c == 0:
                        act.wait_ge(o_st[s], i * 16 + START)
                    act.wait_ge(o_r[q], u + 1 + START)
                    src = psO[0:DH, q]
                    if c < LAST:
                        ins = nc.scalar.copy(o[:, s, :, c * P:(c + 1) * P], src.rearrange("d (r t) -> d r t", r=QH))
                    else:
                        ins = nc.scalar.copy(o[:, s, :, SEQ:T].rearrange("d r (b t) -> d r b t", t=TS), src.rearrange("d (b r t) -> d r b t", r=QH, t=TS))
                    ins.then_inc(oc_r[q], 1)

                for s in range(2):
                    act.wait_ge(loaded[s], i * 96 + 96 + START)
                    nc.scalar.copy(qs[:, s].rearrange("d b (r t) -> d r b t", r=QH), qT[:, s, :, SEQ:T].rearrange("d r (b t) -> d r b t", t=TS)).then_inc(qs_r[s], 1)
                    exps(s, 0)
                    for c in range(NT):
                        turned(s, c)
                        if c < LAST:
                            exps(s, c + 1)
                        outputs(s, c)
                    for e in range(2):
                        k = s * NT + LAST - e
                        act.wait_ge(oc_r[k % 2], i * NT + k // 2 + 1 + START)
                    act.dma_start(heads(scr["attn"], (i * 2 + s) * 2, 2), o[:, s]).then_inc(o_st[s], 16)
            for s in range(2):
                act.wait_ge(o_st[s], NKV // 2 * 16 + START)

        @block.vector
        def _(dve):
            vv = nc.vector
            dve.wait_ge(small, 32 + START)
            with dve.Fori(0, NKV // 2) as i:
                ch = Steps(dve, chain, 2 * (2 + 4 * NT), i)
                for s in range(2):
                    g = i * 2 + s
                    ch.step(vv.tensor_copy(sink[:, s, 0], sink_p[:, ds(g, 1)].rearrange("p g r -> p (g r)")))
                    ch.link(vv.tensor_copy(sink[:, s, 1], sink_s[:, ds(g, 1)].to_broadcast([P, QH])))

                    def maxima(c):
                        q, u = tile_(s, c)
                        u = i * NT + u
                        ks = columns(c)
                        n = ks.stop - ks.start
                        dve.wait_ge(s_r[q], u + 1 + START)
                        dve.wait_ge(p_r[q], u + START)
                        if c < LAST:
                            ins = vv.tensor_tensor(s_[:, q, :, ks], psS[:, q, :, ks], amask[:, ks].unsqueeze(1).to_broadcast([P, QH, n]), ALU.add)
                        else:
                            ins = vv.tensor_copy(s_[:, q, :, ks], psS[:, q, :, ks])
                        ins.then_inc(m_r[q], 1)
                        dve.wait_ge(m_r[q], u + 1 + START)
                        ch.link(vv.tensor_reduce(mx[:, q], s_[:, q, :, ks], AX.X, ALU.max))
                        sk = sink[:, s, int(c == LAST)]
                        ch.link(vv.scalar_tensor_tensor(out=mx[:, q], in0=mx[:, q], scalar=SCALE, in1=sk, op0=ALU.mult, op1=ALU.max))
                        vv.tensor_tensor(es[:, q], sk, mx[:, q], ALU.subtract)
                        vv.tensor_scalar(nm[:, q], mx[:, q], -1.0, None, ALU.mult).then_inc(nm_r[q], 1)

                    def normalize(c):
                        q, u = tile_(s, c)
                        u = i * NT + u
                        ks = columns(c)
                        n = ks.stop - ks.start
                        dve.wait_ge(p_r[q], u + 1 + START)
                        dve.wait_ge(es_r[q], u + 1 + START)
                        ch.link(vv.tensor_tensor(den[:, q], den[:, q], es[:, q], ALU.add))
                        ch.link(vv.reciprocal(den[:, q], den[:, q]))
                        vv.tensor_tensor(pr[:, q, :, ks], pr[:, q, :, ks], den[:, q].unsqueeze(2).to_broadcast([P, QH, n]), ALU.mult).then_inc(pn_r[q], 1)

                    maxima(0)
                    maxima(1)
                    for c in range(NT):
                        normalize(c)
                        if c < LAST - 1:
                            maxima(c + 2)
                ch.close()


def load_tiles(sp, dst, src, n, loaded):
    for k in range(n):
        sp.dma_start(dst[:, k], src[k]).then_inc(loaded, 16)


def phase_split_product(nc, io, per, name, src, weights, kt, extras, scale, dst):
    with ExitStack() as ctx:
        sb, pb, sem = open_(nc, ctx)
        x = [sb(f"{name}_x_{n}", [P, kt, T], F32R) for n in ("hi", "lo")]
        w = [sb(f"{name}_w_{n}", [P, 2, kt, P], F32R) for n in ("hi", "lo")]
        w_new = sb(f"{name}_w_new", [P, kt, P])
        ex = sb(f"{name}_extras", [P, len(extras), T])
        out = sb(f"{name}_out", [P, 2, T])
        g1 = sb(f"{name}_gate", [P, 2, NC_])
        ps = pb(f"{name}_ps", [P, 2, 3, 512])
        x_in, x_hi, x_lo = sem(f"{name}_x_in", 2), sem(f"{name}_x_hi"), sem(f"{name}_x_lo")
        w_in, w_hi, w_lo, mm, ex_in, scaled, done, stored, gate_r = (
            sem(f"{name}_{n}", 2) for n in ("w_in", "w_hi", "w_lo", "mm", "ex_in", "scaled", "done", "stored", "gate_r"))
        adds = scale == "modulation" or len(extras) > 1
        if not adds:
            done = scaled
        block = begin(nc, ctx)

        @block.sync
        def _(sp):
            def load_weights(i, s):
                sp.wait_ge(w_lo[1 - s], i + s + START)
                sp.dma_start(w_new[:], weights[ds(i * 2 + s, 1)].rearrange("m p k c -> p (m k) c")).then_inc(w_in[s], 16)

            def load_extras(i, s):
                sp.wait_ge(done[1 - s], i + s + START)
                for n, tile in enumerate(extras):
                    sp.dma_start(ex[:, n], tile(i * 2 + s)).then_inc(ex_in[s], 16)

            load_weights(0, 0)
            for k in range(kt):
                if k >= 2:
                    sp.wait_ge(x_lo, k - 1 + START)
                sp.dma_start(out[:, k % 2], src[k]).then_inc(x_in[k % 2], 16)
            load_weights(0, 1)
            with sp.Fori(0, KD // 2 - 1) as i:
                for s in range(2):
                    load_extras(i, s)
                    load_weights(i + 1, s)
            for s in range(2):
                load_extras(KD // 2 - 1, s)

        @block.scalar
        def _(act):
            def high_weights(i, s):
                act.wait_ge(w_in[s], i * 16 + 16 + START)
                act.wait_ge(mm[s], i + START)
                nc.scalar.copy(w[0][:, s], w_new[:]).then_inc(w_hi[s], 1)

            def store(i, s):
                act.wait_ge(done[s], i + 1 + START)
                act.dma_start(dst[ds(i * 2 + s, 1)].rearrange("m p t -> p (m t)"), out[:, s]).then_inc(stored[s], 16)

            high_weights(0, 0)
            for k in range(kt):
                act.wait_ge(x_in[k % 2], k // 2 * 16 + 16 + START)
                nc.scalar.copy(x[0][:, k], out[:, k % 2]).then_inc(x_hi, 1)
            high_weights(0, 1)
            with act.Fori(0, KD // 2 - 1) as i:
                for s in range(2):
                    high_weights(i + 1, s)
                    store(i, s)
            for s in range(2):
                store(KD // 2 - 1, s)
            for s in range(2):
                act.wait_ge(stored[s], KD // 2 * 16 + START)

        @block.tensor
        def _(pe):
            for k in range(kt):
                if k == 0:
                    pe.wait_ge(w_lo[0], 1 + START)
                pe.wait_ge(x_lo, k + 1 + START)
                for a, b in SPLIT:
                    for c in range(3):
                        last = nc.tensor.matmul(ps[:, 0, c, 0:CW], w[a][:, 0, k], x[b][:, k, c * CW:(c + 1) * CW],
                                                start=(k == 0 and (a, b) == SPLIT[0]), stop=(k == kt - 1 and (a, b) == SPLIT[-1]))
            last.then_inc(mm[0], 1)

            def tile(i, s):
                pe.wait_ge(w_lo[s], i + 1 + START)
                pe.wait_ge(scaled[s], i + START)
                product3(nc, ps[:, s], [y[:, s] for y in w], x, kt).then_inc(mm[s], 1)

            tile(0, 1)
            with pe.Fori(1, KD // 2) as i:
                for s in range(2):
                    tile(i, s)

        @block.vector
        def _(dve):
            v = nc.vector

            def low_weights(i, s):
                dve.wait_ge(w_hi[s], i + 1 + START)
                v.tensor_tensor(w[1][:, s], w_new[:], w[0][:, s].bitcast(F32), ALU.subtract).then_inc(w_lo[s], 1)

            def finish(i, s):
                m = i * 2 + s
                if scale == "modulation":
                    v.tensor_copy(g1[:, s], per["mod"][:, ds(m + 2 * KD, 1)].rearrange("p m c -> p (m c)")).then_inc(gate_r[s], 1)
                    dve.wait_ge(gate_r[s], i + 1 + START)
                dve.wait_ge(stored[s], i * 16 + START)
                dve.wait_ge(ex_in[s], (i + 1) * 16 * len(extras) + START)
                dve.wait_ge(mm[s], i + 1 + START)
                if scale == "modulation":
                    v.tensor_scalar(cut(out[:, s, 0:2 * CW]), ps[:, s, 0:2, 0:CW], g1[:, s, 0:1], None, ALU.mult)
                    v.tensor_scalar(out[:, s, 2 * CW:SEQ], ps[:, s, 2, 0:SEQ - 2 * CW], g1[:, s, 0:1], None, ALU.mult)
                    v.tensor_tensor(samples(out[:, s]), ps[:, s, 2, SEQ - 2 * CW:CW].rearrange("p (b t) -> p b t", t=TS),
                                    g1[:, s, 1:NC_].unsqueeze(2).to_broadcast([P, NB, TS]), ALU.mult).then_inc(scaled[s], 1)
                else:
                    v.tensor_tensor(cut(out[:, s]), banks(ps[:, s]), cut(ex[:, 0]), ALU.mult).then_inc(scaled[s], 1)
                if adds:
                    dve.wait_ge(scaled[s], i + 1 + START)
                    v.tensor_tensor(out[:, s], out[:, s], ex[:, len(extras) - 1], ALU.add).then_inc(done[s], 1)

            low_weights(0, 0)
            for k in range(kt):
                dve.wait_ge(x_hi, k + 1 + START)
                v.tensor_tensor(x[1][:, k], out[:, k % 2], x[0][:, k].bitcast(F32), ALU.subtract).then_inc(x_lo, 1)
            low_weights(0, 1)
            with dve.Fori(0, KD // 2 - 1) as i:
                for s in range(2):
                    low_weights(i + 1, s)
                    finish(i, s)
            for s in range(2):
                finish(KD // 2 - 1, s)


def phase_merge(nc, io, per, scr):
    tile_of = lambda array, first: lambda m: array[ds(m + first, 1)].rearrange("m p t -> p (m t)")
    phase_split_product(nc, io, per, "ms", scr["ynorm"], io["w_ssm"], INNER // P, [tile_of(scr["plain"], TG)], "gate", scr["branch"])
    phase_split_product(nc, io, per, "ma", scr["attn"], io["w_attn"], ATTN // P, [tile_of(scr["plain"], TG + KD), tile_of(scr["branch"], 0)], "gate", scr["merged"])


def phase_out(nc, io, per, scr):
    x_tile = lambda m: io["x"][:, ds(m, 1)].rearrange("p m t -> p (m t)")
    phase_split_product(nc, io, per, "ou", scr["merged"], io["w_out"], KD, [x_tile], "modulation", scr["x1"])


def phase_peer(nc, io, per, scr):
    with ExitStack() as ctx:
        h2 = [ctx.enter_context(nc.sbuf_tensor("h2_" + n, [P, KD, T], F32R)) for n in ("hi", "lo")]
        with ExitStack() as ctx2:
            picks = ctx2.enter_context(nc.sbuf_tensor("picks", [P, 3, T], F32))
            phase_norm2(nc, io, per, scr, h2)
            phase_picks(nc, io, per, h2, picks)
            phase_gates(nc, io, per, scr, picks)
        phase_experts(nc, io, per, scr, h2)


def phase_norm2(nc, io, per, scr, h2):
    with ExitStack() as ctx:
        sb, pb, sem = open_(nc, ctx)
        x = sb("n2_x", [P, KD, T])
        sq, tmp, rstd, out = sb("n2_sq", [P, 2, T]), sb("n2_tmp", [P, 2, T]), sb("n2_rstd", [P, T]), sb("n2_out", [P, 2, T])
        ps = pb("n2_ps", [P, TB])
        x_in = sem("n2_x_in")
        sems = [sem(f"n2_{n}") for n in ("squared", "summed", "rooted", "chain")]
        block = begin(nc, ctx)

        @block.sync
        def _(sp):
            load_tiles(sp, x, scr["x1"], KD, x_in)
        norm_engines(nc, block, per, x, x_in, KD * 16, sq, ps, rstd, sems, modulated(nc, per, x, rstd, h2[0], h2[1], 1, 3 * KD, tmp, out))


def top16(v, ch, vals, idx, spare, src, turns):
    for t in turns:
        ch.step(v.max(vals[:, t, 0:8], src[:, t]))
    ch.wait()
    for t in turns:
        ch.step(v.max_index(idx[:, t, 0:8], vals[:, t, 0:8], src[:, t]))
        ch.step(v.match_replace(spare[:, t], vals[:, t, 0:8], src[:, t], NEG))
    ch.wait()
    for t in turns:
        ch.step(v.max(vals[:, t, 8:16], spare[:, t]))
    ch.wait()
    for t in turns:
        ch.step(v.max_index(idx[:, t, 8:16], vals[:, t, 8:16], spare[:, t]))
    ch.wait()


def phase_picks(nc, io, per, h2, picks):
    KK = TOPK * TOPK
    HALVES = 2
    with ExitStack() as ctx:
        sb, pb, sem = open_(nc, ctx)
        w, keys = sb("pk_w", [P, HALVES, KD, P]), sb("pk_keys", [P, HALVES, N_KEYS])
        w2 = [sb("pk_w_" + n, [P, HALVES, KD, P], F32R) for n in ("hi", "lo")]
        q, score = sb("pk_q", [P, HALVES, T]), sb("pk_score", [P, HALVES, NT, N_KEYS])
        val, idx = sb("pk_val", [P, HALVES, NT, TOPK]), sb("pk_idx", [P, HALVES, NT, TOPK], U32)
        idx_f = sb("pk_idx_f", [P, HALVES, NT, TOPK])
        spare = sb("pk_spare", [P, NT, KK])
        comb, hot = sb("pk_comb", [P, NT, KK]), sb("pk_hot", [P, NT, TOPK, TOPK])
        best, best_at = sb("pk_best", [P, NT, TOPK]), sb("pk_best_at", [P, NT, TOPK], U32)
        place_u, place = sb("pk_place_u", [P, HALVES, NT, TOPK], U32), sb("pk_place", [P, HALVES, NT, TOPK])
        out = sb("pk_out", [P, 3, NT, PH, TOPK])
        den = sb("pk_den", [P, NT * PH])
        ps, pst = pb("pk_ps", [P, HALVES, 3, 512]), pb("pk_pst", [P, 2, 512])
        w_in, k_in, w_hi, w_lo, mm, q_r, sc_mm, sc_r, done = (sem("pk_" + n, HALVES) for n in ("win", "kin", "whi", "wlo", "mm", "qr", "scmm", "scr", "done"))
        chain, e_in, e_out, out_r = (sem("pk_" + n) for n in ("chain", "ein", "eout", "outr"))
        tr, copied = sem("pk_tr", 2), sem("pk_copied", 2)
        block = begin(nc, ctx)
        ident = per["const"][:, C_ID:C_ID + P]
        iota = per["const"][:, C_IOTA:C_IOTA + TOPK]

        @block.sync
        def _(sp):
            with sp.Fori(0, PH) as i:
                for s in range(HALVES):
                    sp.wait_ge(w_lo[s], i + START)
                    sp.dma_start(w[:, s], io["w_query"][ds(i * 2 + s, 1)].rearrange("m p k c -> p (m k) c")).then_inc(w_in[s], 16)
                    sp.wait_ge(sc_mm[s], i + START)
                    sp.dma_start(keys[:, s], io["keys"][ds(i * 2 + s, 1)].rearrange("m d k -> d (m k)")).then_inc(k_in[s], 16)

        @block.tensor
        def _(pe):
            def queries(n, s):
                pe.wait_ge(w_lo[s], n + 1 + START)
                pe.wait_ge(sc_r[s], n + START)
                product3(nc, ps[:, s], [x[:, s] for x in w2], h2, KD).then_inc(mm[s], 1)

            def scores(n, s):
                pe.wait_ge(q_r[s], n + 1 + START)
                pe.wait_ge(k_in[s], n * 16 + 16 + START)
                for t in range(NT):
                    last = nc.tensor.matmul(ps[:, s, t // 3, t % 3 * P:(t % 3 + 1) * P], q[:, s, t * P:(t + 1) * P], keys[:, s], start=True, stop=True)
                last.then_inc(sc_mm[s], 1)

            queries(0, 0)
            with pe.Fori(0, PH - 1) as i:
                queries(i, 1)
                scores(i, 0)
                queries(i + 1, 0)
                scores(i, 1)
            queries(PH - 1, 1)
            scores(PH - 1, 0)
            scores(PH - 1, 1)
            pe.wait_ge(out_r, 1 + START)
            for t in range(NT):
                if t >= 2:
                    pe.wait_ge(copied[t % 2], t // 2 + START)
                for n in range(3):
                    last = nc.tensor.transpose(pst[:, t % 2, n * P:(n + 1) * P], out[:, n, t].rearrange("p h k -> p (h k)"), ident)
                last.then_inc(tr[t % 2], 1)

        @block.scalar
        def _(act):
            def round_weights(n, s):
                act.wait_ge(w_in[s], n * 16 + 16 + START)
                act.wait_ge(mm[s], n + START)
                nc.scalar.copy(w2[0][:, s], w[:, s]).then_inc(w_hi[s], 1)

            def take_queries(n, s):
                act.wait_ge(mm[s], n + 1 + START)
                act.wait_ge(sc_mm[s], n + START)
                nc.scalar.copy(cut(q[:, s]), banks(ps[:, s])).then_inc(q_r[s], 1)

            def take_scores(n, s):
                act.wait_ge(sc_mm[s], n + 1 + START)
                act.wait_ge(done[s], n + START)
                nc.scalar.copy(cut(score[:, s].rearrange("p t k -> p (t k)")), banks(ps[:, s])).then_inc(sc_r[s], 1)

            for s in range(HALVES):
                round_weights(0, s)
            take_queries(0, 0)
            round_weights(1, 0)
            with act.Fori(0, PH - 2) as i:
                take_queries(i, 1)
                round_weights(i + 1, 1)
                take_scores(i, 0)
                take_queries(i + 1, 0)
                round_weights(i + 2, 0)
                take_scores(i, 1)
            take_queries(PH - 2, 1)
            round_weights(PH - 1, 1)
            take_scores(PH - 2, 0)
            take_queries(PH - 1, 0)
            take_scores(PH - 2, 1)
            take_queries(PH - 1, 1)
            for s in range(HALVES):
                take_scores(PH - 1, s)
            act.wait_ge(e_in, 1 + START)
            nc.scalar.activation(out[:, 2], out[:, 2], ACT.Exp).then_inc(e_out, 1)
            for t in range(NT):
                act.wait_ge(tr[t % 2], t // 2 + 1 + START)
                nc.scalar.copy(picks[:, :, t * P:(t + 1) * P], pst[:, t % 2, 0:3 * P].rearrange("p (n t) -> p n t", n=3)).then_inc(copied[t % 2], 1)

        @block.vector
        def _(dve):
            v = nc.vector
            wide = lambda x: x.to_broadcast([P, NT, TOPK, TOPK])

            def rest_of_weights(n, s):
                dve.wait_ge(w_hi[s], n + 1 + START)
                v.tensor_tensor(w2[1][:, s], w[:, s], w2[0][:, s].bitcast(F32), ALU.subtract).then_inc(w_lo[s], 1)

            def best_of_half(ch, i, s):
                dve.wait_ge(sc_r[s], i + 1 + START)
                ch.link(v.memset(spare[:, 0, 0:1], NEG))
                top16(v, ch, val[:, s], idx[:, s], spare[:, :, 0:N_KEYS], score[:, s], range(NT))

            def keep_keys(i, s):
                v.tensor_copy(idx_f[:, s], idx[:, s]).then_inc(done[s], 1)
                dve.wait_ge(done[s], i + 1 + START)

            def best_sums(ch, i):
                ch.link(v.tensor_tensor(comb[:].rearrange("p t (a b) -> p t a b", a=TOPK), wide(val[:, 0].unsqueeze(3)), wide(val[:, 1].unsqueeze(2)), ALU.add))
                top16(v, ch, best, best_at, spare, comb, range(NT))

            def keys_of_best(ch, i):
                ch.step(v.tensor_copy(out[:, 2, :, ds(i, 1)].rearrange("p t h k -> p t (h k)"), best[:]))
                ch.step(v.tensor_scalar(place_u[:, 0], best_at[:], 4, None, ALU.logical_shift_right))
                ch.link(v.tensor_scalar(place_u[:, 1], best_at[:], TOPK - 1, None, ALU.bitwise_and))
                ch.link(v.tensor_copy(place[:], place_u[:]))
                for n in range(HALVES):
                    ch.link(v.tensor_tensor(hot[:], wide(place[:, n].unsqueeze(3)), wide(iota.unsqueeze(1).unsqueeze(1)), ALU.is_equal))
                    ch.link(v.tensor_tensor(hot[:], hot[:], wide(idx_f[:, n].unsqueeze(2)), ALU.mult))
                    ch.link(v.tensor_reduce(out[:, n, :, ds(i, 1)].rearrange("p t h k -> p t (h k)"), hot[:], AX.X, ALU.add))

            def head(i, before, more):
                ch = Steps(dve, chain)
                if before is not None:
                    best_sums(ch, before)
                if more:
                    rest_of_weights(i + 1, 0)
                best_of_half(ch, i, 0)
                if before is not None:
                    keys_of_best(ch, before)
                keep_keys(i, 0)
                if more:
                    rest_of_weights(i + 1, 1)
                best_of_half(ch, i, 1)
                keep_keys(i, 1)
                ch.link(v.memset(spare[:, 0, 0:1], NEG))
                dve.sem_clear(chain)
                dve.sem_inc(chain, START)

            for s in range(HALVES):
                rest_of_weights(0, s)
            head(0, None, True)
            with dve.Fori(1, PH - 1) as i:
                head(i, i - 1, True)
            head(PH - 1, PH - 2, False)
            ch = Steps(dve, chain)
            best_sums(ch, PH - 1)
            keys_of_best(ch, PH - 1)
            sums = out[:, 2].rearrange("p t h k -> p (t h) k")
            ch.link(v.tensor_copy(den[:], sums[:, :, 0:1].rearrange("p m k -> p (m k)")))
            v.tensor_tensor(sums, sums, den[:].unsqueeze(2).to_broadcast([P, NT * PH, TOPK]), ALU.subtract).then_inc(e_in, 1)
            dve.wait_ge(e_out, 1 + START)
            ch.link(v.tensor_reduce(den[:], sums, AX.X, ALU.add))
            ch.link(v.reciprocal(den[:], den[:]))
            v.tensor_tensor(sums, sums, den[:].unsqueeze(2).to_broadcast([P, NT * PH, TOPK]), ALU.mult).then_inc(out_r, 1)


def phase_gates(nc, io, per, scr, picks):
    B = 8
    ON_ACT = 5
    NBAT = P // B
    S = 4
    US, UP = NBAT // S, NBAT // 2
    with ExitStack() as ctx:
        sb, pb, sem = open_(nc, ctx)
        cur = sb("gt_cur", [P, 2, 3, HALF])
        one1, one2 = sb("gt_one1", [P, S, B, P]), sb("gt_one2", [P, S, B, P])
        stage = sb("gt_stage", [P, 2, N_KEYS, HALF])
        ps = pb("gt_ps", [P, 2, B * P])
        cur_r, stored, ev = sem("gt_cur_r", 2), sem("gt_stored", 2), sem("gt_ev", 2)
        hot_r, weighed, weighed_too, mm = (sem("gt_" + n, S) for n in ("hot", "weighed", "weighed_too", "mm"))
        block = begin(nc, ctx)
        iota = per["const"][:, C_IOTA:C_IOTA + P]

        def batch(j):
            return j % S, j // S, j // (NBAT // 2), j % (NBAT // 2) * B

        @block.vector
        def _(dve):
            v = nc.vector
            with dve.Fori(0, NT) as t:
                for j in range(NBAT):
                    s, u, h, at = batch(j)
                    u = t * US + u
                    dve.wait_ge(mm[s], u + START)
                    if at == 0:
                        for e in range(S):
                            dve.wait_ge(mm[e], t * US + h * (US // 2) + START)
                        v.tensor_copy(cur[:, h], picks[:, :, ds(t * P + h * HALF, HALF)]).then_inc(cur_r[h], 1)
                        dve.wait_ge(cur_r[h], t + 1 + START)
                    keys = lambda n, c: (iota.unsqueeze(1).to_broadcast([P, c, P]), cur[:, h, n, at:at + c].unsqueeze(2).to_broadcast([P, c, P]))
                    v.tensor_tensor(one2[:, s, 0:ON_ACT], *keys(1, ON_ACT), ALU.is_equal).then_inc(hot_r[s], 1)
                    v.tensor_tensor(one1[:, s], *keys(0, B), ALU.is_equal)
                    for b in range(ON_ACT, B):
                        last = v.tensor_scalar(one2[:, s, b], iota, cur[:, h, 1, at + b:at + b + 1], cur[:, h, 2, at + b:at + b + 1], ALU.is_equal, ALU.mult)
                    last.then_inc(weighed_too[s], 1)

        @block.tensor
        def _(pe):
            with pe.Fori(0, NT * NBAT // S) as i:
                for s in range(S):
                    pe.wait_ge(weighed[s], i + 1 + START)
                    pe.wait_ge(weighed_too[s], i + 1 + START)
                    pe.wait_ge(ev[s % 2], i * (S // 2) + s // 2 + START)
                    for b in range(B):
                        last = nc.tensor.matmul(ps[:, s % 2, b * P:(b + 1) * P], one1[:, s, b], one2[:, s, b], start=True, stop=True)
                    last.then_inc(mm[s], 1)

        @block.scalar
        def _(act):
            def weigh(t, j):
                s, u, h, at = batch(j)
                act.wait_ge(hot_r[s], t * US + u + 1 + START)
                for b in range(ON_ACT):
                    last = nc.scalar.activation(one2[:, s, b], one2[:, s, b], ACT.Copy, scale=cur[:, h, 2, at + b:at + b + 1])
                last.then_inc(weighed[s], 1)

            def evacuate(t, j):
                s, u, h, at = batch(j)
                if at == 0:
                    act.wait_ge(stored[h], t * 16 + START)
                act.wait_ge(mm[s], t * US + u + 1 + START)
                nc.scalar.copy(stage[:, h, :, at:at + B].rearrange("p k t -> p t k"), ps[:, j % 2].rearrange("p (t k) -> p t k", t=B)).then_inc(ev[j % 2], 1)

            def turn(t, more):
                for j in range(NBAT):
                    if j < NBAT - 2:
                        weigh(t, j + 2)
                    elif more:
                        weigh(t + 1, j + 2 - NBAT)
                    evacuate(t, j)

            for j in range(2):
                weigh(0, j)
            with act.Fori(0, NT - 1) as t:
                turn(t, True)
            turn(NT - 1, False)

        @block.sync
        def _(sp):
            with sp.Fori(0, NT) as t:
                for h in range(2):
                    for s in range(2):
                        sp.wait_ge(ev[s], t * UP + (h + 1) * (UP // 2) + START)
                    sp.dma_start(scr["gate"][:, ds(t * 2 + h, 1)].rearrange("p h k t -> p (h k) t"), stage[:, h]).then_inc(stored[h], 16)
            for h in range(2):
                sp.wait_ge(stored[h], NT * 16 + START)


def phase_experts(nc, io, per, scr, h2):
    E = 2
    BATCHES = N_KEYS // E
    SUMS = 3 * KD // 2
    with ExitStack() as ctx:
        sb, pb, sem = open_(nc, ctx)
        acc = sb("ex_acc", [P, KD, T])
        with ExitStack() as ctx2:
            sb2, pb2, _ = open_(nc, ctx2)
            pair = lambda name, shape: [sb2(name + n, shape, F32R) for n in ("_hi", "_lo")]
            u, vv = sb2("ex_u", [P, E, KD, P]), sb2("ex_v", [P, E, D])
            u2, v2, g2 = pair("ex_u", [P, E, KD, P]), pair("ex_v", [P, E, D]), pair("ex_g", [P, E, T])
            gate = sb2("ex_gate", [P, T // HALF, E, HALF])
            act_ = sb2("ex_act", [P, E, T])
            ps, pv = pb2("ex_ps", [P, E, 3, 512]), pb2("ex_pv", [P, 2, 512])
            u_in, v_in, mm = (sem("ex_" + n, E) for n in ("uin", "vin", "mm"))
            gate_in = sem("ex_gatein")
            u_hi, u_lo, v_hi, v_lo = (sem("ex_" + n, E) for n in ("uhi", "ulo", "vhi", "vlo"))
            gelu_r, gated, g_hi, g_lo = (sem("ex_" + n, E) for n in ("gelur", "gated", "ghi", "glo"))
            sum_mm, sum_r = sem("ex_summm", 2), sem("ex_sumr", 2)
            zero = sem("ex_zero")
            block = begin(nc, ctx2)

            @block.sync
            def _(sp):
                with sp.Fori(0, BATCHES) as b:
                    for e in range(E):
                        sp.wait_ge(u_lo[e], b + START)
                        sp.dma_start(u[:, e], io["expert_u"][ds(b * E + e, 1)].rearrange("e p k c -> p (e k) c")).then_inc(u_in[e], 16)
                    for e in range(E):
                        sp.wait_ge(gated[e], b + START)
                    sp.dma_start(gate[:], scr["gate"][:, :, ds(b * E, E)]).then_inc(gate_in, 16)
                    for e in range(E):
                        sp.wait_ge(v_lo[e], b + START)
                        sp.dma_start(vv[:, e], io["expert_v"][ds(b * E + e, 1)].rearrange("e p d -> p (e d)")).then_inc(v_in[e], 16)

            @block.tensor
            def _(pe):
                def u_products(b):
                    for e in range(E):
                        pe.wait_ge(u_lo[e], b + 1 + START)
                        pe.wait_ge(gelu_r[e], b + START)
                        product3(nc, ps[:, e], [x[:, e] for x in u2], h2, KD).then_inc(mm[e], 1)

                def v_products(b):
                    for e in range(E):
                        pe.wait_ge(v_lo[e], b + 1 + START)
                        pe.wait_ge(g_lo[e], b + 1 + START)
                    for d in range(KD):
                        for c in range(3):
                            j = d * 3 + c
                            pe.wait_ge(sum_r[j % 2], b * SUMS + j // 2 + START)
                            for e in range(E):
                                for x, y in SPLIT:
                                    last = nc.tensor.matmul(pv[:, j % 2, 0:CW], v2[x][:, e, d * P:(d + 1) * P], g2[y][:, e, c * CW:(c + 1) * CW],
                                                            start=(e == 0 and (x, y) == SPLIT[0]), stop=(e == E - 1 and (x, y) == SPLIT[-1]))
                            last.then_inc(sum_mm[j % 2], 1)

                u_products(0)
                with pe.Fori(0, BATCHES - 1) as b:
                    u_products(b + 1)
                    v_products(b)
                v_products(BATCHES - 1)

            @block.scalar
            def _(act):
                def round_u(b, e):
                    act.wait_ge(u_in[e], b * 16 + 16 + START)
                    act.wait_ge(mm[e], b + START)
                    nc.scalar.copy(u2[0][:, e], u[:, e]).then_inc(u_hi[e], 1)

                def gelu(b, e):
                    act.wait_ge(mm[e], b + 1 + START)
                    act.wait_ge(g_lo[e], b + START)
                    nc.scalar.activation(cut(act_[:, e]), banks(ps[:, e]), ACT.Gelu_apprx_tanh).then_inc(gelu_r[e], 1)

                def round_g_and_v(b):
                    for z in range(2):
                        act.wait_ge(sum_mm[z], b * SUMS + START)
                    for e in range(E):
                        act.wait_ge(gated[e], b + 1 + START)
                        nc.scalar.copy(g2[0][:, e], act_[:, e]).then_inc(g_hi[e], 1)
                        act.wait_ge(v_in[e], b * 16 + 16 + START)
                        nc.scalar.copy(v2[0][:, e], vv[:, e]).then_inc(v_hi[e], 1)

                def batch(b, more):
                    for e in range(E):
                        gelu(b, e)
                        if more:
                            round_u(b + 1, e)
                    round_g_and_v(b)

                for e in range(E):
                    round_u(0, e)
                with act.Fori(0, BATCHES - 1) as b:
                    batch(b, True)
                batch(BATCHES - 1, False)

            @block.vector
            def _(dve):
                v = nc.vector

                def rest_of_u(b, e):
                    dve.wait_ge(u_hi[e], b + 1 + START)
                    v.tensor_tensor(u2[1][:, e], u[:, e], u2[0][:, e].bitcast(F32), ALU.subtract).then_inc(u_lo[e], 1)

                def apply_gate(b, e):
                    dve.wait_ge(gelu_r[e], b + 1 + START)
                    dve.wait_ge(gate_in, b * 16 + 16 + START)
                    by_half = act_[:, e].rearrange("p (h t) -> p h t", t=HALF)
                    v.tensor_tensor(by_half, by_half, gate[:, :, e], ALU.mult).then_inc(gated[e], 1)

                def rest_of_g_and_v(b):
                    for e in range(E):
                        dve.wait_ge(g_hi[e], b + 1 + START)
                        v.tensor_tensor(g2[1][:, e], act_[:, e], g2[0][:, e].bitcast(F32), ALU.subtract).then_inc(g_lo[e], 1)
                        dve.wait_ge(v_hi[e], b + 1 + START)
                        v.tensor_tensor(v2[1][:, e], vv[:, e], v2[0][:, e].bitcast(F32), ALU.subtract).then_inc(v_lo[e], 1)

                def add_sums(b, first, end):
                    for j in range(first, end):
                        a = (j % 3) * CW
                        dve.wait_ge(sum_mm[j % 2], b * SUMS + j // 2 + 1 + START)
                        v.tensor_tensor(acc[:, j // 3, a:a + CW], acc[:, j // 3, a:a + CW], pv[:, j % 2, 0:CW], ALU.add).then_inc(sum_r[j % 2], 1)

                v.memset(acc[:], 0.0).then_inc(zero, 1)
                dve.wait_ge(zero, 1 + START)
                for e in range(E):
                    rest_of_u(0, e)
                apply_gate(0, 0)
                rest_of_u(1, 0)
                apply_gate(0, 1)
                rest_of_u(1, 1)
                rest_of_g_and_v(0)

                def batch(b, more):
                    apply_gate(b + 1, 0)
                    if more:
                        rest_of_u(b + 2, 0)
                    add_sums(b, 0, 6)
                    apply_gate(b + 1, 1)
                    add_sums(b, 6, 10)
                    if more:
                        rest_of_u(b + 2, 1)
                    add_sums(b, 10, 3 * KD)
                    rest_of_g_and_v(b + 1)

                with dve.Fori(0, BATCHES - 2) as b:
                    batch(b, True)
                batch(BATCHES - 2, False)
                add_sums(BATCHES - 1, 0, 3 * KD)
        finish_output(nc, io, per, scr, acc)


def finish_output(nc, io, per, scr, acc):
    with ExitStack() as ctx:
        sb, pb, sem = open_(nc, ctx)
        x = sb("fo_x", [P, KD, T])
        fg = sb("fo_g", [P, KD])
        sq, rstd, y = sb("fo_sq", [P, 2, T]), sb("fo_rstd", [P, T]), sb("fo_y", [P, 2, T])
        ps = pb("fo_ps", [P, TB])
        x_in, x_r, y_st, y_r = sem("fo_xin"), sem("fo_xr"), sem("fo_yst", 2), sem("fo_yr")
        pre = sem("fo_pre")
        squared, summed, rooted, chain = (sem("fo_" + n) for n in ("sq", "sum", "root", "chain"))
        block = begin(nc, ctx)
        ones = per["const"][:, C_ONE:C_ONE + P]

        @block.sync
        def _(sp):
            load_tiles(sp, x, scr["x1"], KD, x_in)
            sp.dma_start(fg[:], io["final_g"][:]).then_inc(x_in, 16)
            for k in range(KD):
                sp.wait_ge(y_r, k + 1 + START)
                sp.dma_start(io["y"][k], y[:, k % 2]).then_inc(y_st[k % 2], 16)
            for s in range(2):
                sp.wait_ge(y_st[s], KD // 2 * 16 + START)

        @block.vector
        def _(dve):
            v, mod = nc.vector, per["mod"]
            dve.wait_ge(x_in, (KD + 1) * 16 + START)
            for k in range(KD):
                v.tensor_scalar(acc[:, k, 0:SEQ], acc[:, k, 0:SEQ], mod[:, 5 * KD + k, 0:1], None, ALU.mult)
                v.tensor_tensor(samples(acc[:, k]), samples(acc[:, k]), per_token(mod[:, 5 * KD:6 * KD], k), ALU.mult).then_inc(pre, 1)
            for k in range(KD):
                dve.wait_ge(pre, k + 1 + START)
                v.tensor_tensor(x[:, k], x[:, k], acc[:, k], ALU.add).then_inc(x_r, 1)
            dve.wait_ge(rooted, 1 + START)
            v.reciprocal(rstd[:], rstd[:]).then_inc(chain, 1)
            dve.wait_ge(chain, 1 + START)
            for k in range(KD):
                if k >= 2:
                    dve.wait_ge(y_st[k % 2], k // 2 * 16 + START)
                v.scalar_tensor_tensor(out=y[:, k % 2], in0=x[:, k], scalar=fg[:, k:k + 1], in1=rstd[:], op0=ALU.mult, op1=ALU.mult).then_inc(y_r, 1)

        @block.scalar
        def _(act):
            for k in range(KD):
                act.wait_ge(x_r, k + 1 + START)
                if k >= 2:
                    act.wait_ge(summed, k - 1 + START)
                nc.scalar.activation(sq[:, k % 2], x[:, k], ACT.Square).then_inc(squared, 1)
            act.wait_ge(summed, KD + START)
            nc.scalar.activation(rstd[:], ps[:, 0:T], ACT.Sqrt, bias=per["eps"][:, 0:1], scale=1.0 / D).then_inc(rooted, 1)

        @block.tensor
        def _(pe):
            for k in range(KD):
                pe.wait_ge(squared, k + 1 + START)
                for a, n in COLS:
                    last = nc.tensor.matmul(ps[:, a:a + n], ones, sq[:, k % 2, a:a + n], start=(k == 0), stop=(k == KD - 1))
                last.then_inc(summed, 1)


def build(nc, io, outs):
    io = dict(io, **outs)
    with ExitStack() as ctx:
        sb, pb, sem = open_(nc, ctx)
        dram = lambda name, shape: nc.dram_tensor(name, shape, F32, kind="Internal").ap()
        scr = {
            "plain": dram("scr_plain", [NPLAIN, P, T]), "xbc": dram("scr_xbc", [MX, P, T]),
            "vd": dram("scr_vd", [P, NT, KV + H]), "ynorm": dram("scr_ynorm", [INNER // P, P, T]),
            "attn": dram("scr_attn", [ATTN // P, P, T]), "merged": dram("scr_merged", [KD, P, T]), "branch": dram("scr_branch", [KD, P, T]),
            "x1": dram("scr_x1", [KD, P, T]), "gate": dram("scr_gate", [P, T // HALF, N_KEYS, HALF]),
        }
        per = {"const": sb("const", [P, C_N]), "mod": sb("mod", [P, 6 * KD, NC_]),
               "gain": sb("gain", [P, 2, KD, NC_]), "eps": sb("eps", [P, 1]),
               "cond": sb("cond_silu", [P, KD, NC_]), "ada_b": sb("ada_bias", [P, 6 * KD]), "norm_g": sb("norm_gains", [P, 2, KD])}
        nc.vector.memset(per["eps"][:], EPS)
        phase_modulation(nc, io, per)
        with nc.sbuf_tensor("h_hi", [P, KD, T], F32R) as hi, nc.sbuf_tensor("h_lo", [P, KD, T], F32R) as lo:
            phase_norm1(nc, io, per, hi, lo)
            phase_projection(nc, io, per, (hi, lo), scr)
        phase_ssd(nc, io, per, scr)
        phase_attention(nc, io, per, scr)
        phase_merge(nc, io, per, scr)
        phase_out(nc, io, per, scr)
        phase_peer(nc, io, per, scr)



def kernel(**inputs):
    import numpy as np
    import concourse.bacc as bacc
    from concourse.bass_utils import run_bass_kernel_spmd

    a = {k: np.asarray(v) for k, v in inputs.items()}

    def col(v, m):
        return v.reshape((m, P) + v.shape[1:]).swapaxes(0, 1)

    def tiles(w):
        return w.reshape(w.shape[0] // P, P, w.shape[1] // P, P).transpose(2, 1, 0, 3)

    def constants():
        i = np.arange(P)
        out = np.zeros((P, C_N), np.float32)
        out[:, C_ID:C_ID + P] = np.eye(P)
        out[:, C_ONE:C_ONE + P] = 1
        for n, size in enumerate((P, TS)):
            same = i[:, None] // size == i[None] // size
            upto = same & (i[:, None] <= i[None])
            out[:, C_TRI + n * P:C_TRI + (n + 1) * P] = upto
            out[:, C_STRI + n * P:C_STRI + (n + 1) * P] = same & (i[:, None] > i[None])
            out[:, C_NEG + n * P:C_NEG + (n + 1) * P] = np.where(upto, 0, NEG)
        q, k = i[:, None] // CHUNK, np.arange(2 * P)[None] // CHUNK
        out[:, C_AM:C_AM + 2 * P] = np.where((k >= q) & (k <= q + 2), 0, NEG)
        out[:, C_IOTA:C_IOTA + P] = i[None]
        out[:, C_BM:C_BM + NB] = i[:, None] // TS == np.arange(NB)[None]
        return out

    w_in = a["w_in"][0]
    off_xbc, off_dt = INNER, INNER + CONV
    off_q = off_dt + H
    off_k, off_v, off_g = off_q + ATTN, off_q + ATTN + KV, off_q + ATTN + 2 * KV
    cols = lambda s, n: w_in[:, s:s + n]
    sinks = a["attn_sinks"][0].reshape(NKV, QH)
    arrays = {
        "const": constants(),
        "x": col(np.concatenate([a["x_prompt"][0], a["x_sample"].reshape(-1, D)]).T, KD),
        "c": col(np.concatenate([a["c_prompt"], a["c_sample"]]).T, KD),
        "ada_w": tiles(a["ada_w"][0]), "ada_b": col(a["ada_b"][0], 6 * KD),
        "norm_g": np.stack([col(a["norm1_g"][0], KD), col(a["norm2_g"][0], KD)], 1),
        "final_g": col(a["final_g"], KD),
        "w_main": tiles(np.concatenate([cols(0, INNER), cols(off_g, 2 * D), cols(off_q, ATTN), cols(off_k, KV), cols(off_xbc, CONV)], 1)),
        "w_vdt": col(np.concatenate([cols(off_v, KV), cols(off_dt, H)], 1), KD),
        "conv_hist": col(a["state_conv"][0].transpose(2, 0, 1), MX),
        "conv_w": col(np.concatenate([a["conv_w"][0], a["conv_b"]]).T, MX),
        "ssm_in": a["state_ssm"][0].reshape(NB, G, R * HD, N).transpose(1, 3, 0, 2),
        "dt_rows": np.broadcast_to(np.stack([a["dt_bias"][0], a["a_log"][0]]), (P, 2, H)),
        "d_skip": np.repeat(a["d_skip"][0].reshape(H // 2, 2), HD, 1).T.reshape(P, G, 2),
        "ssm_g": col(a["ssm_norm_g"][0], INNER // P).reshape(P, G, 2),
        "k_cache": a["cache_attn_k"][0].transpose(2, 3, 0, 1),
        "v_cache": a["cache_attn_v"][0].transpose(2, 1, 0, 3),
        "sink_prompt": np.broadcast_to(sinks[None], (P, NKV, QH)),
        "sink_sample": np.broadcast_to(sinks.T[None, :, None], (2, QH, TS, NKV)).reshape(P, NKV),
        "w_ssm": tiles(a["w_branch_ssm"][0]), "w_attn": tiles(a["w_branch_attn"][0]), "w_out": tiles(a["w_out"][0]),
        "w_query": tiles(a["peer_wq"][0]),
        "keys": a["peer_keys"][0].reshape(2 * PH, N_KEYS, P).transpose(0, 2, 1),
        "expert_u": a["peer_u"][0].reshape(N_KEYS, N_KEYS, KD, P).transpose(1, 3, 2, 0),
        "expert_v": a["peer_v"][0].reshape(N_KEYS, N_KEYS, D).transpose(1, 0, 2),
    }
    out_shapes = {
        "y": [KD, P, T], "k_prompt": [MK, P, P], "v_prompt": [P, KV], "k_sample": [MK, P, P], "v_sample": [P, KV],
        "conv_prompt": [P, MX, TAPS - 1], "conv_sample": [P, MX, NB * (TAPS - 1)],
        "ssm_prompt": [G, N, R * HD], "ssm_sample": [G, N, NB, R * HD],
    }
    nc = bacc.Bacc("TRN2", target_bir_lowering=False, num_devices=1)
    feed, io = {}, {}
    for name, v in arrays.items():
        feed["in_" + name] = np.ascontiguousarray(v)
        io[name] = nc.dram_tensor("in_" + name, feed["in_" + name].shape, F32, kind="ExternalInput").ap()
    outs = {n: nc.dram_tensor("out_" + n, s, F32, kind="ExternalOutput").ap() for n, s in out_shapes.items()}
    build(nc, io, outs)
    r = run_bass_kernel_spmd(nc, [feed], core_ids=[0]).results[0]
    o = {n: np.asarray(r["out_" + n]) for n in out_shapes}
    y = o["y"].reshape(D, T).T
    uncol = lambda v: v.swapaxes(0, 1).reshape((-1,) + v.shape[2:])
    return (
        np.ascontiguousarray(y[:SEQ]).reshape(1, SEQ, D), np.ascontiguousarray(y[SEQ:]).reshape(NB, TS, D),
        o["k_prompt"].reshape(KV, P).T.reshape(1, 1, P, NKV, DH), o["v_prompt"].reshape(1, 1, P, NKV, DH),
        uncol(o["conv_prompt"]).T.reshape(1, 1, TAPS - 1, CONV),
        o["ssm_prompt"].transpose(0, 2, 1).reshape(1, 1, H, HD, N),
        o["k_sample"].reshape(KV, NB, TS).transpose(1, 2, 0).reshape(1, NB, TS, NKV, DH),
        o["v_sample"].reshape(1, NB, TS, NKV, DH),
        uncol(o["conv_sample"]).reshape(CONV, NB, TAPS - 1).transpose(1, 2, 0)[None],
        o["ssm_sample"].transpose(2, 0, 3, 1).reshape(1, NB, H, HD, N),
    )
```
